# Optimizing a Trainium2 kernel written in Bass

```python
import math
import jax, jax.numpy as jnp
from jax import lax
import numpy as np

D_MODEL = 1024
BATCH = 1
SEQ = 256
DEPTH = 1

CHUNK = 64
D_SSM = D_MODEL // 2
SSM_GROUP = 16
N_GROUPS = D_SSM // SSM_GROUP
STATE = 64
N_HEADS = 8
HEAD_DIM = 64
D_ATTN = N_HEADS * HEAD_DIM
D_IN = D_SSM + 3 * D_ATTN
D_FF = 4 * D_MODEL
Q_BLOCK = 128
EPS = 1e-6
DT_MIN = 1e-3
DT_MAX = 1e-1


def rmsnorm(x, g):
    xf = x.astype(jnp.float32)
    y = xf * lax.rsqrt(jnp.mean(xf * xf, axis=-1, keepdims=True) + EPS)
    return (y * g.astype(jnp.float32)).astype(x.dtype)

def s5_branch(u, A_re, A_im, log_dt, B_re, B_im, C_re, C_im, D_skip, w_glu, b_glu):
    f32 = jnp.float32
    bsz, seq, _ = u.shape
    uf = u.astype(f32)
    ug = uf.reshape(bsz, seq, N_GROUPS, SSM_GROUP)
    lam = lax.complex(A_re.astype(f32), A_im.astype(f32))
    dt = jnp.exp(log_dt.astype(f32))[:, None]
    a_bar = jnp.exp(lam * dt)
    b_bar = ((a_bar - 1.0) / lam)[..., None] * lax.complex(B_re.astype(f32), B_im.astype(f32))
    bu = lax.complex(jnp.einsum('bsgc,gpc->bsgp', ug, b_bar.real),
                     jnp.einsum('bsgc,gpc->bsgp', ug, b_bar.imag))
    a = jnp.broadcast_to(a_bar, (1, seq, N_GROUPS, STATE))

    def combine(left, right):
        a_l, b_l = left
        a_r, b_r = right
        return a_r * a_l, a_r * b_l + b_r

    _, states = lax.associative_scan(combine, (a, bu), axis=1)
    y = (jnp.einsum('bsgp,gcp->bsgc', states.real, C_re.astype(f32))
         - jnp.einsum('bsgp,gcp->bsgc', states.imag, C_im.astype(f32)))
    y = y.reshape(bsz, seq, D_SSM) + D_skip.astype(f32) * uf
    y = jax.nn.gelu(y)
    y = y * jax.nn.sigmoid(y @ w_glu.astype(f32) + b_glu.astype(f32))
    return y.astype(u.dtype)

def stick_breaking_attention(q, k, v):
    f32 = jnp.float32
    bsz, seq, nh, dh = q.shape
    nb = seq // Q_BLOCK
    qb = q.astype(f32).reshape(bsz, nb, Q_BLOCK, nh, dh).transpose(1, 0, 2, 3, 4)
    kf = k.astype(f32)
    vf = v.astype(f32)
    key_pos = jnp.arange(seq)
    scale = HEAD_DIM ** -0.5

    def one_block(args):
        blk, q_blk = args
        q_pos = blk * Q_BLOCK + jnp.arange(Q_BLOCK)
        z = jnp.einsum('bqhd,bkhd->bhqk', q_blk, kf) * scale
        mask = key_pos[None, :] < q_pos[:, None]
        log_fail = jnp.where(mask, jax.nn.log_sigmoid(-z), 0.0)
        after = lax.cumsum(log_fail, axis=3, reverse=True) - log_fail
        log_w = jax.nn.log_sigmoid(z) + after
        w = jnp.where(mask, jnp.exp(log_w), 0.0)
        return jnp.einsum('bhqk,bkhd->bqhd', w, vf)

    out = lax.map(one_block, (jnp.arange(nb), qb))
    return out.transpose(1, 0, 2, 3, 4).reshape(bsz, seq, nh * dh).astype(q.dtype)

def first_inputs(seed: int = 0) -> dict:
    key = jax.random.key(seed)
    ks = jax.random.split(key, 22)
    f32 = jnp.float32

    def nrm(k, shape, scale):
        return jax.random.normal(k, shape, f32) * scale

    x = nrm(ks[0], (BATCH, SEQ, D_MODEL), 1.0)
    norm_mix = 1.0 + nrm(ks[1], (DEPTH, D_MODEL), 0.02)
    w_in = nrm(ks[2], (DEPTH, D_MODEL, D_IN), D_MODEL ** -0.5)
    A_re = -0.5 + nrm(ks[3], (DEPTH, N_GROUPS, STATE), 0.01)
    A_im = jnp.pi * jnp.arange(STATE, dtype=f32) + nrm(ks[4], (DEPTH, N_GROUPS, STATE), 0.01)
    log_dt = jax.random.uniform(ks[5], (DEPTH, N_GROUPS), f32, math.log(DT_MIN), math.log(DT_MAX))
    B_re = nrm(ks[6], (DEPTH, N_GROUPS, STATE, SSM_GROUP), (2 * SSM_GROUP) ** -0.5)
    B_im = nrm(ks[7], (DEPTH, N_GROUPS, STATE, SSM_GROUP), (2 * SSM_GROUP) ** -0.5)
    C_re = nrm(ks[8], (DEPTH, N_GROUPS, SSM_GROUP, STATE), STATE ** -0.5)
    C_im = nrm(ks[9], (DEPTH, N_GROUPS, SSM_GROUP, STATE), STATE ** -0.5)
    D_skip = nrm(ks[10], (DEPTH, D_SSM), 1.0)
    w_glu = nrm(ks[11], (DEPTH, D_SSM, D_SSM), D_SSM ** -0.5)
    b_glu = nrm(ks[12], (DEPTH, D_SSM), 0.02)
    w_up_ssm = nrm(ks[13], (DEPTH, D_SSM, D_MODEL), D_SSM ** -0.5)
    w_up_attn = nrm(ks[14], (DEPTH, D_ATTN, D_MODEL), D_ATTN ** -0.5)
    w_gate = nrm(ks[15], (DEPTH, D_MODEL, 2 * D_MODEL), D_MODEL ** -0.5)
    b_gate = nrm(ks[16], (DEPTH, 2 * D_MODEL), 0.02)
    w_out = nrm(ks[17], (DEPTH, D_MODEL, D_MODEL), D_MODEL ** -0.5)
    norm_mlp = 1.0 + nrm(ks[18], (DEPTH, D_MODEL), 0.02)
    w_ff1 = nrm(ks[19], (DEPTH, D_MODEL, D_FF), D_MODEL ** -0.5)
    w_ff2 = nrm(ks[20], (DEPTH, D_FF, D_MODEL), D_FF ** -0.5)
    norm_final = 1.0 + nrm(ks[21], (D_MODEL,), 0.02)
    return {"x": x, "norm_mix": norm_mix, "w_in": w_in, "A_re": A_re, "A_im": A_im,
            "log_dt": log_dt, "B_re": B_re, "B_im": B_im, "C_re": C_re, "C_im": C_im,
            "D_skip": D_skip, "w_glu": w_glu, "b_glu": b_glu, "w_up_ssm": w_up_ssm,
            "w_up_attn": w_up_attn, "w_gate": w_gate, "b_gate": b_gate, "w_out": w_out,
            "norm_mlp": norm_mlp, "w_ff1": w_ff1, "w_ff2": w_ff2, "norm_final": norm_final}

def first_block(x, norm_mix, w_in, A_re, A_im, log_dt, B_re, B_im, C_re, C_im, D_skip, w_glu, b_glu,
              w_up_ssm, w_up_attn, w_gate, b_gate, w_out, norm_mlp, w_ff1, w_ff2, norm_final):
    h = x
    bsz, seq, _ = x.shape
    for l in range(DEPTH):
        u = rmsnorm(h, norm_mix[l])
        proj = u @ w_in[l]
        u_ssm, q, k, v = jnp.split(proj, [D_SSM, D_SSM + D_ATTN, D_SSM + 2 * D_ATTN], axis=-1)
        y_ssm = s5_branch(u_ssm, A_re[l], A_im[l], log_dt[l], B_re[l], B_im[l], C_re[l], C_im[l],
                          D_skip[l], w_glu[l], b_glu[l])
        y_attn = stick_breaking_attention(q.reshape(bsz, seq, N_HEADS, HEAD_DIM),
                                          k.reshape(bsz, seq, N_HEADS, HEAD_DIM),
                                          v.reshape(bsz, seq, N_HEADS, HEAD_DIM))
        gates = jax.nn.sigmoid((u @ w_gate[l] + b_gate[l]).astype(jnp.float32)).astype(u.dtype)
        g_ssm, g_attn = jnp.split(gates, 2, axis=-1)
        merged = g_ssm * (y_ssm @ w_up_ssm[l]) + g_attn * (y_attn @ w_up_attn[l])
        h = h + merged @ w_out[l]
        hid = jax.nn.relu(rmsnorm(h, norm_mlp[l]) @ w_ff1[l])
        h = h + (hid * hid) @ w_ff2[l]
    return rmsnorm(h, norm_final)


DEPTH_2 = 2

CONF_WIDTH = 512
CONF_KERNEL = 31
SC_WIDTH = 512
SC_KERNEL = 3
MLA_HEADS = 8
QK_NOPE = 64
QK_ROPE = 32
V_HEAD = 64
Q_LORA = 384
KV_LORA = 256
MLA_WIDTH = MLA_HEADS * V_HEAD
ROPE_THETA = 10000.0
N_BRANCH = 3
LN_EPS = 1e-5
RMS_EPS = 1e-6
DEEPNORM_ALPHA = (2 * DEPTH_2) ** 0.25
DEEPNORM_BETA = (8 * DEPTH_2) ** -0.25
ADA_SCALE = 0.5

IN_SIZES = (2 * CONF_WIDTH, CONF_WIDTH, 3 * SC_WIDTH, SC_WIDTH, Q_LORA, KV_LORA, QK_ROPE, MLA_WIDTH, N_BRANCH * D_MODEL)
D_IN_2 = 2 * CONF_WIDTH + CONF_WIDTH + 3 * SC_WIDTH + SC_WIDTH + Q_LORA + KV_LORA + QK_ROPE + MLA_WIDTH + N_BRANCH * D_MODEL


def layer_norm(x, g, b):
    x32 = x.astype(jnp.float32)
    mu = jnp.mean(x32, axis=-1, keepdims=True)
    var = jnp.mean(jnp.square(x32 - mu), axis=-1, keepdims=True)
    y = (x32 - mu) * lax.rsqrt(var + LN_EPS)
    return (y * g.astype(jnp.float32) + b.astype(jnp.float32)).astype(x.dtype)

def rms_norm(x, g):
    x32 = x.astype(jnp.float32)
    y = x32 * lax.rsqrt(jnp.mean(jnp.square(x32), axis=-1, keepdims=True) + RMS_EPS)
    return (y * g.astype(jnp.float32)).astype(x.dtype)

def causal_depthwise_conv(x, w):
    k_width, ch = w.shape
    return lax.conv_general_dilated(
        x, w.astype(x.dtype)[:, None, :], window_strides=(1,), padding=((k_width - 1, 0),),
        dimension_numbers=("NWC", "WIO", "NWC"), feature_group_count=ch)

def rope_tables(positions):
    inv_freq = ROPE_THETA ** (-jnp.arange(0, QK_ROPE, 2, dtype=jnp.float32) / QK_ROPE)
    ang = positions.astype(jnp.float32)[..., None] * inv_freq
    return jnp.cos(ang), jnp.sin(ang)

def apply_rope(x, cos, sin):
    cos = cos.astype(x.dtype)
    sin = sin.astype(x.dtype)
    x1, x2 = jnp.split(x, 2, axis=-1)
    return jnp.concatenate([x1 * cos - x2 * sin, x2 * cos + x1 * sin], axis=-1)

def causal_block_attention(q, k, v):
    b, s, h, dv = v.shape
    scale = (QK_NOPE + QK_ROPE) ** -0.5
    key_idx = jnp.arange(s)

    def one_block(i):
        start = i * Q_BLOCK
        qb = lax.dynamic_slice_in_dim(q, start, Q_BLOCK, axis=1)
        sc = jnp.einsum("bqhd,bkhd->bhqk", qb, k, preferred_element_type=jnp.float32) * scale
        q_idx = start + jnp.arange(Q_BLOCK)
        mask = key_idx[None, :] <= q_idx[:, None]
        sc = jnp.where(mask[None, None], sc, -jnp.inf)
        p = jax.nn.softmax(sc, axis=-1).astype(v.dtype)
        return jnp.einsum("bhqk,bkhd->bqhd", p, v)

    out = lax.map(one_block, jnp.arange(s // Q_BLOCK))
    return out.transpose(1, 0, 2, 3, 4).reshape(b, s, h, dv)

def hybrid_layer(x, c_act, cos, sin, w_ada, b_ada, w_in, conv_a_w, conv_a_b, ln_a_g, ln_a_b, w_a_out,
                 conv_b_w, w_b_out, q_norm_g, kv_norm_g, w_uq, w_ukv, w_c_out, w_o, ln_g, ln_b):
    b, s, _ = x.shape
    ada = c_act @ w_ada + b_ada
    shift, scale, gate = jnp.split(ada, 3, axis=-1)
    u = x * (1.0 + scale[:, None, :]) + shift[:, None, :]

    proj = jnp.einsum("bsd,dp->bsp", u, w_in)
    split_pts = [int(v) for v in np.cumsum(IN_SIZES)[:-1]]
    a_in, a_gate, b_in, b_gate, q_lat, kv_lat, k_rope, c_gate, merge_logits = jnp.split(proj, split_pts, axis=-1)

    a1, a2 = jnp.split(a_in, 2, axis=-1)
    a = a1 * jax.nn.sigmoid(a2)
    a = causal_depthwise_conv(a, conv_a_w) + conv_a_b
    a = jax.nn.silu(layer_norm(a, ln_a_g, ln_a_b))
    y_a = jnp.einsum("bsc,cd->bsd", a * jax.nn.silu(a_gate), w_a_out)

    xb, gb, gc = jnp.split(b_in, 3, axis=-1)
    yb = gb * causal_depthwise_conv(gc * xb, conv_b_w)
    y_b = jnp.einsum("bsc,cd->bsd", yb * jax.nn.silu(b_gate), w_b_out)

    q = jnp.einsum("bsr,rk->bsk", rms_norm(q_lat, q_norm_g), w_uq).reshape(b, s, MLA_HEADS, QK_NOPE + QK_ROPE)
    q_nope, q_pe = jnp.split(q, [QK_NOPE], axis=-1)
    q_pe = apply_rope(q_pe, cos[:, :, None, :], sin[:, :, None, :])
    kv = jnp.einsum("bsr,rk->bsk", rms_norm(kv_lat, kv_norm_g), w_ukv).reshape(b, s, MLA_HEADS, QK_NOPE + V_HEAD)
    k_nope, v = jnp.split(kv, [QK_NOPE], axis=-1)
    k_pe = apply_rope(k_rope, cos, sin)[:, :, None, :]
    qf = jnp.concatenate([q_nope, q_pe], axis=-1)
    kf = jnp.concatenate([k_nope, jnp.broadcast_to(k_pe, (b, s, MLA_HEADS, QK_ROPE))], axis=-1)
    o = causal_block_attention(qf, kf, v).reshape(b, s, MLA_WIDTH)
    y_c = jnp.einsum("bsc,cd->bsd", o * jax.nn.silu(c_gate), w_c_out)

    g_a, g_b, g_c = jnp.split(jax.nn.sigmoid(merge_logits), N_BRANCH, axis=-1)
    m = g_a * y_a + g_b * y_b + g_c * y_c
    out = jnp.einsum("bsd,de->bse", m, w_o)

    return layer_norm(DEEPNORM_ALPHA * x + gate[:, None, :] * out, ln_g, ln_b)

def second_inputs(seed: int = 0) -> dict:
    key = jax.random.key(seed)
    ks = jax.random.split(key, 24)
    L, D = DEPTH_2, D_MODEL

    def nrm(k, shape, scale):
        return jax.random.normal(k, shape, dtype=jnp.float32) * scale

    x = nrm(ks[0], (BATCH, SEQ, D), 1.0)
    c = nrm(ks[1], (BATCH, D), 1.0)
    offsets = jax.random.randint(ks[2], (BATCH, 1), 0, 1024, dtype=jnp.int32)
    positions = (jnp.arange(SEQ, dtype=jnp.int32)[None, :] + offsets).astype(jnp.int32)
    return {
        "x": x,
        "c": c,
        "positions": positions,
        "w_ada": nrm(ks[3], (L, D, 3 * D), ADA_SCALE * D ** -0.5),
        "b_ada": nrm(ks[4], (L, 3 * D), 0.02),
        "w_in": nrm(ks[5], (L, D, D_IN_2), D ** -0.5),
        "conv_a_w": nrm(ks[6], (L, CONF_KERNEL, CONF_WIDTH), CONF_KERNEL ** -0.5),
        "conv_a_b": nrm(ks[7], (L, CONF_WIDTH), 0.02),
        "ln_a_g": 1.0 + nrm(ks[8], (L, CONF_WIDTH), 0.02),
        "ln_a_b": nrm(ks[9], (L, CONF_WIDTH), 0.02),
        "w_a_out": nrm(ks[10], (L, CONF_WIDTH, D), DEEPNORM_BETA * CONF_WIDTH ** -0.5),
        "conv_b_w": nrm(ks[11], (L, SC_KERNEL, SC_WIDTH), SC_KERNEL ** -0.5),
        "w_b_out": nrm(ks[12], (L, SC_WIDTH, D), DEEPNORM_BETA * SC_WIDTH ** -0.5),
        "q_norm_g": 1.0 + nrm(ks[13], (L, Q_LORA), 0.02),
        "kv_norm_g": 1.0 + nrm(ks[14], (L, KV_LORA), 0.02),
        "w_uq": nrm(ks[15], (L, Q_LORA, MLA_HEADS * (QK_NOPE + QK_ROPE)), Q_LORA ** -0.5),
        "w_ukv": nrm(ks[16], (L, KV_LORA, MLA_HEADS * (QK_NOPE + V_HEAD)), KV_LORA ** -0.5),
        "w_c_out": nrm(ks[17], (L, MLA_WIDTH, D), DEEPNORM_BETA * MLA_WIDTH ** -0.5),
        "w_o": nrm(ks[18], (L, D, D), DEEPNORM_BETA * D ** -0.5),
        "ln_g": 1.0 + nrm(ks[19], (L, D), 0.02),
        "ln_b": nrm(ks[20], (L, D), 0.02),
    }

def second_block(x, c, positions, w_ada, b_ada, w_in, conv_a_w, conv_a_b, ln_a_g, ln_a_b, w_a_out,
              conv_b_w, w_b_out, q_norm_g, kv_norm_g, w_uq, w_ukv, w_c_out, w_o, ln_g, ln_b):
    c_act = jax.nn.silu(c)
    cos, sin = rope_tables(positions)
    h = x
    for l in range(DEPTH_2):
        h = hybrid_layer(h, c_act, cos, sin, w_ada[l], b_ada[l], w_in[l], conv_a_w[l], conv_a_b[l],
                         ln_a_g[l], ln_a_b[l], w_a_out[l], conv_b_w[l], w_b_out[l], q_norm_g[l],
                         kv_norm_g[l], w_uq[l], w_ukv[l], w_c_out[l], w_o[l], ln_g[l], ln_b[l])
    return h


def setup_inputs(seed=0):
    out = dict(first_inputs(seed))
    for name, value in second_inputs(seed + 1).items():
        if name != "x":
            out[name + "_2"] = value
    return out


def reference(
    x, norm_mix, w_in, A_re, A_im, log_dt, B_re, B_im, C_re, C_im, D_skip, w_glu, b_glu,
    w_up_ssm, w_up_attn, w_gate, b_gate, w_out, norm_mlp, w_ff1, w_ff2, norm_final, c_2,
    positions_2, w_ada_2, b_ada_2, w_in_2, conv_a_w_2, conv_a_b_2, ln_a_g_2, ln_a_b_2,
    w_a_out_2, conv_b_w_2, w_b_out_2, q_norm_g_2, kv_norm_g_2, w_uq_2, w_ukv_2, w_c_out_2,
    w_o_2, ln_g_2, ln_b_2,
):
    x = first_block(
        x, norm_mix, w_in, A_re, A_im, log_dt, B_re, B_im, C_re, C_im, D_skip, w_glu, b_glu,
        w_up_ssm, w_up_attn, w_gate, b_gate, w_out, norm_mlp, w_ff1, w_ff2, norm_final,
    )
    return second_block(
        x, c_2, positions_2, w_ada_2, b_ada_2, w_in_2, conv_a_w_2, conv_a_b_2, ln_a_g_2,
        ln_a_b_2, w_a_out_2, conv_b_w_2, w_b_out_2, q_norm_g_2, kv_norm_g_2, w_uq_2, w_ukv_2,
        w_c_out_2, w_o_2, ln_g_2, ln_b_2,
    )


_drawn_inputs = setup_inputs


def setup_inputs(seed=0):
    import zlib

    import numpy as np

    out = dict(_drawn_inputs(seed))
    spreads = {}
    factors = {'norm_mix': 5.242,
     'A_re': 200.0,
     'A_im': 3.214,
     'log_dt': 3.423,
     'B_re': 4.565,
     'B_im': 4.572,
     'C_re': 4.59,
     'C_im': 4.588,
     'b_glu': 8.0,
     'b_gate': 8.0,
     'norm_mlp': 3.313,
     'norm_final': 2.754,
     'b_ada_2': 8.0,
     'conv_a_w_2': 3.494,
     'conv_a_b_2': 8.0,
     'ln_a_g_2': 8.0,
     'ln_a_b_2': 8.0,
     'w_a_out_2': 3.21,
     'q_norm_g_2': 8.0,
     'kv_norm_g_2': 8.0,
     'w_uq_2': 8.0,
     'w_ukv_2': 4.176,
     'w_c_out_2': 4.274}
    for name, (base, spread) in spreads.items():
        noise = np.random.default_rng([zlib.crc32(name.encode()), seed]).standard_normal(out[name].shape)
        drawn = base * np.exp(spread * noise) if base else spread * noise
        out[name] = __import__('jax').numpy.asarray(drawn.astype(out[name].dtype))
    for name, factor in factors.items():
        out[name] = (out[name] * factor).astype(out[name].dtype)
    return out
```

```python
import math
from contextlib import ExitStack

import numpy as np

import concourse.bass as bass
from concourse import mybir

F32 = mybir.dt.float32
F32R = mybir.dt.float32r
I32 = mybir.dt.int32
ALU = mybir.AluOpType
ACT = mybir.ActivationFunctionType
AX = mybir.AxisListType

P = 128
T = 256
D = 1024
KT = D // P
W = 512
WT = W // P
HEADS = 8
DH = 64
DFF = 4 * D
GROUPS, CIN, STATE = 32, 16, 64
PAIRS = GROUPS // 2
CONV_A, CONV_B = 31, 3
NOPE, ROPE = 64, 32
QK = NOPE + ROPE
QL, KVL = 384, 256
LAYERS = 2
RMS_EPS, LN_EPS = 1e-6, 1e-5
ALPHA = (2 * LAYERS) ** 0.25
SCALE2 = QK ** -0.5
BIG = 3.0e38

A1, A2, AG = 0, W, 2 * W
XB, GB, GC, BG = 3 * W, 4 * W, 5 * W, 6 * W
CQ = 7 * W
CKV = CQ + QL
CKR = CKV + KVL
CG = CKR + ROPE
CM = CG + W

COL = {}
_at = 0
for _name, _n in (("norm_mix", 8), ("b_gate", 16), ("norm_mlp", 8), ("norm_final", 8), ("D_skip", 4),
                  ("b_glu", 4), ("c", 8), ("A_re", 16), ("A_im", 16), ("log_dt", 16), ("inv_freq", 1)):
    COL[_name] = _at
    _at += _n
for _l in range(LAYERS):
    for _name, _n in (("b_ada", 24), ("conv_a_b", 4), ("ln_a_g", 4), ("ln_a_b", 4), ("conv_b_w", 12),
                      ("q_norm_g", 3), ("kv_norm_g", 2), ("ln_g", 8), ("ln_b", 8), ("conv_a_w", 124)):
        COL[_name, _l] = _at
        _at += _n
NPAR = _at

RAW = 4
HL = 3
SLOT = 2048

LN2_HI, LN2_LO = 0.693359375, -2.12194440e-4
TWO_PI = (6.28125, 1.9350051879882812e-3, 3.0199159819e-7)
PI_IN = 3.1415925
ROUND = 12582912.0


def schedule():
    panels, order = [], []
    count = {"split": 0, "group": 0, "gt": 0}

    def panel(job, layer, n, name, row, col, kt, cols, groups, split=True):
        gt = None
        if job in ("cg", "ag", "bg", "merge0", "merge1", "merge2"):
            gt = count["gt"]
            count["gt"] += 1
        panels.append(dict(index=len(panels), job=job, layer=layer, n=n, name=name, row=row, col=col, kt=kt,
                           cols=cols, split=split, s=count["split"] if split else None, g=count["group"],
                           groups=groups, gt=gt))
        count["split"] += split
        count["group"] += groups
        order.append(("panel", len(panels) - 1, 0))

    def wide(job, layer, name, col, width, row=0):
        for n in range(width // 256):
            panel(job, layer, n, name, row, col + 256 * n, KT, 256, 1)

    def half(job, layer, name, width, row=0):
        for n in range(width // 512):
            panel(job, layer, n, name, row, 512 * n, WT, 512, 2)

    def step(kind, a=0, b=0):
        order.append((kind, a, b))

    step("norm", 0)
    step("split", "u0")
    wide("ssm", 0, "w_in", 0, W)
    step("s5_prep")
    wide("q", 0, "w_in", W, W)
    wide("k", 0, "w_in", 2 * W, W)
    wide("v", 0, "w_in", 3 * W, W)
    ada = 0
    for r in range(PAIRS + 1):
        if r < PAIRS:
            step("bu", r)
            if r < HEADS:
                step("stick_scores", r)
            if 1 <= r <= HEADS:
                step("stick_out", r - 1)
            step("scan", r)
            if r < HEADS:
                panel("gate", 0, r, "w_gate", 0, 256 * r, KT, 256, 1)
                step("stick_soft", r)
                step("stick_weights", r)
        if r >= 1:
            step("s5_out", r - 1)
        if r >= 4 and ada < 24:
            for _ in range(2):
                panel("ada", ada // 12, ada % 12, "w_ada_2", 0, 256 * (ada % 12), KT, 256, 0, split=False)
                ada += 1
            if ada % 12 == 0:
                step("ada_end", ada // 12 - 1)
    step("split", "ctx")
    step("split", "y")
    half("up_attn", 0, "w_up_attn", D)
    half("glu", 0, "w_glu", W)
    step("glu_mul")
    step("split", "yg")
    half("up_ssm", 0, "w_up_ssm", D)
    step("split", "u1")
    wide("out", 0, "w_out", 0, D)
    step("norm", 1)
    step("split", "u2")
    chunks = DFF // W
    for c in range(chunks + 1):
        if c < chunks:
            for n in range(2):
                panel("ff1", 0, 2 * c + n, "w_ff1", 0, W * c + 256 * n, KT, 256, 1)
        if c >= 1:
            for n in range(2):
                panel("ff2", 0, 2 * (c - 1) + n, "w_ff2", W * (c - 1), 512 * n, WT, 512, 2)
        if c == 2:
            step("rope_tables")
    step("norm", 2)
    for l in range(LAYERS):
        step("modulate", l)
        step("split", ("u", l))
        step("prescale", l)
        panel("q_lat", l, 0, "w_in_2", 0, CQ, KT, 256, 1)
        panel("q_lat", l, 1, "w_in_2", 0, CQ + 256, KT, 128, 1)
        panel("kv_lat", l, 0, "w_in_2", 0, CKV, KT, 256, 1)
        panel("k_rope", l, 0, "w_in_2", 0, CKR + ROPE - QK, KT, QK, 1)
        step("latent_sums", l)
        wide("a2", l, "w_in_2", A2, W)
        step("latent_norm", l)
        step("split", ("ql", l))
        step("split", ("kvl", l))
        wide("a1", l, "w_in_2", A1, W)
        for n in range(2):
            panel("uq", l, n, "w_uq_2", 0, 4 * QK * n, QL // P, 4 * QK, 2)
        panel("ukv", l, 0, "w_ukv_2", 0, 0, KVL // P, 1024, 6)
        step("rope", l)
        wide("cg", l, "w_in_2", CG, W)
        step("conv_a", l, 0)
        for h in range(HEADS + 2):
            if h < HEADS:
                step("scores", l, h)
            if 1 <= h <= HEADS:
                step("turn", l, h - 1)
            if h >= 2:
                step("context", l, h - 2)
            if h in (1, 2, 3, 4, 5, 6):
                job, at = (("xb", XB), ("gc", GC), ("gb", GB))[(h - 1) // 2]
                if h == 5:
                    step("conv_b", l)
                n = (h - 1) % 2
                panel(job, l, n, "w_in_2", 0, at + 256 * n, KT, 256, 1)
            if h in (2, 4, 6):
                step("conv_a", l, h // 2)
        step("ln_a_mean", l)
        wide("bg", l, "w_in_2", BG, W)
        step("split", ("b", l))
        step("ln_a_var", l)
        wide("ag", l, "w_in_2", AG, W)
        half("branch1", l, "w_b_out_2", D)
        step("ln_a_out", l)
        step("split", ("a", l))
        wide("merge1", l, "w_in_2", CM + D, D)
        half("branch0", l, "w_a_out_2", D)
        step("split", ("c", l))
        wide("merge0", l, "w_in_2", CM, D)
        half("branch2", l, "w_c_out_2", D)
        wide("merge2", l, "w_in_2", CM + 2 * D, D)
        step("split", ("m", l))
        wide("w_o", l, "w_o_2", 0, D)
        step("ln", l)
    return panels, order


PANELS, ORDER = schedule()
SPLIT = [q for q in PANELS if q["split"]]


def groups_of(job, layer=0):
    return [g for q in PANELS if q["job"] == job and q["layer"] == layer for g in range(q["g"], q["g"] + q["groups"])]


def find(job, layer=0, n=0):
    return next(q for q in PANELS if q["job"] == job and q["layer"] == layer and q["n"] == n)


ROOTS = [("norm", 0), ("norm", 1), ("norm", 2)]
for _l in range(LAYERS):
    ROOTS += [("lat_q", _l), ("lat_kv", _l), ("var_a", _l), ("var", _l)]

SUMS = [("norm", 0), ("ada", 0), ("ada", 1), ("norm", 1), ("norm", 2)]
for _l in range(LAYERS):
    SUMS += [("lat", _l), ("mean_a", _l), ("var_a", _l), ("mean", _l), ("var", _l)]


def build(nc, t, out, marks, dry):
    ctx = ExitStack()
    with ctx:
        sems = {}
        counts = {}

        def sem(name):
            if name not in sems:
                sems[name] = ctx.enter_context(nc.semaphore(name))
                counts[name] = 0
            return sems[name]

        def event(name, *key):
            s = sem(name)
            counts[name] += 1
            marks[(name, *key)] = counts[name]
            return s, 1

        def over(name, *key):
            sem(name)
            return 1 if dry and (name, *key) not in marks else marks[(name, *key)]

        def emptied(groups):
            for b in range(2):
                of_bank = [g for g in groups if g % 2 == b]
                if of_bank:
                    yield sem(f"bank_free{b}"), max(of_bank) // 2 + 1

        def landed(q):
            return sem(f"raw{q['index'] % RAW}"), 16 * (q["index"] // RAW + 1)

        def slot_free(q):
            return sem(f"raw_free{q['index'] % RAW}"), q["index"] // RAW + 1

        class Count:

            def __init__(self, own):
                self.own = own
                self.last = (sem(own), 0)

            def event(self, name, *key):
                s, _ = event(name, *key)
                self.last = (s, counts[name])
                return s, 1

            def step(self):
                return self.event(self.own)

            def bank_free(self, g):
                self.last = (sem(f"bank_free{g % 2}"), g // 2 + 1)
                return self.last[0], 1

        def sb(name, shape, dt=F32):
            return ctx.enter_context(nc.sbuf_tensor(name, shape, dt))

        def bank(name):
            return ctx.enter_context(nc.psum_tensor(name, [P, 512], F32))

        raw = sb("raw", [P, RAW, SLOT])
        w_hi = sb("w_hi", [P, HL, SLOT], F32R)
        w_lo = sb("w_lo", [P, HL, SLOT], F32R)
        u_hi = sb("u_hi", [P, KT, T], F32R)
        u_lo = sb("u_lo", [P, KT, T], F32R)
        v_hi = [sb("va_hi", [P, WT, T], F32R), sb("vb_hi", [P, WT, T], F32R)]
        v_lo = [sb("va_lo", [P, WT, T], F32R), sb("vb_lo", [P, WT, T], F32R)]
        h = sb("h", [P, KT, T])
        par = sb("par", [P, NPAR])
        ident = sb("ident", [P, P])
        ones = sb("ones", [P, P])
        ntri = sb("ntri", [P, P])
        nones = sb("nones", [P, P])
        mask1 = sb("mask1", [P, 384])
        neg1 = sb("neg1", [P, 384])
        mask2 = sb("mask2", [P, 384])
        rot = sb("rot", [P, ROPE])
        pos = sb("pos", [P, T], I32)
        rcos = sb("rcos", [P, T])
        rsin = sb("rsin", [P, T])
        root = sb("root", [P, 2, T])
        rstd = sb("rstd", [P, 2, T])
        nmean = sb("nmean", [P, T])
        silu_c = sb("silu_c", [P, KT])
        ada = sb("ada", [P, LAYERS, 24])
        scale1 = sb("scale1", [P, KT])
        sums = sb("sums", [P, 2, 2])
        nmax = sb("nmax", [P, 2, 2])
        mx = sb("mx", [P, 2, 2])
        rsum = sb("rsum", [P, 2, 2])
        AREA = 18150
        area = sb("area", [P, AREA])
        spot = [0]

        def cut(*shape):
            n = math.prod(shape)
            a = area[:, spot[0]:spot[0] + n]
            spot[0] += n
            assert spot[0] <= AREA, spot
            if len(shape) == 2:
                return a.rearrange("p (a b) -> p a b", a=shape[0])
            if len(shape) == 3:
                return a.rearrange("p (a b c) -> p a b c", a=shape[0], b=shape[1])
            return a

        tmp = cut(KT, T)
        gates = cut(16, T)
        ussm = cut(WT, T)
        q1 = cut(WT, T)
        k1 = cut(WT, T)
        v1 = cut(2, W)
        merged = cut(KT, T)
        ct = cut(2, 4, P)
        bt = cut(2, 4, P)
        bst = merged[:, 0:2, :]
        bd = merged[:, 2:6, :].rearrange("p (a b) n -> p a (b n)", a=2)
        btmp = merged[:, 6:7, :].rearrange("p a n -> p (a n)")
        small = cut(22, 16)
        power = cut(8, 3, 16)
        PAD = 16
        xs = cut(4, 2, PAD + T)
        stick_w = cut(2, 384)
        stick_z = tmp[:, 4:7, :].rearrange("p a n -> p (a n)").rearrange("p (a n) -> p a n", a=2)
        stick = [stick_z[:, 0], stick_z[:, 1], stick_w[:, 0], stick_w[:, 1]]
        context1 = merged[:, 0:4, :]
        yv = tmp[:, 0:4, :]
        yt = tmp[:, 4:8, :]
        y1 = tmp[:, 7, :]
        spot[0] = KT * T
        qf = cut(HEADS, T)
        kf = cut(HEADS, T)
        v2 = cut(2, W)
        q_lat = cut(3, T)
        kv_lat = cut(2, T)
        kpe = cut(T)
        kpr = cut(T)
        apad = cut(WT, T + CONV_A - 1)
        acc = cut(WT, T)
        agate = cut(WT, T)
        bpad = cut(WT, T + CONV_B - 1)
        cgate = cut(WT, T)
        lat_sq = cut(5, T)
        soft = cut(2, 384)
        soft_t = cut(2, 384)
        rtmp = tmp[:, 0:2, :]
        gtmp = cut(2, 512)
        xbv = lat_sq[:, 0:4, :]
        bconv = tmp[:, 4:8, :]
        ybr = qf
        mer = kf

        pg = [bank("pg0"), bank("pg1")]
        p_bu, p_y, p_z, p_c, p_o, p_s = (bank(n) for n in ("p_bu", "p_y", "p_z", "p_c", "p_o", "p_s"))

        def col(name, n=0, w=1):
            a = COL[name] + n
            return par[:, a:a + w]

        def pair(ap):
            return ap.rearrange("p (a n) -> p a n", a=2)

        def spread(ap, *shape):
            return ap.unsqueeze(1).broadcast_to(list(shape))

        def slot(tensor, q):
            n = q["index"] % RAW if tensor is raw else q["s"] % HL
            return tensor[:, n, 0:q["kt"] * q["cols"]].rearrange("p (k n) -> p k n", k=q["kt"])

        def operand(src, hi, lo, pieces, ready, after):
            return dict(src=src, hi=hi, lo=lo, pieces=pieces, ready=ready, after=after)

        def u_operand(src, ready, after):
            return operand(src, u_hi, u_lo, [(2 * j, 2 * j + 2) for j in range(4)], ready, after)

        def v_operand(src, n, tiles, ready, after):
            return operand(src, v_hi[n], v_lo[n], [(0, tiles)], ready, after)

        OPERANDS = {
            "u0": u_operand(tmp, "rows", None),
            "ctx": v_operand(context1, 0, WT, None, None),
            "y": v_operand(yv, 1, WT, "rows", None),
            "yg": v_operand(yv, 0, WT, "rows", groups_of("up_attn")[-1]),
            "u1": u_operand(merged, "rows", groups_of("gate")[-1]),
            "u2": u_operand(tmp, "rows", groups_of("out")[-1]),
        }
        for l in range(LAYERS):
            OPERANDS["u", l] = u_operand(tmp, "rows", groups_of("ff1")[-1] if l == 0 else groups_of("w_o", 0)[-1])
            OPERANDS["ql", l] = v_operand(q_lat, 1, 3, "rows",
                                          groups_of("ff2")[-1] if l == 0 else groups_of("branch2", 0)[-1])
            OPERANDS["kvl", l] = v_operand(kv_lat, 0, 2, "rows",
                                           groups_of("ff2")[-1] if l == 0 else groups_of("branch0", 0)[-1])
            OPERANDS["b", l] = v_operand(bconv, 1, WT, "bg", groups_of("uq", l)[-1])
            OPERANDS["a", l] = v_operand(acc, 0, WT, "rows", groups_of("ukv", l)[-1])
            OPERANDS["c", l] = v_operand(cgate, 1, WT, "rows", groups_of("branch1", l)[-1])
            OPERANDS["m", l] = u_operand(mer, "merge2", groups_of("merge2", l)[-1])

        USES = {"ssm": "u0", "q": "u0", "k": "u0", "v": "u0", "gate": "u0", "up_attn": "ctx", "glu": "y",
                "up_ssm": "yg", "out": "u1", "ff1": "u2"}

        def operand_of(q):
            if q["job"] in USES:
                return USES[q["job"]]
            own = {"uq": "ql", "ukv": "kvl", "branch1": "b", "branch0": "a", "branch2": "c", "w_o": "m"}
            return own.get(q["job"], "u"), q["layer"]

        def sums_before(key):
            key = SUMS[SUMS.index(key) - 1]
            name = "ada" if key[0] == "ada" else "nmean" if key[0] in ("mean_a", "mean") else "root"
            return sem(name), over(name, ("lat_kv", key[1]) if key[0] == "lat" else key)

        block = ctx.enter_context(nc.Block())

        @block.sync
        def _(sp):
            sp.dma_start(h[:, :, :], t["x_t"].rearrange("(k p) n -> p k n", p=P)).then_inc(sem("x_landed"), 16)
            for q in PANELS:
                n = q["index"] % RAW
                if q["index"] >= RAW:
                    sp.wait_ge(sem(f"raw_free{n}"), q["index"] // RAW)
                w = t[q["name"]][q["layer"], q["row"]:q["row"] + P * q["kt"], q["col"]:q["col"] + q["cols"]]
                sp.dma_start(slot(raw, q), w.rearrange("(k p) n -> p k n", p=P)).then_inc(sem(f"raw{n}"), 16)
            sp.wait_ge(sem("affine"), over("affine", LAYERS - 1))
            sp.dma_start(out.rearrange("(k p) n -> p k n", p=P), h[:, :, :]).then_inc(sem("stored"), 16)
            sp.wait_ge(sem("stored"), 16)

        @block.gpsimd
        def _(pool):
            c = Count("const")
            pool.dma_start(par[:, :], t["params"]).then_inc(sem("par_landed"), 16)
            pool.dma_start(bst, t["b_state"]).then_inc(sem("s5_landed"), 16)
            pool.dma_start(ct, t["c_state"]).then_inc(sem("s5_landed"), 16)
            pool.dma_start(pos[NOPE:QK, :], t["positions"].partition_broadcast(ROPE)).then_inc(sem("pos_landed"), 16)
            pool.memset(ones[:, :], 1.0).then_inc(*c.step())
            pool.memset(nones[:, :], -1.0).then_inc(*c.step())
            pool.memset(ident[:, :], 0.0).then_inc(*c.step())
            pool.memset(mask1[:, :], 1.0).then_inc(*c.step())
            pool.memset(neg1[:, :], 0.0).then_inc(*c.step())
            pool.memset(mask2[:, :], 0.0).then_inc(*c.step())
            pool.memset(ntri[:, :], -1.0).then_inc(*c.step())
            pool.memset(rot[:, :], 0.0).then_inc(*c.step())
            pool.wait_ge(*c.last)
            pool.affine_select(out=ident[:, :], in_=ident[:, :], compare_op=ALU.not_equal, fill=1.0,
                                      base=0, pattern=[[-1, P]], channel_multiplier=1).then_inc(*c.step())
            pool.affine_select(out=ntri[:, :], in_=ntri[:, :], compare_op=ALU.is_ge, fill=0.0,
                                      base=0, pattern=[[-1, P]], channel_multiplier=1).then_inc(*c.step())
            for lo, w in ((0, 256), (256, 128)):
                pool.affine_select(out=mask1[:, lo:lo + w], in_=mask1[:, lo:lo + w], compare_op=ALU.is_gt,
                                          fill=0.0, base=0, pattern=[[1, w]], channel_multiplier=-1).then_inc(*c.step())
                pool.affine_select(out=neg1[:, lo:lo + w], in_=neg1[:, lo:lo + w], compare_op=ALU.is_gt,
                                          fill=-BIG, base=0, pattern=[[1, w]], channel_multiplier=-1).then_inc(*c.step())
            for lo in (0, 256):
                pool.affine_select(out=mask2[:, lo:lo + P], in_=mask2[:, lo:lo + P], compare_op=ALU.is_ge,
                                          fill=-BIG, base=0, pattern=[[-1, P]], channel_multiplier=1).then_inc(*c.step())
            half_rope = ROPE // 2
            for sign, base in ((-1.0, -half_rope), (1.0, half_rope)):
                pool.wait_ge(*c.last)
                pool.affine_select(out=rot[NOPE:QK, :], in_=rot[NOPE:QK, :], compare_op=ALU.not_equal,
                                          fill=sign, base=base, pattern=[[-1, ROPE]], channel_multiplier=1).then_inc(*c.step())
            pool.wait_ge(*c.last)
            pool.memset(sums[:, :, :], 0.0).then_inc(*c.event("const", "all"))
            for q in SPLIT:
                pool.wait_ge(sem("w_hi"), over("w_hi", q["s"]))
                if q["s"] >= HL:
                    past = SPLIT[q["s"] - HL]
                    pool.wait_ge(sem("groups"), past["g"] + past["groups"] - 1 + 1)
                n = q["kt"] * q["cols"]
                r, s = q["index"] % RAW, q["s"] % HL
                pool.tensor_tensor(w_lo[:, s, 0:n], raw[:, r, 0:n], w_hi[:, s, 0:n].bitcast(F32),
                                   ALU.subtract).then_inc(sem(f"raw_free{r}"), 1)

        @block.scalar
        def _(act):
            c = Count("act")
            ahead = [0]

            def fn(out_, in_, func, **kw):
                act.wait_ge(*c.last)
                return act.activation(out_, in_, func, **kw)

            def high_halves(at):
                passed = sum(q["split"] for q in PANELS[:at])
                while ahead[0] < min(passed + HL, len(SPLIT)) and SPLIT[ahead[0]]["index"] < at + RAW:
                    q = SPLIT[ahead[0]]
                    act.wait_ge(*landed(q))
                    if q["s"] >= HL:
                        past = SPLIT[q["s"] - HL]
                        act.wait_ge(sem("groups"), past["g"] + past["groups"] - 1 + 1)
                        act.wait_ge(*slot_free(past))
                    n = q["kt"] * q["cols"]
                    act.activation(w_hi[:, q["s"] % HL, 0:n], raw[:, q["index"] % RAW, 0:n], ACT.Copy).then_inc(*c.event("w_hi", q["s"]))
                    ahead[0] += 1

            def take(g, dst, src, func=ACT.Copy, **kw):
                act.wait_ge(sem("groups"), g + 1)
                act.wait_ge(*c.last)
                act.activation(dst, src, func, **kw).then_inc(*c.bank_free(g))

            def square_root(key, region, mean_of, eps, which=0):
                act.wait_ge(sem("stats"), over("stats", ("lat", key[1]) if key[0] in ("lat_q", "lat_kv") else key))
                if key[0] != "norm" or key[1]:
                    act.wait_ge(sem("rstd"), over("rstd", ROOTS[ROOTS.index(key) - 1]))
                fn(root[:, which, :], p_s[:, region * T:region * T + T], ACT.Sqrt, bias=eps,
                   scale=1.0 / mean_of).then_inc(*c.event("root", key))

            def split(key, _):
                o = OPERANDS[key]
                if o["after"] is not None:
                    act.wait_ge(sem("groups"), o["after"] + 1)
                for j, (a, b) in enumerate(o["pieces"]):
                    if o["ready"] == "rows":
                        act.wait_ge(sem("rows"), over("rows", key, j))
                    elif o["ready"]:
                        act.wait_ge(sem("gt_used"), over("gt_used", find(o["ready"], key[1], j if len(o["pieces"]) > 1 else 1)["gt"]))
                    fn(o["hi"][:, a:b, :], o["src"][:, a:b, :], ACT.Copy).then_inc(*c.event("hi", key, j))

            def norm(k, _):
                if k == 0:
                    act.wait_ge(sem("x_landed"), 16)
                else:
                    for s, v in emptied(groups_of("out" if k == 1 else "ff2")):
                        act.wait_ge(s, v)
                fn(tmp, h[:, :, :], ACT.Square).then_inc(*c.event("squares", ("norm", k)))
                square_root(("norm", k), 0, D, RMS_EPS)

            def panel(p, _):
                q = PANELS[p]
                job, l, n, g = q["job"], q["layer"], q["n"], q["g"]
                high_halves(p)
                both = pair(pg[g % 2][:, :])
                if job == "ssm":
                    take(g, ussm[:, 2 * n:2 * n + 2, :], both)
                elif job == "q":
                    take(g, q1[:, 2 * n:2 * n + 2, :], both, scale=DH ** -0.5)
                elif job == "k":
                    take(g, k1[:, 2 * n:2 * n + 2, :], both)
                elif job == "v":
                    take(g, v1[:, :, 256 * n:256 * n + 256], both)
                elif job == "gate":
                    act.wait_ge(sem("groups"), g + 1)
                    fn(gates[:, 2 * n, :], both[:, 0, :], ACT.Sigmoid, bias=col("b_gate", 2 * n)).then_inc(*c.step())
                    take(g, gates[:, 2 * n + 1, :], both[:, 1, :], ACT.Sigmoid, bias=col("b_gate", 2 * n + 1))
                elif job == "glu":
                    for i in range(2):
                        b = pair(pg[(g + i) % 2][:, :])
                        act.wait_ge(sem("groups"), g + i + 1)
                        act.wait_ge(sem("lo"), over("lo", "y", 0))
                        fn(yt[:, 2 * i, :], b[:, 0, :], ACT.Sigmoid, bias=col("b_glu", 2 * i)).then_inc(*c.step())
                        take(g + i, yt[:, 2 * i + 1, :], b[:, 1, :], ACT.Sigmoid, bias=col("b_glu", 2 * i + 1))
                elif job == "ff1":
                    f, f2 = 4 * (n % 2), 4 * (n % 2) + 2
                    for s, v in emptied([g]):
                        act.wait_ge(s, v)
                    if n >= 2:
                        act.wait_ge(sem("ff_lo"), over("ff_lo", n - 2))
                    fn(tmp[:, f2:f2 + 2, :], tmp[:, f:f + 2, :], ACT.Square).then_inc(*c.step())
                    ch = n // 2
                    past = groups_of("ff2")[4 * (ch - 2) + 3] if ch >= 2 else groups_of("glu" if ch == 0 else "up_ssm")[-1]
                    act.wait_ge(sem("groups"), past + 1)
                    fn(v_hi[(ch + 1) % 2][:, 2 * (n % 2):2 * (n % 2) + 2, :], tmp[:, f2:f2 + 2, :], ACT.Copy).then_inc(*c.event("ff_hi", n))
                elif job == "q_lat":
                    take(g, q_lat[:, 2 * n:2 * n + q["cols"] // P, :], both[:, 0:q["cols"] // P, :])
                elif job == "kv_lat":
                    take(g, kv_lat, both)
                elif job == "k_rope":
                    take(g, kpe[NOPE:QK, :], pg[g % 2][NOPE:QK, 0:T])
                elif job == "a2":
                    take(g, acc[:, 2 * n:2 * n + 2, :], both, ACT.Sigmoid)
                elif job == "uq":
                    for i in range(2):
                        a = 4 * n + 2 * i
                        take(g + i, qf[0:QK, a:a + 2, :], pair(pg[(g + i) % 2][0:QK, :]))
                elif job == "ukv":
                    for i in range(4):
                        take(g + i, kf[0:NOPE, 2 * i:2 * i + 2, :], pair(pg[(g + i) % 2][0:NOPE, :]))
                    for i in range(2):
                        take(g + 4 + i, v2[:, i, :], pg[(g + 4 + i) % 2][:, :])
                elif job == "xb":
                    take(g, xbv[:, 2 * n:2 * n + 2, :], both)
                elif job in ("cg", "ag", "bg"):
                    gt_free(q["gt"])
                    act.wait_ge(sem("groups"), g + 1)
                    fn(gtmp[:, q["gt"] % 2, :], pg[g % 2][:, :], ACT.Sigmoid).then_inc(*c.event("sigmoid", q["gt"]))
                elif job in ("branch0", "branch1", "branch2"):
                    before = {"branch1": None, "branch0": "merge1", "branch2": "merge0"}[job]
                    for i in range(2):
                        a = 4 * n + 2 * i
                        if before:
                            act.wait_ge(sem("gt_used"), over("gt_used", find(before, l, a // 2)["gt"]))
                        take(g + i, ybr[:, a:a + 2, :], pair(pg[(g + i) % 2][:, :]))
                elif job in ("merge0", "merge1", "merge2"):
                    gt_free(q["gt"])
                    take(g, gtmp[:, q["gt"] % 2, :], pg[g % 2][:, :], ACT.Sigmoid)

            def gt_free(k):
                if k >= 2:
                    past = next(q for q in PANELS if q["gt"] == k - 2)
                    if past["job"] in ("cg", "ag"):
                        for s, v in emptied([past["g"]]):
                            act.wait_ge(s, v)
                    else:
                        act.wait_ge(sem("gt_used"), over("gt_used", k - 2))

            def s5_prep(_, __):
                act.wait_ge(sem("angle"), over("angle"))
                fn(small[:, 20:22, :], small[:, 18:20, :], ACT.Sin).then_inc(*c.event("sines"))
                act.wait_ge(sem("bt_ps"), over("bt_ps"))
                for k, b in enumerate((p_bu, p_z)):
                    fn(bt[:, k, :, :], b[:, :].rearrange("p (a n) -> p a n", a=4), ACT.Copy).then_inc(*c.event("bt", k))

            def bu(r, _):
                act.wait_ge(sem("bu"), over("bu", r))
                if r >= 2:
                    act.wait_ge(sem("cx"), over("cx", r - 2))
                else:
                    act.wait_ge(sem("pads"), over("pads"))
                fn(xs[:, 2 * (r % 2), :, PAD:PAD + T], pair(p_bu[:, :]), ACT.Copy).then_inc(*c.event("bu_sb", r))

            def s5_out(r, _):
                if r % 4 == 3:
                    f = r // 4
                    act.wait_ge(sem("y_rows"), over("y_rows", f))
                    fn(y1, yv[:, f, :], ACT.Square).then_inc(*c.event("y_sq", f))
                    act.wait_ge(sem("y_inner"), over("y_inner", f))
                    fn(y1, y1, ACT.Sigmoid, scale=2 * math.sqrt(2 / math.pi)).then_inc(*c.event("y_sig", f))

            def stick_scores(hd, _):
                act.wait_ge(sem("z"), over("z", hd))
                if hd:
                    act.wait_ge(sem("soft"), over("soft", hd - 1))
                fn(stick[0], p_z[:, 0:384], ACT.Abs).then_inc(*c.step())
                fn(stick[0], stick[0], ACT.Exp, scale=-1.0).then_inc(*c.step())
                fn(stick[0], stick[0], ACT.Ln, bias=1.0).then_inc(*c.event("log1p", hd))

            def stick_weights(hd, _):
                act.wait_ge(sem("logw"), over("logw", hd))
                fn(stick[2 + hd % 2], stick[2 + hd % 2], ACT.Exp).then_inc(*c.event("w_stick", hd))

            def stick_out(hd, _):
                if hd % 2:
                    i = hd // 2
                    act.wait_ge(sem("o_stick"), over("o_stick", hd))
                    fn(context1[:, i, :], p_o[:, T * (i % 2):T * (i % 2) + T], ACT.Copy).then_inc(*c.event("ctx", i))

            def rope_tables(_, __):
                act.wait_ge(sem("rope_angle"), over("rope_angle"))
                fn(rsin[NOPE:QK, :], rsin[NOPE:QK, :], ACT.Sin).then_inc(*c.step())
                fn(rcos[NOPE:QK, :], rcos[NOPE:QK, :], ACT.Sin).then_inc(*c.event("rope_sines"))

            def prescale(l, _):
                act.wait_ge(sem("rows"), over("rows", ("u", l), 3))
                fn(h[:, :, :], h[:, :, :], ACT.Copy, scale=ALPHA).then_inc(*c.event("alpha_h", l))

            def latent_sums(l, _):
                fn(lat_sq[:, 0:3, :], q_lat, ACT.Square).then_inc(*c.step())
                fn(lat_sq[:, 3:5, :], kv_lat, ACT.Square).then_inc(*c.event("squares", ("lat", l)))

            def latent_norm(l, _):
                square_root(("lat_q", l), 0, QL, RMS_EPS, 0)
                square_root(("lat_kv", l), 1, KVL, RMS_EPS, 1)

            def scores(l, hd):
                b = hd % 2
                act.wait_ge(sem("nmax"), over("nmax", l, hd))
                for tt, (lo, hi) in enumerate(((0, P), (P, 3 * P))):
                    fn(soft[:, b, lo:hi], soft[:, b, lo:hi], ACT.Exp,
                       bias=nmax[:, b, tt:tt + 1], scale=SCALE2, accum_out=sums[:, b, tt:tt + 1]).then_inc(*c.event("probs", l, hd, tt))

            def turn(l, hd):
                act.wait_ge(sem("turned"), over("turned", l, hd))
                fn(soft_t[:, hd % 2, :], p_c[:, 0:384], ACT.Copy).then_inc(*c.event("probs_t", l, hd))

            def ln_a_var(l, _):
                act.wait_ge(sem("centred_a"), over("centred_a", l))
                fn(tmp[:, 0:4, :], acc, ACT.Square).then_inc(*c.event("squares", ("var_a", l)))
                square_root(("var_a", l), 1, W, LN_EPS)

            def ln_a_out(l, _):
                for j in range(WT):
                    act.wait_ge(sem("a_affine"), over("a_affine", l, j))
                    fn(tmp[:, j, :], acc[:, j, :], ACT.Sigmoid).then_inc(*c.event("a_sig", l, j))

            def ln(l, _):
                act.wait_ge(sem("centred"), over("centred", l))
                fn(tmp, h[:, :, :], ACT.Square).then_inc(*c.event("squares", ("var", l)))
                square_root(("var", l), 1, D, LN_EPS)
                act.wait_ge(sem("ln_rows"), over("ln_rows", l))
                for j in range(KT):
                    fn(h[:, j, :], h[:, j, :], ACT.Identity,
                       bias=col(("ln_b", l), j), scale=col(("ln_g", l), j)).then_inc(*(c.event("affine", l) if j == KT - 1 else c.step()))

            act.wait_ge(sem("par_landed"), 16)
            act.wait_ge(sem("const"), over("const", "all"))
            fn(silu_c[:, :], col("c", 0, KT), ACT.Sigmoid).then_inc(*c.event("c_sig"))
            steps = dict(norm=norm, split=split, panel=panel, s5_prep=s5_prep, bu=bu, s5_out=s5_out,
                         stick_scores=stick_scores, stick_weights=stick_weights, stick_out=stick_out,
                         rope_tables=rope_tables, prescale=prescale, latent_sums=latent_sums,
                         latent_norm=latent_norm, scores=scores, turn=turn, ln_a_var=ln_a_var,
                         ln_a_out=ln_a_out, ln=ln)
            for kind, a, b in ORDER:
                if kind in steps:
                    steps[kind](a, b)

        @block.vector
        def _(dve):
            c = Count("dve")

            def tt(out_, a, b, op):
                dve.wait_ge(*c.last)
                return dve.tensor_tensor(out_, a, b, op)

            def ts(out_, a, s1, s2, op0, op1=ALU.bypass):
                dve.wait_ge(*c.last)
                return dve.tensor_scalar(out_, a, s1, s2, op0, op1)

            def stt(out_, a, s, b, op0, op1):
                dve.wait_ge(*c.last)
                return dve.scalar_tensor_tensor(out=out_, in0=a, scalar=s, in1=b, op0=op0, op1=op1)

            def copy(out_, a):
                dve.wait_ge(*c.last)
                return dve.tensor_copy(out_, a)

            def take(g, out_, a, b, op):
                dve.wait_ge(sem("groups"), g + 1)
                dve.wait_ge(*c.last)
                dve.tensor_tensor(out_, a, b, op).then_inc(*c.bank_free(g))

            def split(key, _):
                o = OPERANDS[key]
                for j, (a, b) in enumerate(o["pieces"]):
                    dve.wait_ge(sem("hi"), over("hi", key, j))
                    tt(o["lo"][:, a:b, :], o["src"][:, a:b, :], o["hi"][:, a:b, :].bitcast(F32),
                       ALU.subtract).then_inc(*c.event("lo", key, j))

            def invert(key, which=0):
                dve.wait_ge(sem("root"), over("root", key))
                dve.wait_ge(*c.last)
                dve.reciprocal(rstd[:, which, :], root[:, which, :]).then_inc(*c.event("rstd", key))

            def norm(k, _):
                invert(("norm", k))
                name = ("norm_mix", "norm_mlp", "norm_final")[k]
                for j in range(KT):
                    dst = tmp[:, j, :] if k < 2 else h[:, j, :]
                    stt(dst, h[:, j, :], col(name, j), rstd[:, 0, :], ALU.mult, ALU.mult).then_inc(*(c.event("rows", "u0" if k == 0 else "u2", j // 2) if k < 2 and j % 2 else c.step()))

            def s5_prep(_, __):
                S = lambda k: small[:, k, :]
                dve.wait_ge(sem("par_landed"), 16)
                dve.wait_ge(sem("s5_landed"), 32)

                def exp_parts(x, f, two_n, p, n):
                    ts(f, x, -87.0, 88.0, ALU.max, ALU.min).then_inc(*c.step())
                    ts(n, f, 1.0 / math.log(2.0), ROUND, ALU.mult, ALU.add).then_inc(*c.step())
                    ts(n, n, -ROUND, None, ALU.add).then_inc(*c.step())
                    stt(f, n, -LN2_HI, f, ALU.mult, ALU.add).then_inc(*c.step())
                    stt(f, n, -LN2_LO, f, ALU.mult, ALU.add).then_inc(*c.step())
                    ts(n.bitcast(I32), n, 127.0, None, ALU.add).then_inc(*c.step())
                    ts(two_n.bitcast(I32), n.bitcast(I32), 23, None, ALU.logical_shift_left).then_inc(*c.step())
                    ts(p, f, 1.0 / math.factorial(8), None, ALU.mult).then_inc(*c.step())
                    for k in range(7, 0, -1):
                        stt(p, p, 1.0 / math.factorial(k), f, ALU.add, ALU.mult).then_inc(*c.step())

                f, two_n, p, n = S(0), S(1), S(2), S(3)
                exp_parts(col("log_dt", 0, 16), f, two_n, p, n)
                dt = S(4)
                stt(dt, p, 1.0, two_n, ALU.add, ALU.mult).then_inc(*c.step())
                tt(S(5), col("A_re", 0, 16), dt, ALU.mult).then_inc(*c.step())
                exp_parts(S(5), f, two_n, p, n)
                tt(S(6), p, two_n, ALU.mult).then_inc(*c.step())
                stt(S(6), two_n, -1.0, S(6), ALU.add, ALU.add).then_inc(*c.step())
                tt(S(7), col("A_im", 0, 16), dt, ALU.mult).then_inc(*c.step())
                turns(S(7), S(18), S(8))
                ts(S(19), S(18), 0.5, None, ALU.mult).then_inc(*c.event("angle"))
                dve.wait_ge(sem("sines"), over("sines"))
                sin, half_sin = S(20), S(21)
                cm1 = S(9)
                stt(cm1, half_sin, -2.0, half_sin, ALU.mult, ALU.mult).then_inc(*c.step())
                nre, nim = S(10), S(11)
                stt(nre, cm1, 1.0, S(6), ALU.add, ALU.mult).then_inc(*c.step())
                tt(nre, nre, cm1, ALU.add).then_inc(*c.step())
                stt(nim, S(6), 1.0, sin, ALU.add, ALU.mult).then_inc(*c.step())
                ts(power[:, 0, 0, :], nre, 1.0, None, ALU.add).then_inc(*c.step())
                copy(power[:, 0, 1, :], nim).then_inc(*c.step())
                ts(power[:, 0, 2, :], nim, -1.0, None, ALU.mult).then_inc(*c.step())
                for k in range(1, 8):
                    re, im, nm = (power[:, k - 1, i, :] for i in range(3))
                    tt(S(12), im, nm, ALU.mult).then_inc(*c.step())
                    tt(S(13), re, re, ALU.mult).then_inc(*c.step())
                    tt(power[:, k, 0, :], S(13), S(12), ALU.add).then_inc(*c.step())
                    stt(power[:, k, 1, :], re, 2.0, im, ALU.mult, ALU.mult).then_inc(*c.step())
                    ts(power[:, k, 2, :], power[:, k, 1, :], -1.0, None, ALU.mult).then_inc(*c.step())
                are, aim = col("A_re", 0, 16), col("A_im", 0, 16)
                tt(S(12), are, are, ALU.mult).then_inc(*c.step())
                tt(S(13), aim, aim, ALU.mult).then_inc(*c.step())
                tt(S(12), S(12), S(13), ALU.add).then_inc(*c.step())
                dve.wait_ge(*c.last)
                dve.reciprocal(S(14), S(12)).then_inc(*c.step())
                tt(S(12), nre, are, ALU.mult).then_inc(*c.step())
                tt(S(13), nim, aim, ALU.mult).then_inc(*c.step())
                tt(S(12), S(12), S(13), ALU.add).then_inc(*c.step())
                tt(S(15), S(12), S(14), ALU.mult).then_inc(*c.step())
                tt(S(12), nim, are, ALU.mult).then_inc(*c.step())
                tt(S(13), nre, aim, ALU.mult).then_inc(*c.step())
                tt(S(12), S(12), S(13), ALU.subtract).then_inc(*c.step())
                tt(S(16), S(12), S(14), ALU.mult).then_inc(*c.step())
                dve.wait_ge(*c.last)
                dve.memset(bd, 0.0).then_inc(*c.step())
                wide = [P, 16, 16]
                fre = S(15).unsqueeze(2).broadcast_to(wide)
                fim = S(16).unsqueeze(2).broadcast_to(wide)
                bre, bim = (bst[:, i, :].rearrange("p (r c) -> p r c", r=16) for i in range(2))
                bt3 = btmp.rearrange("p (r c) -> p r c", r=16)
                bt4 = nmean[:, :].rearrange("p (r c) -> p r c", r=16)
                for comp, (x, y, op) in enumerate(((bre, bim, ALU.subtract), (bim, bre, ALU.add))):
                    tt(bt3, fre, x, ALU.mult).then_inc(*c.step())
                    tt(bt4, fim, y, ALU.mult).then_inc(*c.step())
                    for g2 in range(2):
                        rows = slice(64 * g2, 64 * g2 + 64)
                        dst = bd[rows, comp, :].rearrange("p (r g c) -> p r g c", r=16, g=2)[:, :, g2, :]
                        tt(dst, bt3[rows], bt4[rows], op).then_inc(*c.event("b_diag", comp, g2))
                ts(ct[:, 1, :, :], ct[:, 1, :, :], -1.0, None, ALU.mult).then_inc(*c.event("ct"))
                dve.wait_ge(*c.last)
                dve.memset(xs[:, :, :, 0:PAD], 0.0).then_inc(*c.event("pads"))

            def turns(angle, dst, k):
                ts(k, angle, 1.0 / (2 * math.pi), ROUND, ALU.mult, ALU.add).then_inc(*c.step())
                ts(k, k, -ROUND, None, ALU.add).then_inc(*c.step())
                stt(dst, k, -TWO_PI[0], angle, ALU.mult, ALU.add).then_inc(*c.step())
                stt(dst, k, -TWO_PI[1], dst, ALU.mult, ALU.add).then_inc(*c.step())
                stt(dst, k, -TWO_PI[2], dst, ALU.mult, ALU.add).then_inc(*c.step())
                ts(dst, dst, -PI_IN, PI_IN, ALU.max, ALU.min).then_inc(*c.step())

            def scan(r, _):
                dve.wait_ge(sem("bu_sb"), over("bu_sb", r))
                b0 = 2 * (r % 2)
                for k in range(8):
                    d = 1 << k
                    src, dst = xs[:, b0 + k % 2], xs[:, b0 + 1 - k % 2]
                    re, im, nm = (power[:, k, i, r:r + 1] for i in range(3))
                    lo = 0 if d <= PAD else d
                    if lo:
                        copy(dst[:, :, PAD:PAD + d], src[:, :, PAD:PAD + d]).then_inc(*c.step())
                    here, past = slice(PAD + lo, PAD + T), slice(PAD + lo - d, PAD + T - d)
                    stt(dst[:, :, here], src[:, :, past], re, src[:, :, here], ALU.mult, ALU.add).then_inc(*c.step())
                    stt(dst[:, 0, here], src[:, 1, past], nm, dst[:, 0, here], ALU.mult, ALU.add).then_inc(*c.step())
                    stt(dst[:, 1, here], src[:, 0, past], im, dst[:, 1, here],
                        ALU.mult, ALU.add).then_inc(*(c.event("scan", r) if k == 7 else c.step()))

            def s5_out(r, _):
                if r % 4 == 3:
                    f = r // 4
                    dve.wait_ge(sem("cx"), over("cx", r))
                    stt(yv[:, f, :], ussm[:, f, :], col("D_skip", f),
                        p_y[:, T * (f % 2):T * (f % 2) + T], ALU.mult, ALU.add).then_inc(*c.event("y_rows", f))
                    dve.wait_ge(sem("y_sq"), over("y_sq", f))
                    ts(y1, y1, 0.044715, 1.0, ALU.mult, ALU.add).then_inc(*c.step())
                    tt(y1, y1, yv[:, f, :], ALU.mult).then_inc(*c.event("y_inner", f))
                    dve.wait_ge(sem("y_sig"), over("y_sig", f))
                    tt(yv[:, f, :], yv[:, f, :], y1, ALU.mult).then_inc(*(c.event("rows", "y", 0) if f == WT - 1 else c.step()))

            def stick_soft(hd, _):
                dve.wait_ge(sem("log1p"), over("log1p", hd))
                stt(stick[1], p_z[:, 0:384], 0.0, stick[0], ALU.max, ALU.add).then_inc(*c.step())
                tt(stick[1], stick[1], mask1[:, :], ALU.mult).then_inc(*c.event("soft", hd))

            def stick_weights(hd, _):
                dve.wait_ge(sem("fails"), over("fails", hd))
                if hd >= 2:
                    dve.wait_ge(sem("o_stick"), over("o_stick", hd - 2))
                stt(stick[2 + hd % 2], p_c[:, 0:384], 0.0, neg1[:, :], ALU.min, ALU.add).then_inc(*c.event("logw", hd))

            def ada_end(l, _):
                q = find("ada", l, 11)
                dve.wait_ge(*slot_free(q))
                tt(ada[:, l, :], p_s[:, 24 * l:24 * l + 24], col(("b_ada", l), 0, 24), ALU.add).then_inc(*c.event("ada", ("ada", l)))

            def glu_mul(_, __):
                for s, v in emptied(groups_of("glu")):
                    dve.wait_ge(s, v)
                tt(yv, yv, yt, ALU.mult).then_inc(*c.event("rows", "yg", 0))

            def panel(p, _):
                q = PANELS[p]
                job, l, n, g = q["job"], q["layer"], q["n"], q["g"]
                both = pair(pg[g % 2][:, :])
                gt = pair(gtmp[:, q["gt"] % 2, :]) if q["gt"] is not None else None
                if job in ("up_attn", "up_ssm"):
                    for i in range(2):
                        a = 4 * n + 2 * i
                        b = pair(pg[(g + i) % 2][:, :])
                        if job == "up_attn":
                            take(g + i, merged[:, a:a + 2, :], b, gates[:, KT + a:KT + a + 2, :], ALU.mult)
                        else:
                            take(g + i, tmp[:, 0:2, :], b, gates[:, a:a + 2, :], ALU.mult)
                            tt(merged[:, a:a + 2, :], merged[:, a:a + 2, :], tmp[:, 0:2, :],
                               ALU.add).then_inc(*c.event("rows", "u1", a // 2))
                elif job == "out":
                    take(g, h[:, 2 * n:2 * n + 2, :], both, h[:, 2 * n:2 * n + 2, :], ALU.add)
                elif job == "ff2":
                    for i in range(2):
                        a = 4 * (n % 2) + 2 * i
                        take(g + i, h[:, a:a + 2, :], pair(pg[(g + i) % 2][:, :]), h[:, a:a + 2, :], ALU.add)
                elif job == "ff1":
                    f, ch = 4 * (n % 2), n // 2
                    dve.wait_ge(sem("groups"), g + 1)
                    dve.wait_ge(*c.last)
                    dve.tensor_scalar(tmp[:, f:f + 2, :], both, 0.0, None, ALU.max).then_inc(*c.bank_free(g))
                    dve.wait_ge(sem("ff_hi"), over("ff_hi", n))
                    half = slice(2 * (n % 2), 2 * (n % 2) + 2)
                    tt(v_lo[(ch + 1) % 2][:, half, :], tmp[:, f + 2:f + 4, :],
                       v_hi[(ch + 1) % 2][:, half, :].bitcast(F32), ALU.subtract).then_inc(*c.event("ff_lo", n))
                elif job == "a1":
                    for s, v in emptied(groups_of("a2", l)):
                        dve.wait_ge(s, v)
                    take(g, apad[:, 2 * n:2 * n + 2, CONV_A - 1:], both, acc[:, 2 * n:2 * n + 2, :], ALU.mult)
                elif job == "gc":
                    for s, v in emptied(groups_of("xb", l)):
                        dve.wait_ge(s, v)
                    take(g, bpad[:, 2 * n:2 * n + 2, CONV_B - 1:], both, xbv[:, 2 * n:2 * n + 2, :], ALU.mult)
                elif job == "gb":
                    take(g, bconv[:, 2 * n:2 * n + 2, :], both, bconv[:, 2 * n:2 * n + 2, :], ALU.mult)
                elif job in ("cg", "ag", "bg"):
                    dve.wait_ge(sem("sigmoid"), over("sigmoid", q["gt"]))
                    dst = {"cg": cgate, "ag": agate}[job][:, 2 * n:2 * n + 2, :] if job != "bg" else gt
                    take(g, dst, both, gt, ALU.mult)
                    if job == "bg":
                        tt(bconv[:, 2 * n:2 * n + 2, :], bconv[:, 2 * n:2 * n + 2, :], gt, ALU.mult).then_inc(*c.event("gt_used", q["gt"]))
                elif job in ("merge0", "merge1", "merge2"):
                    for s, v in emptied([g, find("branch%s" % job[-1], l, n // 2)["g"] + n % 2]):
                        dve.wait_ge(s, v)
                    a = slice(2 * n, 2 * n + 2)
                    if job == "merge1":
                        tt(mer[:, a, :], gt, ybr[:, a, :], ALU.mult).then_inc(*c.event("gt_used", q["gt"]))
                    else:
                        tt(gt, gt, ybr[:, a, :], ALU.mult).then_inc(*c.step())
                        tt(mer[:, a, :], mer[:, a, :], gt, ALU.add).then_inc(*c.event("gt_used", q["gt"]))
                elif job == "w_o":
                    dve.wait_ge(sem("groups"), g + 1)
                    dve.wait_ge(sem("alpha_h"), over("alpha_h", l))
                    stt(h[:, 2 * n, :], both[:, 0, :], ada[:, l, 16 + 2 * n:17 + 2 * n], h[:, 2 * n, :],
                        ALU.mult, ALU.add).then_inc(*c.step())
                    dve.wait_ge(*c.last)
                    dve.scalar_tensor_tensor(
                        out=h[:, 2 * n + 1, :], in0=both[:, 1, :], scalar=ada[:, l, 17 + 2 * n:18 + 2 * n],
                        in1=h[:, 2 * n + 1, :], op0=ALU.mult, op1=ALU.add).then_inc(*c.bank_free(g))

            def rope_tables(_, __):
                rows = slice(NOPE, QK)
                dve.wait_ge(sem("pos_landed"), 16)
                copy(nmean[rows, :], pos[rows, :]).then_inc(*c.step())
                ts(nmean[rows, :], nmean[rows, :], col("inv_freq")[rows], None, ALU.mult).then_inc(*c.step())
                turns(nmean[rows, :], rsin[rows, :], rcos[rows, :])
                ts(rcos[rows, :], rsin[rows, :], 0.5, None, ALU.mult).then_inc(*c.event("rope_angle"))
                dve.wait_ge(sem("rope_sines"), over("rope_sines"))
                stt(rcos[rows, :], rcos[rows, :], -2.0, rcos[rows, :], ALU.mult, ALU.mult).then_inc(*c.step())
                ts(rcos[rows, :], rcos[rows, :], 1.0, None, ALU.add).then_inc(*c.step())

            def modulate(l, _):
                if l == 0:
                    dve.wait_ge(*c.last)
                    dve.memset(apad[:, :, 0:CONV_A - 1], 0.0).then_inc(*c.step())
                    dve.wait_ge(*c.last)
                    dve.memset(bpad[:, :, 0:CONV_B - 1], 0.0).then_inc(*c.step())
                else:
                    dve.wait_ge(sem("affine"), over("affine", l - 1))
                ts(scale1[:, :], ada[:, l, 8:16], 1.0, None, ALU.add).then_inc(*c.step())
                for j in range(KT):
                    ts(tmp[:, j, :], h[:, j, :], scale1[:, j:j + 1],
                       ada[:, l, j:j + 1], ALU.mult, ALU.add).then_inc(*(c.event("rows", ("u", l), j // 2) if j % 2 else c.step()))

            def latent_norm(l, _):
                for key, which, x, n, name in ((("lat_q", l), 0, q_lat, 3, "q_norm_g"),
                                               (("lat_kv", l), 1, kv_lat, 2, "kv_norm_g")):
                    invert(key, which)
                    for j in range(n):
                        stt(x[:, j, :],
                            x[:, j, :], col((name, l), j), rstd[:, which, :], ALU.mult, ALU.mult).then_inc(*(c.event("rows", ("ql" if which == 0 else "kvl", l), 0) if j == n - 1 else c.step()))

            def rope(l, _):
                rows = slice(NOPE, QK)
                wide = [ROPE, 2, T]
                sin2, cos2 = spread(rsin[rows, :], *wide), spread(rcos[rows, :], *wide)
                dve.wait_ge(sem("rotated"), over("rotated", l, 0))
                tt(kpr[rows, :], p_y[rows, 0:T], rsin[rows, :], ALU.mult).then_inc(*c.step())
                tt(kpe[rows, :], kpe[rows, :], rcos[rows, :], ALU.mult).then_inc(*c.step())
                tt(kpe[rows, :], kpe[rows, :], kpr[rows, :], ALU.add).then_inc(*c.step())
                copy(kf[rows, :, :], spread(kpe[rows, :], ROPE, HEADS, T)).then_inc(*c.step())
                for i in range(4):
                    b = (p_bu, p_z)[i % 2]
                    a = slice(2 * i, 2 * i + 2)
                    dve.wait_ge(sem("rotated"), over("rotated", l, 1 + i))
                    tt(rtmp[rows, :, :], pair(b[rows, :]), sin2, ALU.mult).then_inc(*c.event("rot_read", l, i))
                    tt(qf[rows, a, :], qf[rows, a, :], cos2, ALU.mult).then_inc(*c.step())
                    tt(qf[rows, a, :], qf[rows, a, :], rtmp[rows, :, :], ALU.add).then_inc(*(c.event("roped", l) if i == 3 else c.step()))

            def conv_a(l, j):
                w = lambda k: col(("conv_a_w", l), 4 * k + j)
                ts(acc[:, j, :], apad[:, j, 0:T], w(0), col(("conv_a_b", l), j), ALU.mult, ALU.add).then_inc(*c.step())
                for k in range(1, CONV_A):
                    stt(acc[:, j, :], apad[:, j, k:k + T], w(k),
                        acc[:, j, :], ALU.mult, ALU.add).then_inc(*(c.event("conv_a", l, j) if k == CONV_A - 1 else c.step()))

            def conv_b(l, _):
                for j in range(WT):
                    w = lambda k: col(("conv_b_w", l), 4 * k + j)
                    ts(bconv[:, j, :], bpad[:, j, 0:T], w(0), None, ALU.mult).then_inc(*c.step())
                    for k in range(1, CONV_B):
                        stt(bconv[:, j, :], bpad[:, j, k:k + T], w(k), bconv[:, j, :], ALU.mult, ALU.add).then_inc(*c.step())

            def scores(l, hd):
                b = hd % 2
                dve.wait_ge(sem("scores"), over("scores", l, hd))
                if hd >= 2 or l:
                    dve.wait_ge(sem("turned"), over("turned", l if hd >= 2 else l - 1, (hd - 2) % HEADS))
                tt(soft[:, b, :], p_z[:, 0:384], mask2[:, :], ALU.add).then_inc(*c.step())
                for i, (lo, hi) in enumerate(((0, P), (P, 3 * P))):
                    dve.wait_ge(*c.last)
                    dve.tensor_reduce(mx[:, b, i:i + 1], soft[:, b, lo:hi], AX.X, ALU.max).then_inc(*c.step())
                ts(nmax[:, b, :], mx[:, b, :], -SCALE2, None, ALU.mult).then_inc(*c.event("nmax", l, hd))

            def turn(l, hd):
                b = hd % 2
                dve.wait_ge(sem("probs"), over("probs", l, hd, 1))
                dve.wait_ge(*c.last)
                dve.reciprocal(rsum[:, b, :], sums[:, b, :]).then_inc(*c.step())
                ts(soft[:, b, 0:P], soft[:, b, 0:P], rsum[:, b, 0:1], None, ALU.mult).then_inc(*c.step())
                ts(soft[:, b, P:3 * P], soft[:, b, P:3 * P], rsum[:, b, 1:2], None, ALU.mult).then_inc(*c.event("probs_n", l, hd))

            def context(l, hd):
                if hd % 2:
                    i = hd // 2
                    dve.wait_ge(sem("o2"), over("o2", l, hd))
                    tt(cgate[:, i, :],
                       p_o[:, T * (i % 2):T * (i % 2) + T], cgate[:, i, :], ALU.mult).then_inc(*(c.event("rows", ("c", l), 0) if i == 3 else c.event("ctx_read", l, i)))

            def mean(key, n):
                dve.wait_ge(sem("stats"), over("stats", key))
                ts(nmean[:, :], p_s[:, 0:T], -1.0 / n, None, ALU.mult).then_inc(*c.event("nmean", key))

            def ln_a_mean(l, _):
                mean(("mean_a", l), W)
                tt(acc, acc, spread(nmean[:, :], P, WT, T), ALU.add).then_inc(*c.event("centred_a", l))

            def ln_a_var(l, _):
                invert(("var_a", l))
                tt(acc, acc, spread(rstd[:, 0, :], P, WT, T), ALU.mult).then_inc(*c.step())
                for j in range(WT):
                    ts(acc[:, j, :], acc[:, j, :], col(("ln_a_g", l), j), col(("ln_a_b", l), j),
                       ALU.mult, ALU.add).then_inc(*c.event("a_affine", l, j))

            def ln_a_out(l, _):
                dve.wait_ge(sem("a_sig"), over("a_sig", l, WT - 1))
                tt(acc, acc, tmp[:, 0:4, :], ALU.mult).then_inc(*c.step())
                tt(acc, acc, agate, ALU.mult).then_inc(*c.event("rows", ("a", l), 0))

            def split_m(l):
                pass

            def ln(l, _):
                mean(("mean", l), D)
                tt(h[:, :, :], h[:, :, :], spread(nmean[:, :], P, KT, T), ALU.add).then_inc(*c.event("centred", l))
                invert(("var", l))
                tt(h[:, :, :], h[:, :, :], spread(rstd[:, 0, :], P, KT, T), ALU.mult).then_inc(*c.event("ln_rows", l))

            dve.wait_ge(sem("const"), over("const", "all"))
            dve.wait_ge(sem("c_sig"), over("c_sig"))
            tt(silu_c[:, :], silu_c[:, :], col("c", 0, KT), ALU.mult).then_inc(*c.event("silu_c"))
            steps = dict(norm=norm, split=split, panel=panel, s5_prep=s5_prep, scan=scan, s5_out=s5_out,
                         stick_soft=stick_soft, stick_weights=stick_weights,
                         ada_end=ada_end, glu_mul=glu_mul, rope_tables=rope_tables, modulate=modulate,
                         latent_norm=latent_norm, rope=rope, conv_a=conv_a, conv_b=conv_b, scores=scores,
                         turn=turn, context=context, ln_a_mean=ln_a_mean, ln_a_var=ln_a_var,
                         ln_a_out=ln_a_out, ln=ln)
            for kind, a, b in ORDER:
                if kind in steps:
                    steps[kind](a, b)

        @block.tensor
        def _(pe):
            def sum_tiles(key, src, tiles, region):
                if SUMS.index(key):
                    pe.wait_ge(*sums_before(key))
                for j in range(tiles):
                    ins = pe.matmul(p_s[:, region * T:region * T + T], ones[:, :], src[:, j, :], start=j == 0,
                                    stop=j == tiles - 1)
                return ins

            def three(dst, w_h, w_l, x_h, x_l, first, last_):
                pe.matmul(dst, w_h, x_h, start=first, stop=False)
                pe.matmul(dst, w_h, x_l, start=False, stop=False)
                return pe.matmul(dst, w_l, x_h, start=False, stop=last_)

            def group_start(g):
                if g >= 2:
                    for s, v in emptied([g - 2]):
                        pe.wait_ge(s, v)

            def blocks(q, g, widths, x_hi, x_lo):
                wh, wl = slot(w_hi, q), slot(w_lo, q)
                group_start(g)
                for i, (a, m) in enumerate(widths):
                    for k in range(q["kt"]):
                        ins = three(pg[g % 2][0:m, i * T:i * T + T], wh[:, k, a:a + m], wl[:, k, a:a + m],
                                    x_hi[:, k, :], x_lo[:, k, :], k == 0, k == q["kt"] - 1)
                ins.then_inc(sem("groups"), 1)

            def panel(p, _):
                q = PANELS[p]
                job, l, n, g = q["job"], q["layer"], q["n"], q["g"]
                if job == "ada":
                    pe.wait_ge(*landed(q))
                    pe.wait_ge(sem("silu_c"), over("silu_c"))
                    w = slot(raw, q)
                    pe.wait_ge(*sums_before(("ada", l)))
                    for i in range(2):
                        at = 24 * l + 2 * n + i
                        for k in range(KT):
                            ins = pe.matmul(p_s[:, at:at + 1], w[:, k, P * i:P * i + P], silu_c[:, k:k + 1],
                                            start=k == 0, stop=k == KT - 1)
                    ins.then_inc(sem(f"raw_free{q['index'] % RAW}"), 1)
                    return
                pe.wait_ge(*slot_free(q))
                if job == "ff2":
                    ch = n // 2
                    pe.wait_ge(sem("ff_lo"), over("ff_lo", 2 * ch + 1))
                    xh, xl = v_hi[(ch + 1) % 2], v_lo[(ch + 1) % 2]
                else:
                    key = operand_of(q)
                    o = OPERANDS[key]
                    pe.wait_ge(sem("lo"), over("lo", key, len(o["pieces"]) - 1))
                    xh, xl = o["hi"], o["lo"]
                if job == "v":
                    wh, wl = slot(w_hi, q), slot(w_lo, q)
                    group_start(g)
                    for tt in range(2):
                        for k in range(KT):
                            tok = slice(P * tt, P * tt + P)
                            dst = pg[g % 2][:, T * tt:T * tt + T]
                            pe.matmul(dst, xh[:, k, tok], wh[:, k, :], start=k == 0, stop=False)
                            pe.matmul(dst, xh[:, k, tok], wl[:, k, :], start=False, stop=False)
                            ins = pe.matmul(dst, xl[:, k, tok], wh[:, k, :], start=False, stop=k == KT - 1)
                    ins.then_inc(sem("groups"), 1)
                elif job == "uq":
                    for i in range(2):
                        blocks(q, g + i, [(QK * (2 * i + j), QK) for j in range(2)], xh, xl)
                elif job == "ukv":
                    for i in range(4):
                        blocks(q, g + i, [(P * (2 * i + j), P) for j in range(2)], xh, xl)
                    wh, wl = (slot(x, q).rearrange("p k (h m) -> p k h m", h=HEADS)[:, :, :, NOPE:P] for x in (w_hi, w_lo))
                    for tt in range(2):
                        group_start(g + 4 + tt)
                        dst = pg[(g + tt) % 2][:, :].rearrange("p (h m) -> p h m", h=HEADS)
                        tok = slice(P * tt, P * tt + P)
                        for k in range(q["kt"]):
                            pe.matmul(dst, xh[:, k, tok], wh[:, k], start=k == 0, stop=False)
                            pe.matmul(dst, xh[:, k, tok], wl[:, k], start=False, stop=False)
                            ins = pe.matmul(dst, xl[:, k, tok], wh[:, k], start=False, stop=k == q["kt"] - 1)
                        ins.then_inc(sem("groups"), 1)
                else:
                    for i in range(q["groups"]):
                        left = min(256, q["cols"] - 256 * i)
                        blocks(q, g + i, [(256 * i + P * j, min(P, left - P * j)) for j in range((left + P - 1) // P)],
                               xh, xl)

            def norm(k, _):
                pe.wait_ge(sem("squares"), over("squares", ("norm", k)))
                sum_tiles(("norm", k), tmp, KT, 0).then_inc(*event("stats", ("norm", k)))

            def s5_prep(_, __):
                pe.wait_ge(sem("b_diag"), over("b_diag", 1, 1))
                for comp, b in enumerate((p_bu, p_z)):
                    for f in range(4):
                        ins = pe.transpose(b[:, P * f:P * f + P], bd[:, comp, P * f:P * f + P], ident[:, :])
                ins.then_inc(*event("bt_ps"))

            def bu(r, _):
                pe.wait_ge(sem("bt"), over("bt", 1))
                for s, v in emptied(groups_of("ssm")):
                    pe.wait_ge(s, v)
                if r:
                    pe.wait_ge(sem("bu_sb"), over("bu_sb", r - 1))
                f, rows = r // 4, slice(32 * (r % 4), 32 * (r % 4) + 32)
                for comp in range(2):
                    ins = pe.matmul(p_bu[:, T * comp:T * comp + T], bt[rows, comp, f, :], ussm[rows, f, :],
                                    start=True, stop=True)
                ins.then_inc(*event("bu", r))

            def s5_out(r, _):
                pe.wait_ge(sem("scan"), over("scan", r))
                pe.wait_ge(sem("ct"), over("ct"))
                f, rows = r // 4, slice(32 * (r % 4), 32 * (r % 4) + 32)
                if f:
                    pe.wait_ge(sem("y_rows"), over("y_rows", f - 1))
                x = xs[:, 2 * (r % 2)]
                for comp in range(2):
                    ins = pe.matmul(p_y[rows, T * (f % 2):T * (f % 2) + T], ct[:, comp, f, rows], x[:, comp, PAD:PAD + T],
                                    start=comp == 0, stop=comp == 1)
                ins.then_inc(*event("cx", r))

            def qk(dst, hd, stop):
                rows, f = slice(64 * (hd % 2), 64 * (hd % 2) + 64), hd // 2
                pe.matmul(dst[:, 0:T], k1[rows, f, 0:P], q1[rows, f, :], start=True, stop=stop)

            def qk_rest(dst, hd, stop):
                rows, f = slice(64 * (hd % 2), 64 * (hd % 2) + 64), hd // 2
                return pe.matmul(dst[:, T:T + P], k1[rows, f, P:T], q1[rows, f, P:T], start=True, stop=stop)

            def stick_scores(hd, _):
                for s, v in emptied(groups_of("q") + groups_of("k")):
                    pe.wait_ge(s, v)
                pe.wait_ge(sem("bt"), over("bt", 1))
                if hd:
                    pe.wait_ge(sem("soft"), over("soft", hd - 1))
                qk(p_z, hd, True)
                qk_rest(p_z, hd, True).then_inc(*event("z", hd))

            def stick_weights(hd, _):
                pe.wait_ge(sem("soft"), over("soft", hd))
                if hd:
                    pe.wait_ge(sem("logw"), over("logw", hd - 1))
                qk(p_c, hd, False)
                pe.matmul(p_c[:, 0:T], ntri[:, :], stick[1][:, 0:T], start=False, stop=False)
                pe.matmul(p_c[:, P:T], nones[:, :], stick[1][:, T:T + P], start=False, stop=True)
                qk_rest(p_c, hd, False)
                pe.matmul(p_c[:, T:T + P], ntri[:, :], stick[1][:, T:T + P], start=False, stop=True).then_inc(*event("fails", hd))

            def weighted_values(values, weights, hd):
                rows, at = slice(64 * (hd % 2), 64 * (hd % 2) + 64), T * (hd // 2 % 2)
                pe.matmul(p_o[rows, at:at + T], values[:, 0, DH * hd:DH * hd + DH], weights[:, 0:T], start=True, stop=False)
                return pe.matmul(p_o[rows, at + P:at + T], values[:, 1, DH * hd:DH * hd + DH], weights[:, T:T + P],
                                 start=False, stop=True)

            def stick_out(hd, _):
                pe.wait_ge(sem("w_stick"), over("w_stick", hd))
                for s, v in emptied(groups_of("v")):
                    pe.wait_ge(s, v)
                if hd >= 2:
                    pe.wait_ge(sem("ctx"), over("ctx", hd // 2 - 1))
                weighted_values(v1, stick[2 + hd % 2], hd).then_inc(*event("o_stick", hd))

            def latent_sums(l, _):
                pe.wait_ge(sem("squares"), over("squares", ("lat", l)))
                sum_tiles(("lat", l), lat_sq[:, 0:3, :], 3, 0)
                sum_tiles(("lat", l), lat_sq[:, 3:5, :], 2, 1).then_inc(*event("stats", ("lat", l)))

            def rope(l, _):
                rows = slice(NOPE, QK)
                for s, v in emptied(groups_of("k_rope", l)):
                    pe.wait_ge(s, v)
                pe.matmul(p_y[rows, 0:T], rot[rows, :], kpe[rows, :], start=True, stop=True).then_inc(*event("rotated", l, 0))
                for s, v in emptied(groups_of("uq", l)):
                    pe.wait_ge(s, v)
                for i in range(4):
                    b = (p_bu, p_z)[i % 2]
                    if i >= 2:
                        pe.wait_ge(sem("rot_read"), over("rot_read", l, i - 2))
                    pe.matmul(b[rows, :], rot[rows, :], qf[rows, 2 * i:2 * i + 2, :], start=True, stop=True).then_inc(*event("rotated", l, 1 + i))

            def scores(l, hd):
                pe.wait_ge(sem("roped"), over("roped", l))
                for s, v in emptied(groups_of("ukv", l)):
                    pe.wait_ge(s, v)
                if hd:
                    pe.wait_ge(sem("nmax"), over("nmax", l, hd - 1))
                pe.matmul(p_z[:, 0:P], qf[0:QK, hd, 0:P], kf[0:QK, hd, 0:P], start=True, stop=True)
                pe.matmul(p_z[:, P:3 * P], qf[0:QK, hd, P:T], kf[0:QK, hd, :], start=True, stop=True).then_inc(*event("scores", l, hd))

            def turn(l, hd):
                pe.wait_ge(sem("probs_n"), over("probs_n", l, hd))
                if hd:
                    pe.wait_ge(sem("probs_t"), over("probs_t", l, hd - 1))
                for i in range(3):
                    ins = pe.transpose(p_c[:, P * i:P * i + P], soft[:, hd % 2, P * i:P * i + P], ident[:, :])
                ins.then_inc(*event("turned", l, hd))

            def context(l, hd):
                pe.wait_ge(sem("probs_t"), over("probs_t", l, hd))
                i = hd // 2
                if i:
                    pe.wait_ge(sem("ctx_read"), over("ctx_read", l, i - 1))
                weighted_values(v2, soft_t[:, hd % 2, :], hd).then_inc(*event("o2", l, hd))

            def ln_a_mean(l, _):
                pe.wait_ge(sem("conv_a"), over("conv_a", l, WT - 1))
                sum_tiles(("mean_a", l), acc, WT, 0).then_inc(*event("stats", ("mean_a", l)))

            def ln_a_var(l, _):
                pe.wait_ge(sem("squares"), over("squares", ("var_a", l)))
                sum_tiles(("var_a", l), tmp[:, 0:4, :], WT, 1).then_inc(*event("stats", ("var_a", l)))

            def ln(l, _):
                for s, v in emptied(groups_of("w_o", l)):
                    pe.wait_ge(s, v)
                sum_tiles(("mean", l), h, KT, 0).then_inc(*event("stats", ("mean", l)))
                pe.wait_ge(sem("squares"), over("squares", ("var", l)))
                sum_tiles(("var", l), tmp, KT, 1).then_inc(*event("stats", ("var", l)))

            pe.wait_ge(sem("const"), over("const", "all"))
            steps = dict(norm=norm, panel=panel, s5_prep=s5_prep, bu=bu, s5_out=s5_out, stick_scores=stick_scores,
                         stick_weights=stick_weights, stick_out=stick_out,
                         latent_sums=latent_sums, rope=rope, scores=scores, turn=turn, context=context,
                         ln_a_mean=ln_a_mean, ln_a_var=ln_a_var, ln=ln)
            for kind, a, b in ORDER:
                if kind in steps:
                    steps[kind](a, b)


WEIGHTS = ["w_in", "w_glu", "w_up_ssm", "w_up_attn", "w_gate", "w_out", "w_ff1", "w_ff2", "w_ada_2", "w_in_2",
           "w_a_out_2", "w_b_out_2", "w_uq_2", "w_ukv_2", "w_c_out_2", "w_o_2"]


def columns(v):
    return np.asarray(v).reshape(-1, P).T


def lay_out(x):
    a = {n: np.ascontiguousarray(x[n]) for n in WEIGHTS}
    a["x_t"] = np.ascontiguousarray(np.asarray(x["x"])[0].T)
    a["positions"] = np.ascontiguousarray(x["positions_2"])
    par = np.zeros((P, NPAR), np.float32)

    def put(key, block):
        par[:, COL[key]:COL[key] + block.shape[1]] = block

    for n in ("norm_mix", "b_gate", "norm_mlp", "norm_final", "D_skip", "b_glu"):
        put(n, columns(x[n]))
    put("c", columns(x["c_2"]))
    for n in ("A_re", "A_im"):
        put(n, np.asarray(x[n])[0].reshape(PAIRS, 2 * STATE).T)
    put("log_dt", np.repeat(np.asarray(x["log_dt"])[0].reshape(PAIRS, 2), STATE, axis=1).T)
    freq = np.float32(10000.0) ** (-np.arange(0, ROPE, 2, dtype=np.float32) / np.float32(ROPE))
    rows = np.zeros((P, 1), np.float32)
    rows[NOPE:QK, 0] = np.tile(freq, 2)
    put("inv_freq", rows)
    for l in range(LAYERS):
        for n in ("b_ada", "conv_a_b", "ln_a_g", "ln_a_b", "q_norm_g", "kv_norm_g", "ln_g", "ln_b"):
            put((n, l), columns(x[n + "_2"][l]))
        for n in ("conv_a_w", "conv_b_w"):
            put((n, l), columns(x[n + "_2"][l]))
    a["params"] = par
    b = [np.asarray(x[n])[0].reshape(PAIRS, 2 * STATE, CIN).transpose(1, 0, 2).reshape(P, PAIRS * CIN)
         for n in ("B_re", "B_im")]
    a["b_state"] = np.ascontiguousarray(np.stack(b, 1))
    c = np.zeros((2, STATE, 2, PAIRS, 2, CIN), np.float32)
    for i, n in enumerate(("C_re", "C_im")):
        v = np.asarray(x[n])[0].reshape(PAIRS, 2, CIN, STATE)
        for g in range(2):
            c[g, :, i, :, g, :] = v[:, g].transpose(2, 0, 1)
    a["c_state"] = np.ascontiguousarray(c.reshape(P, 2, 4, P))
    return a


def program(nc, arrays):
    t = {n: nc.dram_tensor(f"in_{n}", a.shape, mybir.dt.from_np(a.dtype), kind="ExternalInput").ap()
         for n, a in arrays.items()}
    out = nc.dram_tensor("out_t", (D, T), F32, kind="ExternalOutput").ap()
    return t, out


def kernel(**inputs):
    import concourse.bacc as bacc
    from concourse.bass_utils import run_bass_kernel_spmd as run

    arrays = lay_out(inputs)
    marks = {}
    for dry in (True, False):
        nc = bacc.Bacc("TRN2", target_bir_lowering=False, num_devices=1)
        t, out = program(nc, arrays)
        build(nc, t, out, marks, dry)
    r = run(nc, [{f"in_{n}": a for n, a in arrays.items()}], core_ids=[0])
    return np.ascontiguousarray(r.results[0]["out_t"].T)[None]
```

```python
import math
from contextlib import ExitStack

import numpy as np

import concourse.bass as bass
from concourse import mybir

F32 = mybir.dt.float32
F32R = mybir.dt.float32r
I32 = mybir.dt.int32
ALU = mybir.AluOpType
ACT = mybir.ActivationFunctionType
AX = mybir.AxisListType

P = 128
T = 256
D = 1024
KT = D // P
W = 512
WT = W // P
HEADS = 8
DH = 64
DFF = 4 * D
GROUPS, CIN, STATE = 32, 16, 64
PAIRS = GROUPS // 2
CONV_A, CONV_B = 31, 3
CONV_PARTS = 4
CONV_STEP = -(-CONV_A // CONV_PARTS)
NOPE, ROPE = 64, 32
QK = NOPE + ROPE
QL, KVL = 384, 256
LAYERS = 2
RMS_EPS, LN_EPS = 1e-6, 1e-5
ALPHA = (2 * LAYERS) ** 0.25
SCALE2 = QK ** -0.5
BIG = 3.0e38

A1, A2, AG = 0, W, 2 * W
XB, GB, GC, BG = 3 * W, 4 * W, 5 * W, 6 * W
CQ = 7 * W
CKV = CQ + QL
CKR = CKV + KVL
CG = CKR + ROPE
CM = CG + W

COL = {}
_at = 0
for _name, _n in (("norm_mix", 8), ("b_gate", 16), ("norm_mlp", 8), ("norm_final", 8), ("D_skip", 4),
                  ("b_glu", 4), ("c", 8), ("A_re", 16), ("A_im", 16), ("log_dt", 16), ("inv_freq", 1)):
    COL[_name] = _at
    _at += _n
for _l in range(LAYERS):
    for _name, _n in (("b_ada", 24), ("conv_a_b", 4), ("ln_a_g", 4), ("ln_a_b", 4), ("conv_b_w", 12),
                      ("q_norm_g", 3), ("kv_norm_g", 2), ("ln_g", 8), ("ln_b", 8), ("conv_a_w", 124)):
        COL[_name, _l] = _at
        _at += _n
NPAR = _at
ADA = LAYERS * 3 * D // 256
ADA_PARTS = ((0, 15), (15, 18), (18, 21), (21, 24))

RAW = 4
HL = 3
SLOT = 2048

LN2_HI, LN2_LO = 0.693359375, -2.12194440e-4
TWO_PI = (6.28125, 1.9350051879882812e-3, 3.0199159819e-7)
PI_IN = 3.1415925
ROUND = 12582912.0


def schedule():
    panels, order = [], []
    count = {"split": 0, "group": 0, "gt": 0}

    def panel(job, layer, n, name, row, col, kt, cols, groups, split=True):
        gt = None
        if job in ("cg", "ag", "bg", "merge0", "merge1", "merge2"):
            gt = count["gt"]
            count["gt"] += 1
        panels.append(dict(index=len(panels), job=job, layer=layer, n=n, name=name, row=row, col=col, kt=kt,
                           cols=cols, split=split, s=count["split"] if split else None, g=count["group"],
                           groups=groups, gt=gt))
        count["split"] += split
        count["group"] += groups
        order.append(("panel", len(panels) - 1, 0))

    def wide(job, layer, name, col, width, row=0):
        for n in range(width // 256):
            panel(job, layer, n, name, row, col + 256 * n, KT, 256, 1)

    def half(job, layer, name, width, row=0):
        for n in range(width // 512):
            panel(job, layer, n, name, row, 512 * n, WT, 512, 2)

    def step(kind, a=0, b=0):
        order.append((kind, a, b))

    def ada_panel(i):
        panel("ada", i // 12, i % 12, "w_ada_2", 0, 256 * (i % 12), KT, 256, 1, split=False)

    def norm_sums(k, j):
        step("norm_squares", k, j)
        step("norm_sums", k, j)

    def norm_steps(k, key, i):
        ada_panel(i)
        norm_sums(k, 3)
        step("ada_take", i)
        step("norm", k)
        ada_panel(i + 1)
        step("ada_turn", i)
        step("ada_take", i + 1)
        ada_panel(i + 2)
        step("ada_turn", i + 1)
        if k == 2:
            step("modulate", 0)
        step("split", key)
        step("ada_take", i + 2)

    step("s5_angle")
    for j in range(4):
        norm_sums(0, j)
    step("norm", 0)
    step("s5_sines")
    step("split", "u0")
    wide("ssm", 0, "w_in", 0, W)
    step("s5_prep")
    wide("q", 0, "w_in", W, W)
    wide("k", 0, "w_in", 2 * W, W)
    wide("v", 0, "w_in", 3 * W, W)
    step("s5_turn")
    ada = 0
    step("bu", 0)
    step("bu", 1)
    step("stick_scores", 0)
    for i in range(PAIRS // 2 + 1):
        if i >= 1:
            step("s5_out", 2 * i - 2)
            step("s5_out", 2 * i - 1)
            step("stick_weights", i - 1)
        if 2 * i + 2 < PAIRS:
            step("bu", 2 * i + 2)
            step("bu", 2 * i + 3)
        if i < PAIRS // 2:
            step("stick_soft", i)
            step("scan", 2 * i)
            step("stick_fails", i)
            if i + 1 < HEADS:
                step("stick_scores", i + 1)
            panel("gate", 0, i, "w_gate", 0, 256 * i, KT, 256, 1)
        if i >= 1:
            step("stick_out", i - 1)
        if i < PAIRS // 2:
            for j in range(2 if i < 7 else 1):
                ada_panel(ada)
                step("ada_take", ada)
                if j:
                    step("ada_turn", ada - 1)
                ada += 1
            step("ada_turn", ada - 1)
    step("ada_end", 0)
    step("split", "ctx")
    step("split", "y")
    half("up_attn", 0, "w_up_attn", D)
    half("glu", 0, "w_glu", W)
    step("glu_mul")
    step("split", "yg")
    half("up_ssm", 0, "w_up_ssm", D)
    step("split", "u1")
    for n in range(4):
        panel("out", 0, n, "w_out", 0, 256 * n, KT, 256, 1)
        if n:
            norm_sums(1, n - 1)
    norm_steps(1, "u2", 15)
    chunks = DFF // W
    for c in range(chunks + 1):
        if c < chunks:
            for n in range(2):
                panel("ff1", 0, 2 * c + n, "w_ff1", 0, W * c + 256 * n, KT, 256, 1)
                if (c, n) == (0, 0):
                    step("ada_turn", 17)
                    step("ada_end", 1)
        if c >= 1:
            for n in range(2):
                panel("ff2", 0, 2 * (c - 1) + n, "w_ff2", W * (c - 1), 512 * n, WT, 512, 2)
        if c == 2:
            step("rope_tables")
    for j in range(3):
        norm_sums(2, j)
    norm_steps(2, ("u", 0), 18)
    for l in range(LAYERS):
        step("prescale", l)
        panel("q_lat", l, 0, "w_in_2", 0, CQ, KT, 256, 1)
        if l == 0:
            step("ada_turn", 20)
            step("ada_end", 2)
        panel("q_lat", l, 1, "w_in_2", 0, CQ + 256, KT, 128, 1)
        panel("kv_lat", l, 0, "w_in_2", 0, CKV, KT, 256, 1)
        panel("k_rope", l, 0, "w_in_2", 0, CKR + ROPE - QK, KT, QK, 1)
        step("latent_sums", l)
        wide("a2", l, "w_in_2", A2, W)
        step("latent_norm", l)
        step("split", ("ql", l))
        step("split", ("kvl", l))
        wide("a1", l, "w_in_2", A1, W)
        for n in range(2):
            panel("uq", l, n, "w_uq_2", 0, 4 * QK * n, QL // P, 4 * QK, 2)
        panel("ukv", l, 0, "w_ukv_2", 0, 0, KVL // P, 1024, 6)
        step("conv_a", l, 0)
        step("conv_a", l, 1)
        step("rope", l)
        wide("cg", l, "w_in_2", CG, W)
        between = [(job, at, n) for job, at in (("xb", XB), ("gc", GC), ("gb", GB), ("bg", BG), ("ag", AG)) for n in range(2)]
        for h in range(HEADS + 2):
            if h < HEADS:
                step("scores", l, h)
            if h == 4:
                step("conv_b", l)
            job, at, n = between[h]
            panel(job, l, n, "w_in_2", 0, at + 256 * n, KT, 256, 1)
            if 1 <= h <= HEADS:
                step("turn", l, h - 1)
            if h >= 2:
                step("context", l, h - 2)
            if h < 6:
                step("conv_a", l, h + 2)
            if h == 7:
                step("ln_a_mean", l)
                step("split", ("b", l))
            if h == 8:
                step("ln_a_var", l)
        half("branch1", l, "w_b_out_2", D)
        step("ln_a_out", l)
        step("split", ("a", l))
        wide("merge1", l, "w_in_2", CM + D, D)
        half("branch0", l, "w_a_out_2", D)
        step("split", ("c", l))
        wide("merge0", l, "w_in_2", CM, D)
        half("branch2", l, "w_c_out_2", D)
        wide("merge2", l, "w_in_2", CM + 2 * D, D)
        step("split", ("m", l))
        for n in range(4):
            panel("w_o", l, n, "w_o_2", 0, 256 * n, KT, 256, 1)
            if n:
                step("ln_mean", l, n - 1)
        if l == 0:
            ada_panel(21)
        step("ln_mean", l, 3)
        if l == 0:
            step("ada_take", 21)
        step("ln_centre", l)
        if l == 0:
            ada_panel(22)
            step("ada_turn", 21)
            step("ada_take", 22)
        step("ln", l)
        if l == 0:
            ada_panel(23)
            step("ada_turn", 22)
            step("ada_take", 23)
            step("ada_turn", 23)
            step("ada_end", 3)
        step("ln_affine", l)
        if l == 0:
            step("modulate", 1)
            step("split", ("u", 1))
    return panels, order


PANELS, ORDER = schedule()
SPLIT = [q for q in PANELS if q["split"]]


def groups_of(job, layer=0):
    return [g for q in PANELS if q["job"] == job and q["layer"] == layer for g in range(q["g"], q["g"] + q["groups"])]


def find(job, layer=0, n=0):
    return next(q for q in PANELS if q["job"] == job and q["layer"] == layer and q["n"] == n)


ROOTS = [("norm", 0), ("norm", 1), ("norm", 2)]
for _l in range(LAYERS):
    ROOTS += [("lat_q", _l), ("lat_kv", _l), ("var_a", _l), ("var", _l)]

SUMS = [("norm", 0), ("ada", 0), ("norm", 1), ("norm", 2)]
for _l in range(LAYERS):
    SUMS += [("lat", _l), ("mean_a", _l), ("var_a", _l), ("mean", _l), ("var", _l)]


def build(nc, t, out, marks, dry):
    ctx = ExitStack()
    with ctx:
        sems = {}
        counts = {}

        def sem(name):
            if name not in sems:
                sems[name] = ctx.enter_context(nc.semaphore(name))
                counts[name] = 0
            return sems[name]

        def event(name, *key):
            s = sem(name)
            counts[name] += 1
            marks[(name, *key)] = counts[name]
            return s, 1

        def over(name, *key):
            sem(name)
            return 1 if dry and (name, *key) not in marks else marks[(name, *key)]

        def emptied(groups):
            for b in range(2):
                of_bank = [g for g in groups if g % 2 == b]
                if of_bank:
                    yield sem(f"bank_free{b}"), max(of_bank) // 2 + 1

        def landed(q):
            return sem(f"raw{q['index'] % RAW}"), 16 * (q["index"] // RAW + 1)

        def slot_free(q):
            return sem(f"raw_free{q['index'] % RAW}"), q["index"] // RAW + 1

        class Count:

            def __init__(self, own):
                self.own = own
                self.last = (sem(own), 0)

            def event(self, name, *key):
                s, _ = event(name, *key)
                self.last = (s, counts[name])
                return s, 1

            def step(self):
                return self.event(self.own)

            def bank_free(self, g):
                self.last = (sem(f"bank_free{g % 2}"), g // 2 + 1)
                return self.last[0], 1

        def sb(name, shape, dt=F32):
            return ctx.enter_context(nc.sbuf_tensor(name, shape, dt))

        def bank(name):
            return ctx.enter_context(nc.psum_tensor(name, [P, 512], F32))

        raw = sb("raw", [P, RAW, SLOT])
        w_hi = sb("w_hi", [P, HL, SLOT], F32R)
        w_lo = sb("w_lo", [P, HL, SLOT], F32R)
        u_hi = sb("u_hi", [P, KT, T], F32R)
        u_lo = sb("u_lo", [P, KT, T], F32R)
        v_hi = [sb("va_hi", [P, WT, T], F32R), sb("vb_hi", [P, WT, T], F32R)]
        v_lo = [sb("va_lo", [P, WT, T], F32R), sb("vb_lo", [P, WT, T], F32R)]
        h = sb("h", [P, KT, T])
        par = sb("par", [P, NPAR])
        ident = sb("ident", [P, P])
        ones = sb("ones", [P, P])
        ntri = sb("ntri", [P, P])
        nones = sb("nones", [P, P])
        mask1 = sb("mask1", [P, 384])
        neg1 = sb("neg1", [P, 384])
        mask2 = sb("mask2", [P, 384])
        rot = sb("rot", [P, ROPE])
        pos = sb("pos", [P, T], I32)
        rcos = sb("rcos", [P, T])
        rsin = sb("rsin", [P, T])
        root = sb("root", [P, 2, T])
        rstd = sb("rstd", [P, 2, T])
        nmean = sb("nmean", [P, T])
        silu_c = sb("silu_c", [P, KT])
        ada = sb("ada", [P, LAYERS, 24])
        scale1 = sb("scale1", [P, KT])
        sums = sb("sums", [P, 2, 2])
        nmax = sb("nmax", [P, 2, 2])
        mx = sb("mx", [P, 2, 2])
        rsum = sb("rsum", [P, 2, 2])
        AREA = 18150
        area = sb("area", [P, AREA])
        spot = [0]

        def cut(*shape):
            n = math.prod(shape)
            a = area[:, spot[0]:spot[0] + n]
            spot[0] += n
            assert spot[0] <= AREA, spot
            if len(shape) == 2:
                return a.rearrange("p (a b) -> p a b", a=shape[0])
            if len(shape) == 3:
                return a.rearrange("p (a b c) -> p a b c", a=shape[0], b=shape[1])
            return a

        def pair(ap):
            return ap.rearrange("p (a n) -> p a n", a=2)

        tmp = cut(KT, T)
        gates = cut(16, T)
        ussm = cut(WT, T)
        q1 = cut(WT, T)
        k1 = cut(WT, T)
        v1 = cut(2, W)
        merged = cut(KT, T)
        ct = cut(2, 4, P)
        bt = cut(2, 4, P)
        bst = merged[:, 0:2, :]
        bd = merged[:, 2:6, :].rearrange("p (a b) n -> p a (b n)", a=2)
        btmp = merged[:, 6:7, :].rearrange("p a n -> p (a n)")
        PAD = 8
        state4 = cut(2 * (PAD + T))
        small = state4[:, 0:22 * 16].rearrange("p (a n) -> p a n", a=22)
        power = cut(8, 3, 16)
        xs = cut(4, 2, PAD + T)
        state3 = merged[:, 4:8, :].rearrange("p a n -> p (a n)")[:, 0:2 * (PAD + T)]
        states = [xs[:, 0], xs[:, 1], pair(state3), pair(state4)]
        other = [xs[:, 2], xs[:, 3]]
        stick_w = cut(2, 384)
        stick_z = tmp[:, 4:7, :].rearrange("p a n -> p (a n)").rearrange("p (a n) -> p a n", a=2)
        stick = [stick_z[:, 0], stick_z[:, 1], stick_w[:, 0], stick_w[:, 1]]
        context1 = merged[:, 0:4, :]
        yv = tmp[:, 0:4, :]
        yt = tmp[:, 4:8, :]
        y1 = tmp[:, 7, :]
        spot[0] = KT * T
        qf = cut(HEADS, T)
        kf = cut(HEADS, T)
        v2 = cut(2, W)
        q_lat = cut(3, T)
        kv_lat = cut(2, T)
        kpe = cut(T)
        kpr = cut(T)
        apad = cut(WT, T + CONV_A - 1)
        acc = cut(WT, T)
        agate = cut(WT, T)
        bpad = cut(WT, T + CONV_B - 1)
        cgate = cut(WT, T)
        lat_sq = cut(5, T)
        soft = cut(2, 384)
        soft_t = cut(2, 384)
        rtmp = tmp[:, 0:2, :]
        gtmp = cut(2, 512)
        xbv = lat_sq[:, 0:4, :]
        bconv = tmp[:, 4:8, :]
        ybr = qf
        mer = kf

        pg = [bank("pg0"), bank("pg1")]
        p_bu, p_y, p_z, p_c, p_o, p_s = (bank(n) for n in ("p_bu", "p_y", "p_z", "p_c", "p_o", "p_s"))

        def col(name, n=0, w=1):
            a = COL[name] + n
            return par[:, a:a + w]

        def spread(ap, *shape):
            return ap.unsqueeze(1).broadcast_to(list(shape))

        def slot(tensor, q):
            n = q["index"] % RAW if tensor is raw else q["s"] % HL
            return tensor[:, n, 0:q["kt"] * q["cols"]].rearrange("p (k n) -> p k n", k=q["kt"])

        def operand(src, hi, lo, pieces, ready, after):
            return dict(src=src, hi=hi, lo=lo, pieces=pieces, ready=ready, after=after)

        def u_operand(src, ready, after):
            return operand(src, u_hi, u_lo, [(2 * j, 2 * j + 2) for j in range(4)], ready, after)

        def v_operand(src, n, tiles, ready, after):
            return operand(src, v_hi[n], v_lo[n], [(0, tiles)], ready, after)

        OPERANDS = {
            "u0": u_operand(tmp, "rows", None),
            "ctx": v_operand(context1, 0, WT, None, None),
            "y": v_operand(yv, 1, WT, "rows", None),
            "yg": v_operand(yv, 0, WT, "rows", groups_of("up_attn")[-1]),
            "u1": u_operand(merged, "rows", groups_of("gate")[-1]),
            "u2": u_operand(tmp, "rows", groups_of("out")[-1]),
        }
        for l in range(LAYERS):
            OPERANDS["u", l] = u_operand(tmp, "rows", groups_of("ff1")[-1] if l == 0 else groups_of("w_o", 0)[-1])
            OPERANDS["ql", l] = v_operand(q_lat, 1, 3, "rows",
                                          groups_of("ff2")[-1] if l == 0 else groups_of("branch2", 0)[-1])
            OPERANDS["kvl", l] = v_operand(kv_lat, 0, 2, "rows",
                                           groups_of("ff2")[-1] if l == 0 else groups_of("branch0", 0)[-1])
            OPERANDS["b", l] = v_operand(bconv, 1, WT, "bg", groups_of("uq", l)[-1])
            OPERANDS["a", l] = v_operand(acc, 0, WT, "rows", groups_of("ukv", l)[-1])
            OPERANDS["c", l] = v_operand(cgate, 1, WT, "rows", groups_of("branch1", l)[-1])
            OPERANDS["m", l] = u_operand(mer, "merge2", groups_of("merge2", l)[-1])

        FUSED = ("u0", "u2", ("u", 0), ("u", 1))

        USES = {"ssm": "u0", "q": "u0", "k": "u0", "v": "u0", "gate": "u0", "up_attn": "ctx", "glu": "y",
                "up_ssm": "yg", "out": "u1", "ff1": "u2"}

        def operand_of(q):
            if q["job"] in USES:
                return USES[q["job"]]
            own = {"uq": "ql", "ukv": "kvl", "branch1": "b", "branch0": "a", "branch2": "c", "w_o": "m"}
            return own.get(q["job"], "u"), q["layer"]

        def sums_before(key):
            key = SUMS[SUMS.index(key) - 1]
            name = "ada" if key[0] == "ada" else "nmean" if key[0] in ("mean_a", "mean") else "root"
            return sem(name), over(name, 0) if key[0] == "ada" else over(name, ("lat_kv", key[1]) if key[0] == "lat" else key)

        block = ctx.enter_context(nc.Block())

        @block.sync
        def _(sp):
            for j in range(4):
                sp.dma_start(h[:, 2 * j:2 * j + 2, :], t["x_t"].rearrange("(k p) n -> p k n", p=P)[:, 2 * j:2 * j + 2, :]
                             ).then_inc(sem(f"x_landed{j}"), 16)
            for q in PANELS:
                n = q["index"] % RAW
                if q["index"] >= RAW:
                    sp.wait_ge(sem(f"raw_free{n}"), q["index"] // RAW)
                w = t[q["name"]][q["layer"], q["row"]:q["row"] + P * q["kt"], q["col"]:q["col"] + q["cols"]]
                sp.dma_start(slot(raw, q), w.rearrange("(k p) n -> p k n", p=P)).then_inc(sem(f"raw{n}"), 16)
            for j in range(4):
                sp.wait_ge(sem("affine"), over("affine", LAYERS - 1, 2 * j + 1))
                sp.dma_start(out.rearrange("(k p) n -> p k n", p=P)[:, 2 * j:2 * j + 2, :],
                             h[:, 2 * j:2 * j + 2, :]).then_inc(sem("stored"), 16)
            sp.wait_ge(sem("stored"), 4 * 16)

        @block.gpsimd
        def _(pool):
            c = Count("const")
            pool.dma_start(par[:, :], t["params"]).then_inc(sem("par_landed"), 16)
            pool.dma_start(bst, t["b_state"]).then_inc(sem("s5_landed"), 16)
            pool.dma_start(ct, t["c_state"]).then_inc(sem("s5_landed"), 16)
            pool.dma_start(pos[NOPE:QK, :], t["positions"].partition_broadcast(ROPE)).then_inc(sem("pos_landed"), 16)
            pool.memset(ones[:, :], 1.0).then_inc(*c.step())
            pool.memset(nones[:, :], -1.0).then_inc(*c.step())
            pool.memset(ident[:, :], 0.0).then_inc(*c.step())
            pool.memset(mask1[:, :], 1.0).then_inc(*c.step())
            pool.memset(neg1[:, :], 0.0).then_inc(*c.step())
            pool.memset(mask2[:, :], 0.0).then_inc(*c.step())
            pool.memset(ntri[:, :], -1.0).then_inc(*c.step())
            pool.memset(rot[:, :], 0.0).then_inc(*c.step())
            pool.wait_ge(*c.last)
            pool.affine_select(out=ident[:, :], in_=ident[:, :], compare_op=ALU.not_equal, fill=1.0,
                                      base=0, pattern=[[-1, P]], channel_multiplier=1).then_inc(*c.step())
            pool.affine_select(out=ntri[:, :], in_=ntri[:, :], compare_op=ALU.is_ge, fill=0.0,
                                      base=0, pattern=[[-1, P]], channel_multiplier=1).then_inc(*c.step())
            for lo, w in ((0, 256), (256, 128)):
                pool.affine_select(out=mask1[:, lo:lo + w], in_=mask1[:, lo:lo + w], compare_op=ALU.is_gt,
                                          fill=0.0, base=0, pattern=[[1, w]], channel_multiplier=-1).then_inc(*c.step())
                pool.affine_select(out=neg1[:, lo:lo + w], in_=neg1[:, lo:lo + w], compare_op=ALU.is_gt,
                                          fill=-BIG, base=0, pattern=[[1, w]], channel_multiplier=-1).then_inc(*c.step())
            for lo in (0, 256):
                pool.affine_select(out=mask2[:, lo:lo + P], in_=mask2[:, lo:lo + P], compare_op=ALU.is_ge,
                                          fill=-BIG, base=0, pattern=[[-1, P]], channel_multiplier=1).then_inc(*c.step())
            half_rope = ROPE // 2
            for sign, base in ((-1.0, -half_rope), (1.0, half_rope)):
                pool.wait_ge(*c.last)
                pool.affine_select(out=rot[NOPE:QK, :], in_=rot[NOPE:QK, :], compare_op=ALU.not_equal,
                                          fill=sign, base=base, pattern=[[-1, ROPE]], channel_multiplier=1).then_inc(*c.step())
            pool.wait_ge(*c.last)
            pool.memset(sums[:, :, :], 0.0).then_inc(*c.event("const", "all"))
            for q in SPLIT:
                pool.wait_ge(sem("w_hi"), over("w_hi", q["s"]))
                if q["s"] >= HL:
                    past = SPLIT[q["s"] - HL]
                    pool.wait_ge(sem("groups"), past["g"] + past["groups"] - 1 + 1)
                n = q["kt"] * q["cols"]
                r, s = q["index"] % RAW, q["s"] % HL
                pool.tensor_tensor(w_lo[:, s, 0:n], raw[:, r, 0:n], w_hi[:, s, 0:n].bitcast(F32),
                                   ALU.subtract).then_inc(sem(f"raw_free{r}"), 1)

        @block.scalar
        def _(act):
            c = Count("act")
            ahead = [0]

            def fn(out_, in_, func, **kw):
                act.wait_ge(*c.last)
                return act.activation(out_, in_, func, **kw)

            def high_halves(at):
                passed = sum(q["split"] for q in PANELS[:at])
                within = RAW if PANELS[at]["split"] else 2
                while ahead[0] < min(passed + HL, len(SPLIT)) and SPLIT[ahead[0]]["index"] < at + within:
                    q = SPLIT[ahead[0]]
                    act.wait_ge(*landed(q))
                    if q["s"] >= HL:
                        past = SPLIT[q["s"] - HL]
                        act.wait_ge(sem("groups"), past["g"] + past["groups"] - 1 + 1)
                        act.wait_ge(*slot_free(past))
                    n = q["kt"] * q["cols"]
                    act.activation(w_hi[:, q["s"] % HL, 0:n], raw[:, q["index"] % RAW, 0:n], ACT.Copy).then_inc(*c.event("w_hi", q["s"]))
                    ahead[0] += 1

            def take(g, dst, src, func=ACT.Copy, **kw):
                act.wait_ge(sem("groups"), g + 1)
                act.wait_ge(*c.last)
                act.activation(dst, src, func, **kw).then_inc(*c.bank_free(g))

            def square_root(key, region, mean_of, eps, which=0):
                act.wait_ge(sem("stats"), over("stats", ("lat", key[1]) if key[0] in ("lat_q", "lat_kv") else key))
                if key[0] != "norm" or key[1]:
                    act.wait_ge(sem("rstd"), over("rstd", ROOTS[ROOTS.index(key) - 1]))
                fn(root[:, which, :], p_s[:, region * T:region * T + T], ACT.Sqrt, bias=eps,
                   scale=1.0 / mean_of).then_inc(*c.event("root", key))

            def split(key, _):
                o = OPERANDS[key]
                if o["after"] is not None:
                    act.wait_ge(sem("groups"), o["after"] + 1)
                if isinstance(key, tuple) and key[0] == "u":
                    l = key[1]
                    act.wait_ge(sem("scale1"), over("scale1", l))
                    for j in range(KT):
                        if l == 0:
                            act.wait_ge(sem("h_rows"), over("h_rows", j))
                        fn(u_hi[:, j, :], h[:, j, :], ACT.Identity, bias=ada[:, l, j:j + 1],
                           scale=scale1[:, j:j + 1]).then_inc(*(c.event("hi", key, j // 2) if j % 2 else c.step()))
                    return
                for j, (a, b) in enumerate(o["pieces"]):
                    if o["ready"] == "rows":
                        act.wait_ge(sem("rows"), over("rows", key, j))
                    elif o["ready"]:
                        act.wait_ge(sem("gt_used"), over("gt_used", find(o["ready"], key[1], j if len(o["pieces"]) > 1 else 1)["gt"]))
                    fn(o["hi"][:, a:b, :], o["src"][:, a:b, :], ACT.Copy).then_inc(*c.event("hi", key, j))

            def norm_squares(k, j):
                if k == 0:
                    act.wait_ge(sem(f"x_landed{j}"), 16)
                else:
                    for s, v in emptied([groups_of("out" if k == 1 else "ff2")[j - 4]]):
                        act.wait_ge(s, v)
                fn(tmp[:, 2 * j:2 * j + 2, :], h[:, 2 * j:2 * j + 2, :], ACT.Square).then_inc(*c.event("squares", ("norm", k), j))

            def norm(k, _):
                square_root(("norm", k), 0, D, RMS_EPS)

            def ada_take(i, _):
                if i:
                    act.wait_ge(sem("ada_turned"), over("ada_turned", i - 1))
                g = find("ada", i // 12, i % 12)["g"]
                take(g, root[0:1, 1, :], pg[g % 2][0:1, 0:256])

            def panel(p, _):
                q = PANELS[p]
                job, l, n, g = q["job"], q["layer"], q["n"], q["g"]
                high_halves(p)
                both = pair(pg[g % 2][:, :])
                if job == "ssm":
                    take(g, ussm[:, 2 * n:2 * n + 2, :], both)
                elif job == "q":
                    take(g, q1[:, 2 * n:2 * n + 2, :], both, scale=DH ** -0.5)
                elif job == "k":
                    take(g, k1[:, 2 * n:2 * n + 2, :], both)
                elif job == "v":
                    take(g, v1[:, :, 256 * n:256 * n + 256], both)
                elif job == "gate":
                    act.wait_ge(sem("groups"), g + 1)
                    fn(gates[:, 2 * n, :], both[:, 0, :], ACT.Sigmoid, bias=col("b_gate", 2 * n)).then_inc(*c.step())
                    take(g, gates[:, 2 * n + 1, :], both[:, 1, :], ACT.Sigmoid, bias=col("b_gate", 2 * n + 1))
                elif job == "glu":
                    for i in range(2):
                        b = pair(pg[(g + i) % 2][:, :])
                        act.wait_ge(sem("groups"), g + i + 1)
                        act.wait_ge(sem("lo"), over("lo", "y", 0))
                        fn(yt[:, 2 * i, :], b[:, 0, :], ACT.Sigmoid, bias=col("b_glu", 2 * i)).then_inc(*c.step())
                        take(g + i, yt[:, 2 * i + 1, :], b[:, 1, :], ACT.Sigmoid, bias=col("b_glu", 2 * i + 1))
                elif job == "ff1":
                    f, f2 = 4 * (n % 2), 4 * (n % 2) + 2
                    for s, v in emptied([g]):
                        act.wait_ge(s, v)
                    if n >= 2:
                        act.wait_ge(sem("ff_lo"), over("ff_lo", n - 2))
                    fn(tmp[:, f2:f2 + 2, :], tmp[:, f:f + 2, :], ACT.Square).then_inc(*c.step())
                    ch = n // 2
                    past = groups_of("ff2")[4 * (ch - 2) + 3] if ch >= 2 else groups_of("glu" if ch == 0 else "up_ssm")[-1]
                    act.wait_ge(sem("groups"), past + 1)
                    fn(v_hi[(ch + 1) % 2][:, 2 * (n % 2):2 * (n % 2) + 2, :], tmp[:, f2:f2 + 2, :], ACT.Copy).then_inc(*c.event("ff_hi", n))
                elif job == "q_lat":
                    take(g, q_lat[:, 2 * n:2 * n + q["cols"] // P, :], both[:, 0:q["cols"] // P, :])
                elif job == "kv_lat":
                    take(g, kv_lat, both)
                elif job == "k_rope":
                    take(g, kpe[NOPE:QK, :], pg[g % 2][NOPE:QK, 0:T])
                elif job == "a2":
                    take(g, acc[:, 2 * n:2 * n + 2, :], both, ACT.Sigmoid)
                elif job == "uq":
                    for i in range(2):
                        a = 4 * n + 2 * i
                        take(g + i, qf[0:QK, a:a + 2, :], pair(pg[(g + i) % 2][0:QK, :]))
                elif job == "ukv":
                    for i in range(4):
                        take(g + i, kf[0:NOPE, 2 * i:2 * i + 2, :], pair(pg[(g + i) % 2][0:NOPE, :]))
                    for i in range(2):
                        take(g + 4 + i, v2[:, i, :], pg[(g + 4 + i) % 2][:, :])
                elif job == "xb":
                    take(g, xbv[:, 2 * n:2 * n + 2, :], both)
                elif job in ("cg", "ag", "bg"):
                    gt_free(q["gt"])
                    act.wait_ge(sem("groups"), g + 1)
                    fn(gtmp[:, q["gt"] % 2, :], pg[g % 2][:, :], ACT.Sigmoid).then_inc(*c.event("sigmoid", q["gt"]))
                elif job in ("branch0", "branch1", "branch2"):
                    before = {"branch1": None, "branch0": "merge1", "branch2": "merge0"}[job]
                    for i in range(2):
                        a = 4 * n + 2 * i
                        if before:
                            act.wait_ge(sem("gt_used"), over("gt_used", find(before, l, a // 2)["gt"]))
                        take(g + i, ybr[:, a:a + 2, :], pair(pg[(g + i) % 2][:, :]))
                elif job in ("merge0", "merge1", "merge2"):
                    gt_free(q["gt"])
                    take(g, gtmp[:, q["gt"] % 2, :], pg[g % 2][:, :], ACT.Sigmoid)

            def gt_free(k):
                if k >= 2:
                    past = next(q for q in PANELS if q["gt"] == k - 2)
                    if past["job"] in ("cg", "ag"):
                        for s, v in emptied([past["g"]]):
                            act.wait_ge(s, v)
                    else:
                        act.wait_ge(sem("gt_used"), over("gt_used", k - 2))

            def s5_sines(_, __):
                act.wait_ge(sem("angle"), over("angle"))
                fn(small[:, 20:22, :], small[:, 18:20, :], ACT.Sin).then_inc(*c.event("sines"))

            def s5_turn(_, __):
                act.wait_ge(sem("bt_ps"), over("bt_ps"))
                for k, b in enumerate((p_bu, p_z)):
                    fn(bt[:, k, :, :], b[:, :].rearrange("p (a n) -> p a n", a=4), ACT.Copy).then_inc(*c.event("bt", k))

            def bu(r, _):
                act.wait_ge(sem("bu"), over("bu", r))
                if r >= 4:
                    act.wait_ge(sem("cx"), over("cx", r - 4))
                else:
                    act.wait_ge(sem("pads"), over("pads"))
                fn(states[r % 4][:, :, PAD:PAD + T], pair(p_bu[:, :]), ACT.Copy).then_inc(*c.event("bu_sb", r))

            def s5_out(r, _):
                if r % 4 == 3:
                    f = r // 4
                    act.wait_ge(sem("y_rows"), over("y_rows", f))
                    fn(y1, yv[:, f, :], ACT.Square).then_inc(*c.event("y_sq", f))
                    act.wait_ge(sem("y_inner"), over("y_inner", f))
                    fn(y1, y1, ACT.Sigmoid, scale=2 * math.sqrt(2 / math.pi)).then_inc(*c.event("y_sig", f))

            def stick_scores(hd, _):
                act.wait_ge(sem("z"), over("z", hd))
                if hd:
                    act.wait_ge(sem("soft"), over("soft", hd - 1))
                fn(stick[0], p_z[:, 0:384], ACT.Abs).then_inc(*c.step())
                fn(stick[0], stick[0], ACT.Exp, scale=-1.0).then_inc(*c.step())
                fn(stick[0], stick[0], ACT.Ln, bias=1.0).then_inc(*c.event("log1p", hd))

            def stick_weights(hd, _):
                act.wait_ge(sem("logw"), over("logw", hd))
                fn(stick[2 + hd % 2], stick[2 + hd % 2], ACT.Exp).then_inc(*c.event("w_stick", hd))

            def stick_out(hd, _):
                if hd % 2:
                    i = hd // 2
                    act.wait_ge(sem("o_stick"), over("o_stick", hd))
                    fn(context1[:, i, :], p_o[:, T * (i % 2):T * (i % 2) + T], ACT.Copy).then_inc(*c.event("ctx", i))

            def rope_tables(_, __):
                act.wait_ge(sem("rope_angle"), over("rope_angle"))
                fn(rsin[NOPE:QK, :], rsin[NOPE:QK, :], ACT.Sin).then_inc(*c.step())
                fn(rcos[NOPE:QK, :], rcos[NOPE:QK, :], ACT.Sin).then_inc(*c.event("rope_sines"))

            def prescale(l, _):
                act.wait_ge(sem("rows"), over("rows", ("u", l), 3))
                fn(h[:, :, :], h[:, :, :], ACT.Copy, scale=ALPHA).then_inc(*c.event("alpha_h", l))

            def latent_sums(l, _):
                fn(lat_sq[:, 0:3, :], q_lat, ACT.Square).then_inc(*c.step())
                fn(lat_sq[:, 3:5, :], kv_lat, ACT.Square).then_inc(*c.event("squares", ("lat", l)))

            def latent_norm(l, _):
                square_root(("lat_q", l), 0, QL, RMS_EPS, 0)
                square_root(("lat_kv", l), 1, KVL, RMS_EPS, 1)

            def scores(l, hd):
                b = hd % 2
                act.wait_ge(sem("nmax"), over("nmax", l, hd))
                for tt, (lo, hi) in enumerate(((0, P), (P, 3 * P))):
                    fn(soft[:, b, lo:hi], soft[:, b, lo:hi], ACT.Exp,
                       bias=nmax[:, b, tt:tt + 1], scale=SCALE2, accum_out=sums[:, b, tt:tt + 1]).then_inc(*c.event("probs", l, hd, tt))

            def turn(l, hd):
                act.wait_ge(sem("turned"), over("turned", l, hd))
                fn(soft_t[:, hd % 2, :], p_c[:, 0:384], ACT.Copy).then_inc(*c.event("probs_t", l, hd))

            def ln_a_var(l, _):
                act.wait_ge(sem("centred_a"), over("centred_a", l))
                fn(tmp[:, 0:4, :], acc, ACT.Square).then_inc(*c.event("squares", ("var_a", l)))
                square_root(("var_a", l), 1, W, LN_EPS)

            def ln_a_out(l, _):
                for j in range(WT):
                    act.wait_ge(sem("a_affine"), over("a_affine", l, j))
                    fn(tmp[:, j, :], acc[:, j, :], ACT.Sigmoid).then_inc(*c.event("a_sig", l, j))

            def ln_centre(l, _):
                for j in range(4):
                    act.wait_ge(sem("centred"), over("centred", l, j))
                    fn(tmp[:, 2 * j:2 * j + 2, :], h[:, 2 * j:2 * j + 2, :], ACT.Square).then_inc(*c.event("squares", ("var", l), j))

            def ln(l, _):
                square_root(("var", l), 1, D, LN_EPS)

            def ln_affine(l, _):
                for j in range(KT):
                    act.wait_ge(sem("ln_rows"), over("ln_rows", l, j // 2))
                    fn(h[:, j, :], h[:, j, :], ACT.Identity,
                       bias=col(("ln_b", l), j), scale=col(("ln_g", l), j)).then_inc(*c.event("affine", l, j))

            act.wait_ge(sem("par_landed"), 16)
            act.wait_ge(sem("const"), over("const", "all"))
            fn(silu_c[:, :], col("c", 0, KT), ACT.Sigmoid).then_inc(*c.event("c_sig"))
            steps = dict(norm_squares=norm_squares, norm=norm, ada_take=ada_take, ln_centre=ln_centre,
                         ln_affine=ln_affine, split=split, panel=panel, s5_sines=s5_sines, s5_turn=s5_turn, bu=bu, s5_out=s5_out,
                         stick_scores=stick_scores, stick_weights=stick_weights, stick_out=stick_out,
                         rope_tables=rope_tables, prescale=prescale, latent_sums=latent_sums,
                         latent_norm=latent_norm, scores=scores, turn=turn, ln_a_var=ln_a_var,
                         ln_a_out=ln_a_out, ln=ln)
            for kind, a, b in ORDER:
                if kind in steps:
                    steps[kind](a, b)

        @block.vector
        def _(dve):
            c = Count("dve")

            def tt(out_, a, b, op):
                dve.wait_ge(*c.last)
                return dve.tensor_tensor(out_, a, b, op)

            def ts(out_, a, s1, s2, op0, op1=ALU.bypass):
                dve.wait_ge(*c.last)
                return dve.tensor_scalar(out_, a, s1, s2, op0, op1)

            def stt(out_, a, s, b, op0, op1):
                dve.wait_ge(*c.last)
                return dve.scalar_tensor_tensor(out=out_, in0=a, scalar=s, in1=b, op0=op0, op1=op1)

            def copy(out_, a):
                dve.wait_ge(*c.last)
                return dve.tensor_copy(out_, a)

            def take(g, out_, a, b, op):
                dve.wait_ge(sem("groups"), g + 1)
                dve.wait_ge(*c.last)
                dve.tensor_tensor(out_, a, b, op).then_inc(*c.bank_free(g))

            def split(key, _):
                if key not in FUSED:
                    for j in range(len(OPERANDS[key]["pieces"])):
                        low(key, j)

            def low(key, j):
                o = OPERANDS[key]
                a, b = o["pieces"][j]
                dve.wait_ge(sem("hi"), over("hi", key, j))
                tt(o["lo"][:, a:b, :], o["src"][:, a:b, :], o["hi"][:, a:b, :].bitcast(F32),
                   ALU.subtract).then_inc(*c.event("lo", key, j))

            def invert(key, which=0):
                dve.wait_ge(sem("root"), over("root", key))
                dve.wait_ge(*c.last)
                dve.reciprocal(rstd[:, which, :], root[:, which, :]).then_inc(*c.event("rstd", key))

            def norm(k, _):
                invert(("norm", k))
                name = ("norm_mix", "norm_mlp", "norm_final")[k]
                key = ("u0", "u2", None)[k]
                before = c.last
                for j in range(KT):
                    dve.wait_ge(*before)
                    dst = tmp[:, j, :] if k < 2 else h[:, j, :]
                    ins = dve.scalar_tensor_tensor(out=dst, in0=h[:, j, :], scalar=col(name, j), in1=rstd[:, 0, :],
                                                   op0=ALU.mult, op1=ALU.mult)
                    ins.then_inc(*(c.event("h_rows", j) if k == 2 else c.event("rows", key, j // 2) if j % 2 else c.step()))
                    if k < 2 and j % 2 and j >= 3:
                        low(key, j // 2 - 1)
                if k < 2:
                    low(key, 3)

            S = lambda k: small[:, k, :]

            def s5_angle(_, __):
                dve.wait_ge(sem("par_landed"), 16)

                def exp_parts(x, f, two_n, p, n):
                    ts(f, x, -87.0, 88.0, ALU.max, ALU.min).then_inc(*c.step())
                    ts(n, f, 1.0 / math.log(2.0), ROUND, ALU.mult, ALU.add).then_inc(*c.step())
                    ts(n, n, -ROUND, None, ALU.add).then_inc(*c.step())
                    stt(f, n, -LN2_HI, f, ALU.mult, ALU.add).then_inc(*c.step())
                    stt(f, n, -LN2_LO, f, ALU.mult, ALU.add).then_inc(*c.step())
                    ts(n.bitcast(I32), n, 127.0, None, ALU.add).then_inc(*c.step())
                    ts(two_n.bitcast(I32), n.bitcast(I32), 23, None, ALU.logical_shift_left).then_inc(*c.step())
                    ts(p, f, 1.0 / math.factorial(8), None, ALU.mult).then_inc(*c.step())
                    for k in range(7, 0, -1):
                        stt(p, p, 1.0 / math.factorial(k), f, ALU.add, ALU.mult).then_inc(*c.step())

                f, two_n, p, n = S(0), S(1), S(2), S(3)
                exp_parts(col("log_dt", 0, 16), f, two_n, p, n)
                dt = S(4)
                stt(dt, p, 1.0, two_n, ALU.add, ALU.mult).then_inc(*c.step())
                tt(S(5), col("A_re", 0, 16), dt, ALU.mult).then_inc(*c.step())
                exp_parts(S(5), f, two_n, p, n)
                tt(S(6), p, two_n, ALU.mult).then_inc(*c.step())
                stt(S(6), two_n, -1.0, S(6), ALU.add, ALU.add).then_inc(*c.step())
                tt(S(7), col("A_im", 0, 16), dt, ALU.mult).then_inc(*c.step())
                turns(S(7), S(18), S(8))
                ts(S(19), S(18), 0.5, None, ALU.mult).then_inc(*c.event("angle"))

            def s5_prep(_, __):
                dve.wait_ge(sem("s5_landed"), 32)
                dve.wait_ge(sem("sines"), over("sines"))
                sin, half_sin = S(20), S(21)
                cm1 = S(9)
                stt(cm1, half_sin, -2.0, half_sin, ALU.mult, ALU.mult).then_inc(*c.step())
                nre, nim = S(10), S(11)
                stt(nre, cm1, 1.0, S(6), ALU.add, ALU.mult).then_inc(*c.step())
                tt(nre, nre, cm1, ALU.add).then_inc(*c.step())
                stt(nim, S(6), 1.0, sin, ALU.add, ALU.mult).then_inc(*c.step())
                ts(power[:, 0, 0, :], nre, 1.0, None, ALU.add).then_inc(*c.step())
                copy(power[:, 0, 1, :], nim).then_inc(*c.step())
                ts(power[:, 0, 2, :], nim, -1.0, None, ALU.mult).then_inc(*c.step())
                for k in range(1, 8):
                    re, im, nm = (power[:, k - 1, i, :] for i in range(3))
                    tt(S(12), im, nm, ALU.mult).then_inc(*c.step())
                    tt(S(13), re, re, ALU.mult).then_inc(*c.step())
                    tt(power[:, k, 0, :], S(13), S(12), ALU.add).then_inc(*c.step())
                    stt(power[:, k, 1, :], re, 2.0, im, ALU.mult, ALU.mult).then_inc(*c.step())
                    ts(power[:, k, 2, :], power[:, k, 1, :], -1.0, None, ALU.mult).then_inc(*c.step())
                are, aim = col("A_re", 0, 16), col("A_im", 0, 16)
                tt(S(12), are, are, ALU.mult).then_inc(*c.step())
                tt(S(13), aim, aim, ALU.mult).then_inc(*c.step())
                tt(S(12), S(12), S(13), ALU.add).then_inc(*c.step())
                dve.wait_ge(*c.last)
                dve.reciprocal(S(14), S(12)).then_inc(*c.step())
                tt(S(12), nre, are, ALU.mult).then_inc(*c.step())
                tt(S(13), nim, aim, ALU.mult).then_inc(*c.step())
                tt(S(12), S(12), S(13), ALU.add).then_inc(*c.step())
                tt(S(15), S(12), S(14), ALU.mult).then_inc(*c.step())
                tt(S(12), nim, are, ALU.mult).then_inc(*c.step())
                tt(S(13), nre, aim, ALU.mult).then_inc(*c.step())
                tt(S(12), S(12), S(13), ALU.subtract).then_inc(*c.step())
                tt(S(16), S(12), S(14), ALU.mult).then_inc(*c.step())
                dve.wait_ge(*c.last)
                dve.memset(bd, 0.0).then_inc(*c.step())
                wide = [P, 16, 16]
                fre = S(15).unsqueeze(2).broadcast_to(wide)
                fim = S(16).unsqueeze(2).broadcast_to(wide)
                bre, bim = (bst[:, i, :].rearrange("p (r c) -> p r c", r=16) for i in range(2))
                bt3 = btmp.rearrange("p (r c) -> p r c", r=16)
                bt4 = nmean[:, :].rearrange("p (r c) -> p r c", r=16)
                for comp, (x, y, op) in enumerate(((bre, bim, ALU.subtract), (bim, bre, ALU.add))):
                    tt(bt3, fre, x, ALU.mult).then_inc(*c.step())
                    tt(bt4, fim, y, ALU.mult).then_inc(*c.step())
                    for g2 in range(2):
                        rows = slice(64 * g2, 64 * g2 + 64)
                        dst = bd[rows, comp, :].rearrange("p (r g c) -> p r g c", r=16, g=2)[:, :, g2, :]
                        tt(dst, bt3[rows], bt4[rows], op).then_inc(*c.event("b_diag", comp, g2))
                ts(ct[:, 1, :, :], ct[:, 1, :, :], -1.0, None, ALU.mult).then_inc(*c.event("ct"))
                dve.wait_ge(*c.last)
                dve.memset(xs[:, :, :, 0:PAD], 0.0).then_inc(*c.step())
                dve.wait_ge(sem("bt_ps"), over("bt_ps"))
                for x in states[2:]:
                    dve.wait_ge(*c.last)
                    dve.memset(x[:, :, 0:PAD], 0.0).then_inc(*(c.event("pads") if x is states[3] else c.step()))

            def turns(angle, dst, k):
                ts(k, angle, 1.0 / (2 * math.pi), ROUND, ALU.mult, ALU.add).then_inc(*c.step())
                ts(k, k, -ROUND, None, ALU.add).then_inc(*c.step())
                stt(dst, k, -TWO_PI[0], angle, ALU.mult, ALU.add).then_inc(*c.step())
                stt(dst, k, -TWO_PI[1], dst, ALU.mult, ALU.add).then_inc(*c.step())
                stt(dst, k, -TWO_PI[2], dst, ALU.mult, ALU.add).then_inc(*c.step())
                ts(dst, dst, -PI_IN, PI_IN, ALU.max, ALU.min).then_inc(*c.step())

            def scan(first, _):
                two = (first, first + 1)
                for r in two:
                    dve.wait_ge(sem("bu_sb"), over("bu_sb", r))
                done = {r: c.last for r in two}
                for k in range(8):
                    d = 1 << k
                    lo = 0 if d <= PAD else d
                    here, past = slice(PAD + lo, PAD + T), slice(PAD + lo - d, PAD + T - d)
                    src = {r: (states[r % 4], other[r % 2])[k % 2] for r in two}
                    dst = {r: (states[r % 4], other[r % 2])[1 - k % 2] for r in two}
                    re, im, nm = ({r: power[:, k, i, r:r + 1] for r in two} for i in range(3))
                    if lo:
                        for r in two:
                            dve.wait_ge(*done[r])
                            dve.tensor_copy(dst[r][:, :, PAD:PAD + d], src[r][:, :, PAD:PAD + d]).then_inc(*c.step())
                    for r in two:
                        dve.wait_ge(*done[r])
                        dve.scalar_tensor_tensor(out=dst[r][:, :, here], in0=src[r][:, :, past], scalar=re[r],
                                                 in1=src[r][:, :, here], op0=ALU.mult, op1=ALU.add).then_inc(*c.step())
                        done[r] = c.last
                    for r in two:
                        dve.wait_ge(*done[r])
                        dve.scalar_tensor_tensor(out=dst[r][:, 0, here], in0=src[r][:, 1, past], scalar=nm[r],
                                                 in1=dst[r][:, 0, here], op0=ALU.mult, op1=ALU.add).then_inc(*c.step())
                        dve.scalar_tensor_tensor(out=dst[r][:, 1, here], in0=src[r][:, 0, past], scalar=im[r],
                                                 in1=dst[r][:, 1, here], op0=ALU.mult,
                                                 op1=ALU.add).then_inc(*(c.event("scan", r) if k == 7 else c.step()))
                        done[r] = c.last

            def s5_out(r, _):
                if r % 4 == 3:
                    f = r // 4
                    dve.wait_ge(sem("cx"), over("cx", r))
                    stt(yv[:, f, :], ussm[:, f, :], col("D_skip", f),
                        p_y[:, T * (f % 2):T * (f % 2) + T], ALU.mult, ALU.add).then_inc(*c.event("y_rows", f))
                    dve.wait_ge(sem("y_sq"), over("y_sq", f))
                    ts(y1, y1, 0.044715, 1.0, ALU.mult, ALU.add).then_inc(*c.step())
                    tt(y1, y1, yv[:, f, :], ALU.mult).then_inc(*c.event("y_inner", f))
                    dve.wait_ge(sem("y_sig"), over("y_sig", f))
                    tt(yv[:, f, :], yv[:, f, :], y1, ALU.mult).then_inc(*(c.event("rows", "y", 0) if f == WT - 1 else c.step()))

            def stick_soft(hd, _):
                dve.wait_ge(sem("log1p"), over("log1p", hd))
                stt(stick[1], p_z[:, 0:384], 0.0, stick[0], ALU.max, ALU.add).then_inc(*c.step())
                tt(stick[1], stick[1], mask1[:, :], ALU.mult).then_inc(*c.event("soft", hd))

            def stick_weights(hd, _):
                dve.wait_ge(sem("fails"), over("fails", hd))
                if hd >= 2:
                    dve.wait_ge(sem("o_stick"), over("o_stick", hd - 2))
                stt(stick[2 + hd % 2], p_c[:, 0:384], 0.0, neg1[:, :], ALU.min, ALU.add).then_inc(*c.event("logw", hd))

            def ada_end(part, _):
                first, end = ADA_PARTS[part]
                dve.wait_ge(sem("ada_turned"), over("ada_turned", end - 1))
                for l in range(LAYERS):
                    a, b = max(2 * first, 24 * l), min(2 * end, 24 * l + 24)
                    if a < b:
                        ps = p_s if part == 0 else p_c
                        tt(ada[:, l, a - 24 * l:b - 24 * l], ps[:, a:b], col(("b_ada", l), a - 24 * l, b - a),
                           ALU.add).then_inc(*(c.event("ada", part) if b == 2 * end else c.step()))

            def glu_mul(_, __):
                for s, v in emptied(groups_of("glu")):
                    dve.wait_ge(s, v)
                tt(yv, yv, yt, ALU.mult).then_inc(*c.event("rows", "yg", 0))

            def panel(p, _):
                q = PANELS[p]
                job, l, n, g = q["job"], q["layer"], q["n"], q["g"]
                both = pair(pg[g % 2][:, :])
                gt = pair(gtmp[:, q["gt"] % 2, :]) if q["gt"] is not None else None
                if job in ("up_attn", "up_ssm"):
                    for i in range(2):
                        a = 4 * n + 2 * i
                        b = pair(pg[(g + i) % 2][:, :])
                        if job == "up_attn":
                            take(g + i, merged[:, a:a + 2, :], b, gates[:, KT + a:KT + a + 2, :], ALU.mult)
                        else:
                            take(g + i, tmp[:, 0:2, :], b, gates[:, a:a + 2, :], ALU.mult)
                            tt(merged[:, a:a + 2, :], merged[:, a:a + 2, :], tmp[:, 0:2, :],
                               ALU.add).then_inc(*c.event("rows", "u1", a // 2))
                elif job == "out":
                    take(g, h[:, 2 * n:2 * n + 2, :], both, h[:, 2 * n:2 * n + 2, :], ALU.add)
                elif job == "ff2":
                    for i in range(2):
                        a = 4 * (n % 2) + 2 * i
                        take(g + i, h[:, a:a + 2, :], pair(pg[(g + i) % 2][:, :]), h[:, a:a + 2, :], ALU.add)
                elif job == "ff1":
                    f, ch = 4 * (n % 2), n // 2
                    dve.wait_ge(sem("groups"), g + 1)
                    dve.wait_ge(*c.last)
                    dve.tensor_scalar(tmp[:, f:f + 2, :], both, 0.0, None, ALU.max).then_inc(*c.bank_free(g))
                    dve.wait_ge(sem("ff_hi"), over("ff_hi", n))
                    half = slice(2 * (n % 2), 2 * (n % 2) + 2)
                    tt(v_lo[(ch + 1) % 2][:, half, :], tmp[:, f + 2:f + 4, :],
                       v_hi[(ch + 1) % 2][:, half, :].bitcast(F32), ALU.subtract).then_inc(*c.event("ff_lo", n))
                elif job == "a1":
                    for s, v in emptied(groups_of("a2", l)):
                        dve.wait_ge(s, v)
                    take(g, apad[:, 2 * n:2 * n + 2, CONV_A - 1:], both, acc[:, 2 * n:2 * n + 2, :], ALU.mult)
                elif job == "gc":
                    for s, v in emptied(groups_of("xb", l)):
                        dve.wait_ge(s, v)
                    take(g, bpad[:, 2 * n:2 * n + 2, CONV_B - 1:], both, xbv[:, 2 * n:2 * n + 2, :], ALU.mult)
                elif job == "gb":
                    take(g, bconv[:, 2 * n:2 * n + 2, :], both, bconv[:, 2 * n:2 * n + 2, :], ALU.mult)
                elif job in ("cg", "ag", "bg"):
                    dve.wait_ge(sem("sigmoid"), over("sigmoid", q["gt"]))
                    dst = {"cg": cgate, "ag": agate}[job][:, 2 * n:2 * n + 2, :] if job != "bg" else gt
                    take(g, dst, both, gt, ALU.mult)
                    if job == "bg":
                        tt(bconv[:, 2 * n:2 * n + 2, :], bconv[:, 2 * n:2 * n + 2, :], gt, ALU.mult).then_inc(*c.event("gt_used", q["gt"]))
                elif job in ("merge0", "merge1", "merge2"):
                    for s, v in emptied([g, find("branch%s" % job[-1], l, n // 2)["g"] + n % 2]):
                        dve.wait_ge(s, v)
                    a = slice(2 * n, 2 * n + 2)
                    if job == "merge1":
                        tt(mer[:, a, :], gt, ybr[:, a, :], ALU.mult).then_inc(*c.event("gt_used", q["gt"]))
                    else:
                        tt(gt, gt, ybr[:, a, :], ALU.mult).then_inc(*c.step())
                        tt(mer[:, a, :], mer[:, a, :], gt, ALU.add).then_inc(*c.event("gt_used", q["gt"]))
                elif job == "w_o":
                    dve.wait_ge(sem("groups"), g + 1)
                    dve.wait_ge(sem("alpha_h"), over("alpha_h", l))
                    stt(h[:, 2 * n, :], both[:, 0, :], ada[:, l, 16 + 2 * n:17 + 2 * n], h[:, 2 * n, :],
                        ALU.mult, ALU.add).then_inc(*c.step())
                    dve.wait_ge(*c.last)
                    dve.scalar_tensor_tensor(
                        out=h[:, 2 * n + 1, :], in0=both[:, 1, :], scalar=ada[:, l, 17 + 2 * n:18 + 2 * n],
                        in1=h[:, 2 * n + 1, :], op0=ALU.mult, op1=ALU.add).then_inc(*c.bank_free(g))

            def rope_tables(_, __):
                for pad in (apad[:, :, 0:CONV_A - 1], bpad[:, :, 0:CONV_B - 1]):
                    dve.wait_ge(*c.last)
                    dve.memset(pad, 0.0).then_inc(*c.step())
                rows = slice(NOPE, QK)
                dve.wait_ge(sem("pos_landed"), 16)
                copy(nmean[rows, :], pos[rows, :]).then_inc(*c.step())
                ts(nmean[rows, :], nmean[rows, :], col("inv_freq")[rows], None, ALU.mult).then_inc(*c.step())
                turns(nmean[rows, :], rsin[rows, :], rcos[rows, :])
                ts(rcos[rows, :], rsin[rows, :], 0.5, None, ALU.mult).then_inc(*c.event("rope_angle"))
                dve.wait_ge(sem("rope_sines"), over("rope_sines"))
                stt(rcos[rows, :], rcos[rows, :], -2.0, rcos[rows, :], ALU.mult, ALU.mult).then_inc(*c.step())
                ts(rcos[rows, :], rcos[rows, :], 1.0, None, ALU.add).then_inc(*c.step())

            def modulate(l, _):
                ts(scale1[:, :], ada[:, l, 8:16], 1.0, None, ALU.add).then_inc(*c.event("scale1", l))
                before = c.last
                for j in range(KT):
                    if l:
                        dve.wait_ge(sem("affine"), over("affine", l - 1, j))
                    dve.wait_ge(*before)
                    dve.tensor_scalar(tmp[:, j, :], h[:, j, :], scale1[:, j:j + 1], ada[:, l, j:j + 1], ALU.mult,
                                      ALU.add).then_inc(*(c.event("rows", ("u", l), j // 2) if j % 2 else c.step()))
                    if j % 2 and j >= 3:
                        low(("u", l), j // 2 - 1)
                low(("u", l), 3)

            def latent_norm(l, _):
                for key, which, x, n, name in ((("lat_q", l), 0, q_lat, 3, "q_norm_g"),
                                               (("lat_kv", l), 1, kv_lat, 2, "kv_norm_g")):
                    invert(key, which)
                    for j in range(n):
                        stt(x[:, j, :],
                            x[:, j, :], col((name, l), j), rstd[:, which, :], ALU.mult, ALU.mult).then_inc(*(c.event("rows", ("ql" if which == 0 else "kvl", l), 0) if j == n - 1 else c.step()))

            def rope(l, _):
                rows = slice(NOPE, QK)
                wide = [ROPE, 2, T]
                sin2, cos2 = spread(rsin[rows, :], *wide), spread(rcos[rows, :], *wide)
                dve.wait_ge(sem("rotated"), over("rotated", l, 0))
                tt(kpr[rows, :], p_y[rows, 0:T], rsin[rows, :], ALU.mult).then_inc(*c.step())
                tt(kpe[rows, :], kpe[rows, :], rcos[rows, :], ALU.mult).then_inc(*c.step())
                tt(kpe[rows, :], kpe[rows, :], kpr[rows, :], ALU.add).then_inc(*c.step())
                copy(kf[rows, :, :], spread(kpe[rows, :], ROPE, HEADS, T)).then_inc(*c.step())
                for i in range(4):
                    b = (p_bu, p_z)[i % 2]
                    a = slice(2 * i, 2 * i + 2)
                    dve.wait_ge(sem("rotated"), over("rotated", l, 1 + i))
                    tt(rtmp[rows, :, :], pair(b[rows, :]), sin2, ALU.mult).then_inc(*c.event("rot_read", l, i))
                    tt(qf[rows, a, :], qf[rows, a, :], cos2, ALU.mult).then_inc(*c.step())
                    tt(qf[rows, a, :], qf[rows, a, :], rtmp[rows, :, :], ALU.add).then_inc(*(c.event("roped", l) if i == 3 else c.step()))

            def conv_a(l, part):
                tiles = (2 * (part // CONV_PARTS), 2 * (part // CONV_PARTS) + 1)
                first = CONV_STEP * (part % CONV_PARTS)
                done = {j: c.last for j in tiles}
                for k in range(first, min(first + CONV_STEP, CONV_A)):
                    for j in tiles:
                        w = col(("conv_a_w", l), 4 * k + j)
                        dve.wait_ge(*done[j])
                        if k == 0:
                            ins = dve.tensor_scalar(acc[:, j, :], apad[:, j, 0:T], w, col(("conv_a_b", l), j), ALU.mult, ALU.add)
                        else:
                            ins = dve.scalar_tensor_tensor(out=acc[:, j, :], in0=apad[:, j, k:k + T], scalar=w,
                                                           in1=acc[:, j, :], op0=ALU.mult, op1=ALU.add)
                        ins.then_inc(*(c.event("conv_a", l, j) if k == CONV_A - 1 else c.step()))
                        done[j] = c.last

            def conv_b(l, _):
                for j in range(WT):
                    w = lambda k: col(("conv_b_w", l), 4 * k + j)
                    ts(bconv[:, j, :], bpad[:, j, 0:T], w(0), None, ALU.mult).then_inc(*c.step())
                    for k in range(1, CONV_B):
                        stt(bconv[:, j, :], bpad[:, j, k:k + T], w(k), bconv[:, j, :], ALU.mult, ALU.add).then_inc(*c.step())

            def scores(l, hd):
                b = hd % 2
                dve.wait_ge(sem("scores"), over("scores", l, hd))
                if hd >= 2 or l:
                    dve.wait_ge(sem("turned"), over("turned", l if hd >= 2 else l - 1, (hd - 2) % HEADS))
                tt(soft[:, b, :], p_z[:, 0:384], mask2[:, :], ALU.add).then_inc(*c.step())
                for i, (lo, hi) in enumerate(((0, P), (P, 3 * P))):
                    dve.wait_ge(*c.last)
                    dve.tensor_reduce(mx[:, b, i:i + 1], soft[:, b, lo:hi], AX.X, ALU.max).then_inc(*c.step())
                ts(nmax[:, b, :], mx[:, b, :], -SCALE2, None, ALU.mult).then_inc(*c.event("nmax", l, hd))

            def turn(l, hd):
                b = hd % 2
                dve.wait_ge(sem("probs"), over("probs", l, hd, 1))
                dve.wait_ge(*c.last)
                dve.reciprocal(rsum[:, b, :], sums[:, b, :]).then_inc(*c.step())
                ts(soft[:, b, 0:P], soft[:, b, 0:P], rsum[:, b, 0:1], None, ALU.mult).then_inc(*c.step())
                ts(soft[:, b, P:3 * P], soft[:, b, P:3 * P], rsum[:, b, 1:2], None, ALU.mult).then_inc(*c.event("probs_n", l, hd))

            def context(l, hd):
                if hd % 2:
                    i = hd // 2
                    dve.wait_ge(sem("o2"), over("o2", l, hd))
                    tt(cgate[:, i, :],
                       p_o[:, T * (i % 2):T * (i % 2) + T], cgate[:, i, :], ALU.mult).then_inc(*(c.event("rows", ("c", l), 0) if i == 3 else c.event("ctx_read", l, i)))

            def mean(key, n):
                dve.wait_ge(sem("stats"), over("stats", key))
                ts(nmean[:, :], p_s[:, 0:T], -1.0 / n, None, ALU.mult).then_inc(*c.event("nmean", key))

            def ln_a_mean(l, _):
                mean(("mean_a", l), W)
                tt(acc, acc, spread(nmean[:, :], P, WT, T), ALU.add).then_inc(*c.event("centred_a", l))

            def ln_a_var(l, _):
                invert(("var_a", l))
                tt(acc, acc, spread(rstd[:, 0, :], P, WT, T), ALU.mult).then_inc(*c.step())
                for j in range(WT):
                    ts(acc[:, j, :], acc[:, j, :], col(("ln_a_g", l), j), col(("ln_a_b", l), j),
                       ALU.mult, ALU.add).then_inc(*c.event("a_affine", l, j))

            def ln_a_out(l, _):
                dve.wait_ge(sem("a_sig"), over("a_sig", l, WT - 1))
                tt(acc, acc, tmp[:, 0:4, :], ALU.mult).then_inc(*c.step())
                tt(acc, acc, agate, ALU.mult).then_inc(*c.event("rows", ("a", l), 0))

            def ln_centre(l, _):
                mean(("mean", l), D)
                before = c.last
                for j in range(4):
                    dve.wait_ge(*before)
                    dve.tensor_tensor(h[:, 2 * j:2 * j + 2, :], h[:, 2 * j:2 * j + 2, :], spread(nmean[:, :], P, 2, T),
                                      ALU.add).then_inc(*c.event("centred", l, j))

            def ln(l, _):
                invert(("var", l))
                before = c.last
                for j in range(4):
                    dve.wait_ge(*before)
                    dve.tensor_tensor(h[:, 2 * j:2 * j + 2, :], h[:, 2 * j:2 * j + 2, :], spread(rstd[:, 0, :], P, 2, T),
                                      ALU.mult).then_inc(*c.event("ln_rows", l, j))

            dve.wait_ge(sem("const"), over("const", "all"))
            dve.wait_ge(sem("c_sig"), over("c_sig"))
            tt(silu_c[:, :], silu_c[:, :], col("c", 0, KT), ALU.mult).then_inc(*c.event("silu_c"))
            steps = dict(norm=norm, split=split, panel=panel, s5_angle=s5_angle, s5_prep=s5_prep, scan=scan, s5_out=s5_out,
                         stick_soft=stick_soft, stick_weights=stick_weights,
                         ada_end=ada_end, glu_mul=glu_mul, rope_tables=rope_tables, modulate=modulate,
                         latent_norm=latent_norm, rope=rope, conv_a=conv_a, conv_b=conv_b, scores=scores,
                         turn=turn, context=context, ln_a_mean=ln_a_mean, ln_a_var=ln_a_var,
                         ln_a_out=ln_a_out, ln_centre=ln_centre, ln=ln)
            for kind, a, b in ORDER:
                if kind in steps:
                    steps[kind](a, b)

        @block.tensor
        def _(pe):
            def sum_tiles(key, src, tiles, region):
                if SUMS.index(key):
                    pe.wait_ge(*sums_before(key))
                for j in range(tiles):
                    ins = pe.matmul(p_s[:, region * T:region * T + T], ones[:, :], src[:, j, :], start=j == 0,
                                    stop=j == tiles - 1)
                return ins

            def three(dst, w_h, w_l, x_h, x_l, first, last_):
                pe.matmul(dst, w_h, x_h, start=first, stop=False)
                pe.matmul(dst, w_h, x_l, start=False, stop=False)
                return pe.matmul(dst, w_l, x_h, start=False, stop=last_)

            def group_start(g):
                if g >= 2:
                    for s, v in emptied([g - 2]):
                        pe.wait_ge(s, v)

            begun = set()

            def blocks(q, g, widths, x_hi, x_lo, waits):
                wh, wl = slot(w_hi, q), slot(w_lo, q)
                group_start(g)
                for i, (a, m) in enumerate(widths):
                    for k in range(q["kt"]):
                        if i == 0 and k in waits:
                            pe.wait_ge(*waits[k])
                        ins = three(pg[g % 2][0:m, i * T:i * T + T], wh[:, k, a:a + m], wl[:, k, a:a + m],
                                    x_hi[:, k, :], x_lo[:, k, :], k == 0, k == q["kt"] - 1)
                ins.then_inc(sem("groups"), 1)

            def panel(p, _):
                q = PANELS[p]
                job, l, n, g = q["job"], q["layer"], q["n"], q["g"]
                if job == "ada":
                    pe.wait_ge(*landed(q))
                    pe.wait_ge(sem("silu_c"), over("silu_c"))
                    group_start(g)
                    w = slot(raw, q)
                    for k in range(KT):
                        ins = pe.matmul(pg[g % 2][0:1, 0:256], silu_c[:, k:k + 1], w[:, k, :], start=k == 0, stop=k == KT - 1)
                    ins.then_inc(sem("groups"), 1)
                    return
                pe.wait_ge(*slot_free(q))
                waits = {}
                if job == "ff2":
                    ch = n // 2
                    pe.wait_ge(sem("ff_lo"), over("ff_lo", 2 * ch + 1))
                    xh, xl = v_hi[(ch + 1) % 2], v_lo[(ch + 1) % 2]
                else:
                    key = operand_of(q)
                    o = OPERANDS[key]
                    waits = {a: (sem("lo"), over("lo", key, j)) for j, (a, b) in enumerate(o["pieces"])} if key not in begun else {}
                    begun.add(key)
                    xh, xl = o["hi"], o["lo"]
                if job == "v":
                    wh, wl = slot(w_hi, q), slot(w_lo, q)
                    group_start(g)
                    for tt in range(2):
                        for k in range(KT):
                            tok = slice(P * tt, P * tt + P)
                            dst = pg[g % 2][:, T * tt:T * tt + T]
                            pe.matmul(dst, xh[:, k, tok], wh[:, k, :], start=k == 0, stop=False)
                            pe.matmul(dst, xh[:, k, tok], wl[:, k, :], start=False, stop=False)
                            ins = pe.matmul(dst, xl[:, k, tok], wh[:, k, :], start=False, stop=k == KT - 1)
                    ins.then_inc(sem("groups"), 1)
                elif job == "uq":
                    for i in range(2):
                        blocks(q, g + i, [(QK * (2 * i + j), QK) for j in range(2)], xh, xl, waits if i == 0 else {})
                elif job == "ukv":
                    for i in range(4):
                        blocks(q, g + i, [(P * (2 * i + j), P) for j in range(2)], xh, xl, waits if i == 0 else {})
                    wh, wl = (slot(x, q).rearrange("p k (h m) -> p k h m", h=HEADS)[:, :, :, NOPE:P] for x in (w_hi, w_lo))
                    for tt in range(2):
                        group_start(g + 4 + tt)
                        dst = pg[(g + tt) % 2][:, :].rearrange("p (h m) -> p h m", h=HEADS)
                        tok = slice(P * tt, P * tt + P)
                        for k in range(q["kt"]):
                            pe.matmul(dst, xh[:, k, tok], wh[:, k], start=k == 0, stop=False)
                            pe.matmul(dst, xh[:, k, tok], wl[:, k], start=False, stop=False)
                            ins = pe.matmul(dst, xl[:, k, tok], wh[:, k], start=False, stop=k == q["kt"] - 1)
                        ins.then_inc(sem("groups"), 1)
                else:
                    for i in range(q["groups"]):
                        left = min(256, q["cols"] - 256 * i)
                        blocks(q, g + i, [(256 * i + P * j, min(P, left - P * j)) for j in range((left + P - 1) // P)],
                               xh, xl, waits if i == 0 else {})

            def sum_piece(key, src, j, region):
                if j == 0 and SUMS.index(key):
                    pe.wait_ge(*sums_before(key))
                for i in (2 * j, 2 * j + 1):
                    ins = pe.matmul(p_s[:, region * T:region * T + T], ones[:, :], src[:, i, :], start=i == 0, stop=i == KT - 1)
                if j == 3:
                    ins.then_inc(*event("stats", key))

            def norm_sums(k, j):
                pe.wait_ge(sem("squares"), over("squares", ("norm", k), j))
                sum_piece(("norm", k), tmp, j, 0)

            def ada_turn(i, _):
                q = find("ada", i // 12, i % 12)
                part = next(k for k, (a, b) in enumerate(ADA_PARTS) if i < b)
                ps = p_s if part == 0 else p_c
                if i == 0:
                    pe.wait_ge(*sums_before(("ada", 0)))
                elif i == ADA_PARTS[1][0]:
                    pe.wait_ge(sem("logw"), over("logw", HEADS - 1))
                elif part > 1 and i == ADA_PARTS[part][0]:
                    pe.wait_ge(sem("ada"), over("ada", part - 1))
                    if part == 3:
                        pe.wait_ge(sem("probs_t"), over("probs_t", 0, HEADS - 1))
                for s, v in emptied([q["g"]]):
                    pe.wait_ge(s, v)
                for j in range(2):
                    at = 2 * i + j
                    ins = pe.matmul(ps[:, at:at + 1], root[0:1, 1, P * j:P * j + P], ones[0:1, 0:1], start=True, stop=True)
                    ins.then_inc(*((sem(f"raw_free{q['index'] % RAW}"), 1) if j == 0 else event("ada_turned", i)))

            def s5_turn(_, __):
                pe.wait_ge(sem("b_diag"), over("b_diag", 1, 1))
                for comp, b in enumerate((p_bu, p_z)):
                    for f in range(4):
                        ins = pe.transpose(b[:, P * f:P * f + P], bd[:, comp, P * f:P * f + P], ident[:, :])
                ins.then_inc(*event("bt_ps"))

            def bu(r, _):
                pe.wait_ge(sem("bt"), over("bt", 1))
                for s, v in emptied(groups_of("ssm")):
                    pe.wait_ge(s, v)
                if r:
                    pe.wait_ge(sem("bu_sb"), over("bu_sb", r - 1))
                f, rows = r // 4, slice(32 * (r % 4), 32 * (r % 4) + 32)
                for comp in range(2):
                    ins = pe.matmul(p_bu[:, T * comp:T * comp + T], bt[rows, comp, f, :], ussm[rows, f, :],
                                    start=True, stop=True)
                ins.then_inc(*event("bu", r))

            def s5_out(r, _):
                pe.wait_ge(sem("scan"), over("scan", r))
                pe.wait_ge(sem("ct"), over("ct"))
                f, rows = r // 4, slice(32 * (r % 4), 32 * (r % 4) + 32)
                if f:
                    pe.wait_ge(sem("y_rows"), over("y_rows", f - 1))
                x = states[r % 4]
                for comp in range(2):
                    ins = pe.matmul(p_y[rows, T * (f % 2):T * (f % 2) + T], ct[:, comp, f, rows], x[:, comp, PAD:PAD + T],
                                    start=comp == 0, stop=comp == 1)
                ins.then_inc(*event("cx", r))

            def qk(dst, hd, stop):
                rows, f = slice(64 * (hd % 2), 64 * (hd % 2) + 64), hd // 2
                pe.matmul(dst[:, 0:T], k1[rows, f, 0:P], q1[rows, f, :], start=True, stop=stop)

            def qk_rest(dst, hd, stop):
                rows, f = slice(64 * (hd % 2), 64 * (hd % 2) + 64), hd // 2
                return pe.matmul(dst[:, T:T + P], k1[rows, f, P:T], q1[rows, f, P:T], start=True, stop=stop)

            def stick_scores(hd, _):
                for s, v in emptied(groups_of("q") + groups_of("k")):
                    pe.wait_ge(s, v)
                pe.wait_ge(sem("bt"), over("bt", 1))
                if hd:
                    pe.wait_ge(sem("soft"), over("soft", hd - 1))
                qk(p_z, hd, True)
                qk_rest(p_z, hd, True).then_inc(*event("z", hd))

            def stick_fails(hd, _):
                pe.wait_ge(sem("soft"), over("soft", hd))
                if hd:
                    pe.wait_ge(sem("logw"), over("logw", hd - 1))
                qk(p_c, hd, False)
                pe.matmul(p_c[:, 0:T], ntri[:, :], stick[1][:, 0:T], start=False, stop=False)
                pe.matmul(p_c[:, P:T], nones[:, :], stick[1][:, T:T + P], start=False, stop=True)
                qk_rest(p_c, hd, False)
                pe.matmul(p_c[:, T:T + P], ntri[:, :], stick[1][:, T:T + P], start=False, stop=True).then_inc(*event("fails", hd))

            def weighted_values(values, weights, hd):
                rows, at = slice(64 * (hd % 2), 64 * (hd % 2) + 64), T * (hd // 2 % 2)
                pe.matmul(p_o[rows, at:at + T], values[:, 0, DH * hd:DH * hd + DH], weights[:, 0:T], start=True, stop=False)
                return pe.matmul(p_o[rows, at + P:at + T], values[:, 1, DH * hd:DH * hd + DH], weights[:, T:T + P],
                                 start=False, stop=True)

            def stick_out(hd, _):
                pe.wait_ge(sem("w_stick"), over("w_stick", hd))
                for s, v in emptied(groups_of("v")):
                    pe.wait_ge(s, v)
                if hd >= 2:
                    pe.wait_ge(sem("ctx"), over("ctx", hd // 2 - 1))
                weighted_values(v1, stick[2 + hd % 2], hd).then_inc(*event("o_stick", hd))

            def latent_sums(l, _):
                pe.wait_ge(sem("squares"), over("squares", ("lat", l)))
                sum_tiles(("lat", l), lat_sq[:, 0:3, :], 3, 0)
                sum_tiles(("lat", l), lat_sq[:, 3:5, :], 2, 1).then_inc(*event("stats", ("lat", l)))

            def rope(l, _):
                rows = slice(NOPE, QK)
                for s, v in emptied(groups_of("k_rope", l)):
                    pe.wait_ge(s, v)
                pe.matmul(p_y[rows, 0:T], rot[rows, :], kpe[rows, :], start=True, stop=True).then_inc(*event("rotated", l, 0))
                for s, v in emptied(groups_of("uq", l)):
                    pe.wait_ge(s, v)
                for i in range(4):
                    b = (p_bu, p_z)[i % 2]
                    if i >= 2:
                        pe.wait_ge(sem("rot_read"), over("rot_read", l, i - 2))
                    pe.matmul(b[rows, :], rot[rows, :], qf[rows, 2 * i:2 * i + 2, :], start=True, stop=True).then_inc(*event("rotated", l, 1 + i))

            def scores(l, hd):
                pe.wait_ge(sem("roped"), over("roped", l))
                for s, v in emptied(groups_of("ukv", l)):
                    pe.wait_ge(s, v)
                if hd:
                    pe.wait_ge(sem("nmax"), over("nmax", l, hd - 1))
                pe.matmul(p_z[:, 0:P], qf[0:QK, hd, 0:P], kf[0:QK, hd, 0:P], start=True, stop=True)
                pe.matmul(p_z[:, P:3 * P], qf[0:QK, hd, P:T], kf[0:QK, hd, :], start=True, stop=True).then_inc(*event("scores", l, hd))

            def turn(l, hd):
                pe.wait_ge(sem("probs_n"), over("probs_n", l, hd))
                if hd:
                    pe.wait_ge(sem("probs_t"), over("probs_t", l, hd - 1))
                else:
                    pe.wait_ge(sem("ada"), over("ada", 2 + l))
                for i in range(3):
                    ins = pe.transpose(p_c[:, P * i:P * i + P], soft[:, hd % 2, P * i:P * i + P], ident[:, :])
                ins.then_inc(*event("turned", l, hd))

            def context(l, hd):
                pe.wait_ge(sem("probs_t"), over("probs_t", l, hd))
                i = hd // 2
                if i:
                    pe.wait_ge(sem("ctx_read"), over("ctx_read", l, i - 1))
                weighted_values(v2, soft_t[:, hd % 2, :], hd).then_inc(*event("o2", l, hd))

            def ln_a_mean(l, _):
                pe.wait_ge(sem("conv_a"), over("conv_a", l, WT - 1))
                sum_tiles(("mean_a", l), acc, WT, 0).then_inc(*event("stats", ("mean_a", l)))

            def ln_a_var(l, _):
                pe.wait_ge(sem("squares"), over("squares", ("var_a", l)))
                sum_tiles(("var_a", l), tmp[:, 0:4, :], WT, 1).then_inc(*event("stats", ("var_a", l)))

            def ln_mean(l, j):
                for s, v in emptied([groups_of("w_o", l)[j]]):
                    pe.wait_ge(s, v)
                sum_piece(("mean", l), h, j, 0)

            def ln(l, _):
                for j in range(4):
                    pe.wait_ge(sem("squares"), over("squares", ("var", l), j))
                    sum_piece(("var", l), tmp, j, 1)

            pe.wait_ge(sem("const"), over("const", "all"))
            steps = dict(norm_sums=norm_sums, panel=panel, ada_turn=ada_turn, s5_turn=s5_turn, bu=bu, s5_out=s5_out,
                         stick_scores=stick_scores, stick_fails=stick_fails, stick_out=stick_out,
                         latent_sums=latent_sums, rope=rope, scores=scores, turn=turn, context=context,
                         ln_a_mean=ln_a_mean, ln_a_var=ln_a_var, ln_mean=ln_mean, ln=ln)
            for kind, a, b in ORDER:
                if kind in steps:
                    steps[kind](a, b)


WEIGHTS = ["w_in", "w_glu", "w_up_ssm", "w_up_attn", "w_gate", "w_out", "w_ff1", "w_ff2", "w_ada_2", "w_in_2",
           "w_a_out_2", "w_b_out_2", "w_uq_2", "w_ukv_2", "w_c_out_2", "w_o_2"]


def columns(v):
    return np.asarray(v).reshape(-1, P).T


def lay_out(x):
    a = {n: np.ascontiguousarray(x[n]) for n in WEIGHTS}
    a["x_t"] = np.ascontiguousarray(np.asarray(x["x"])[0].T)
    a["positions"] = np.ascontiguousarray(x["positions_2"])
    par = np.zeros((P, NPAR), np.float32)

    def put(key, block):
        par[:, COL[key]:COL[key] + block.shape[1]] = block

    for n in ("norm_mix", "b_gate", "norm_mlp", "norm_final", "D_skip", "b_glu"):
        put(n, columns(x[n]))
    put("c", columns(x["c_2"]))
    for n in ("A_re", "A_im"):
        put(n, np.asarray(x[n])[0].reshape(PAIRS, 2 * STATE).T)
    put("log_dt", np.repeat(np.asarray(x["log_dt"])[0].reshape(PAIRS, 2), STATE, axis=1).T)
    freq = np.float32(10000.0) ** (-np.arange(0, ROPE, 2, dtype=np.float32) / np.float32(ROPE))
    rows = np.zeros((P, 1), np.float32)
    rows[NOPE:QK, 0] = np.tile(freq, 2)
    put("inv_freq", rows)
    for l in range(LAYERS):
        for n in ("b_ada", "conv_a_b", "ln_a_g", "ln_a_b", "q_norm_g", "kv_norm_g", "ln_g", "ln_b"):
            put((n, l), columns(x[n + "_2"][l]))
        for n in ("conv_a_w", "conv_b_w"):
            put((n, l), columns(x[n + "_2"][l]))
    a["params"] = par
    b = [np.asarray(x[n])[0].reshape(PAIRS, 2 * STATE, CIN).transpose(1, 0, 2).reshape(P, PAIRS * CIN)
         for n in ("B_re", "B_im")]
    a["b_state"] = np.ascontiguousarray(np.stack(b, 1))
    c = np.zeros((2, STATE, 2, PAIRS, 2, CIN), np.float32)
    for i, n in enumerate(("C_re", "C_im")):
        v = np.asarray(x[n])[0].reshape(PAIRS, 2, CIN, STATE)
        for g in range(2):
            c[g, :, i, :, g, :] = v[:, g].transpose(2, 0, 1)
    a["c_state"] = np.ascontiguousarray(c.reshape(P, 2, 4, P))
    return a


def program(nc, arrays):
    t = {n: nc.dram_tensor(f"in_{n}", a.shape, mybir.dt.from_np(a.dtype), kind="ExternalInput").ap()
         for n, a in arrays.items()}
    out = nc.dram_tensor("out_t", (D, T), F32, kind="ExternalOutput").ap()
    return t, out


def kernel(**inputs):
    import concourse.bacc as bacc
    from concourse.bass_utils import run_bass_kernel_spmd as run

    arrays = lay_out(inputs)
    marks = {}
    for dry in (True, False):
        nc = bacc.Bacc("TRN2", target_bir_lowering=False, num_devices=1)
        t, out = program(nc, arrays)
        build(nc, t, out, marks, dry)
    r = run(nc, [{f"in_{n}": a for n, a in arrays.items()}], core_ids=[0])
    return np.ascontiguousarray(r.results[0]["out_t"].T)[None]
```

```python
import math
from contextlib import ExitStack

import numpy as np

import concourse.bass as bass
from concourse import mybir

F32 = mybir.dt.float32
F32R = mybir.dt.float32r
I32 = mybir.dt.int32
ALU = mybir.AluOpType
ACT = mybir.ActivationFunctionType
AX = mybir.AxisListType

P = 128
T = 256
D = 1024
KT = D // P
W = 512
WT = W // P
HEADS = 8
DH = 64
DFF = 4 * D
GROUPS, CIN, STATE = 32, 16, 64
PAIRS = GROUPS // 2
CONV_A, CONV_B = 31, 3
CONV_PARTS = 8
CONV_STEP = -(-CONV_A // CONV_PARTS)
NOPE, ROPE = 64, 32
QK = NOPE + ROPE
QL, KVL = 384, 256
LAYERS = 2
RMS_EPS, LN_EPS = 1e-6, 1e-5
ALPHA = (2 * LAYERS) ** 0.25
SCALE2 = QK ** -0.5
BIG = 3.0e38

A1, A2, AG = 0, W, 2 * W
XB, GB, GC, BG = 3 * W, 4 * W, 5 * W, 6 * W
CQ = 7 * W
CKV = CQ + QL
CKR = CKV + KVL
CG = CKR + ROPE
CM = CG + W

COL = {}
_at = 0
for _name, _n in (("norm_mix", 8), ("b_gate", 16), ("norm_mlp", 8), ("norm_final", 8), ("D_skip", 4),
                  ("b_glu", 4), ("c", 8), ("A_re", 16), ("A_im", 16), ("log_dt", 16), ("inv_freq", 1)):
    COL[_name] = _at
    _at += _n
for _l in range(LAYERS):
    for _name, _n in (("b_ada", 24), ("conv_a_b", 4), ("ln_a_g", 4), ("ln_a_b", 4), ("conv_b_w", 12),
                      ("q_norm_g", 3), ("kv_norm_g", 2), ("ln_g", 8), ("ln_b", 8), ("conv_a_w", 124)):
        COL[_name, _l] = _at
        _at += _n
NPAR = _at
ADA = LAYERS * 3 * D // 256
FOUR = 4
LEVELS = int(math.log2(T))
ADA_PARTS = ((0, 14), (14, 17), (17, 20), (20, 24))

RAW = 4
HL = 3
SLOT = 2048

LN2_HI, LN2_LO = 0.693359375, -2.12194440e-4
TWO_PI = (6.28125, 1.9350051879882812e-3, 3.0199159819e-7)
PI_IN = 3.1415925
ROUND = 12582912.0


def schedule():
    panels, order = [], []
    count = {"split": 0, "group": 0, "gt": 0}

    def panel(job, layer, n, name, row, col, kt, cols, groups, split=True):
        gt = None
        if job in ("cg", "ag", "bg", "merge0", "merge1", "merge2"):
            gt = count["gt"]
            count["gt"] += 1
        panels.append(dict(index=len(panels), job=job, layer=layer, n=n, name=name, row=row, col=col, kt=kt,
                           cols=cols, split=split, s=count["split"] if split else None, g=count["group"],
                           groups=groups, gt=gt))
        count["split"] += split
        count["group"] += groups
        order.append(("panel", len(panels) - 1, 0))

    def wide(job, layer, name, col, width, row=0):
        for n in range(width // 256):
            panel(job, layer, n, name, row, col + 256 * n, KT, 256, 1)

    def half(job, layer, name, width, row=0):
        for n in range(width // 512):
            panel(job, layer, n, name, row, 512 * n, WT, 512, 2)

    def step(kind, a=0, b=0):
        order.append((kind, a, b))

    def ada_panel(i):
        panel("ada", i // 12, i % 12, "w_ada_2", 0, 256 * (i % 12), KT, 256, 1, split=False)

    def norm_sums(k, j):
        step("norm_squares", k, j)
        step("norm_sums", k, j)

    def norm_steps(k, key, i):
        ada_panel(i)
        norm_sums(k, 3)
        step("ada_take", i)
        step("norm", k)
        ada_panel(i + 1)
        step("ada_turn", i)
        step("ada_take", i + 1)
        ada_panel(i + 2)
        step("ada_turn", i + 1)
        if k == 2:
            step("modulate", 0)
        step("split", key)
        step("ada_take", i + 2)

    for j in range(4):
        norm_sums(0, j)
    step("split_ahead", 1)
    step("norm", 0)
    step("split_ahead", 2)
    step("split", "u0")
    step("silu")
    step("s5_angle")
    wide("ssm", 0, "w_in", 0, W)
    step("s5_sines")
    step("s5_prep")
    wide("q", 0, "w_in", W, W)
    wide("k", 0, "w_in", 2 * W, W)
    wide("v", 0, "w_in", 3 * W, W)
    step("s5_turn")
    for r in range(FOUR):
        step("bu", r)
    step("stick_scores", 0)
    ada_panel(0)
    step("ada_take", 0)
    step("ada_turn", 0)
    for m in range(HEADS + 1):
        f = m // 2
        if m % 2 == 0 and f:
            for r in range(FOUR):
                step("s5_out", FOUR * (f - 1) + r)
        if m:
            step("stick_weights", m - 1)
        if m == HEADS:
            step("stick_out", m - 1)
            step("split", "ctx")
        if m < HEADS:
            step("stick_soft", m)
        if m % 2 == 0 and f >= 2:
            step("s5_inner", f - 2)
        if m % 2 and f >= 2:
            step("s5_gelu", f - 2)
        if m % 2 and f:
            step("s5_y", f - 1)
        if m == HEADS:
            break
        step("scan_down" if m % 2 else "scan_up", f)
        ahead = [("bu", FOUR * (f + 1) + 2 * (m % 2) + r) for r in range(2)] if f + 1 < PAIRS // FOUR else []
        if ahead:
            step(*ahead[0])
        step("stick_fails", m)
        if m + 1 < HEADS:
            step("stick_scores", m + 1)
        panel("gate", 0, m, "w_gate", 0, 256 * m, KT, 256, 1)
        if ahead:
            step(*ahead[1])
        if m:
            step("stick_out", m - 1)
        ada_panel(m + 1)
        step("ada_take", m + 1)
        step("ada_turn", m + 1)
    step("s5_gelu", WT - 2)
    step("s5_y", WT - 1)
    ada_panel(9)
    step("s5_inner", WT - 1)
    step("ada_take", 9)
    ada_panel(10)
    step("s5_gelu", WT - 1)
    step("ada_turn", 9)
    step("ada_take", 10)
    step("ada_turn", 10)
    step("split", "y")
    half("up_attn", 0, "w_up_attn", D)
    half("glu", 0, "w_glu", W)
    ada_panel(11)
    step("glu_mul")
    step("split", "yg")
    step("ada_take", 11)
    step("ada_turn", 11)
    half("up_ssm", 0, "w_up_ssm", D)
    ada_panel(12)
    step("split", "u1")
    step("ada_take", 12)
    step("ada_turn", 12)
    ada_panel(13)
    step("ada_take", 13)
    step("ada_turn", 13)
    step("ada_end", 0)
    for n in range(4):
        panel("out", 0, n, "w_out", 0, 256 * n, KT, 256, 1)
        if n:
            norm_sums(1, n - 1)
    norm_steps(1, "u2", 14)
    chunks = DFF // W
    for c in range(chunks + 1):
        if c < chunks:
            for n in range(2):
                panel("ff1", 0, 2 * c + n, "w_ff1", 0, W * c + 256 * n, KT, 256, 1)
                if (c, n) == (0, 0):
                    step("ada_turn", 16)
                    step("ada_end", 1)
        if c >= 1:
            for n in range(2):
                panel("ff2", 0, 2 * (c - 1) + n, "w_ff2", W * (c - 1), 512 * n, WT, 512, 2)
        if c == 2:
            step("rope_tables")
    for j in range(3):
        norm_sums(2, j)
    norm_steps(2, ("u", 0), 17)
    for l in range(LAYERS):
        panel("q_lat", l, 0, "w_in_2", 0, CQ, KT, 256, 1)
        if l == 0:
            step("ada_turn", 19)
            step("ada_end", 2)
        else:
            step("ada_turn", 23)
            step("ada_end", 3)
        panel("q_lat", l, 1, "w_in_2", 0, CQ + 256, KT, 128, 1)
        panel("kv_lat", l, 0, "w_in_2", 0, CKV, KT, 256, 1)
        panel("k_rope", l, 0, "w_in_2", 0, CKR + ROPE - QK, KT, QK, 1)
        step("latent_sums", l)
        if l == 0:
            step("prescale", l)
        else:
            step("ln_affine", l - 1)
        step("latent_norm", l)
        wide("a2", l, "w_in_2", A2, W)
        step("split", ("ql", l))
        step("split", ("kvl", l))
        wide("a1", l, "w_in_2", A1, W)
        for n in range(2):
            panel("uq", l, n, "w_uq_2", 0, 4 * QK * n, QL // P, 4 * QK, 2)
        panel("ukv", l, 0, "w_ukv_2", 0, 0, KVL // P, 1024, 6)
        parts = iter(range(2 * CONV_PARTS))
        for _ in range(6):
            step("conv_a", l, next(parts))
        step("rope", l)
        wide("cg", l, "w_in_2", CG, W)
        between = [(job, at, n) for job, at in (("xb", XB), ("gc", GC), ("gb", GB), ("bg", BG), ("ag", AG)) for n in range(2)]
        for h in range(HEADS + 2):
            if h < HEADS:
                step("scores", l, h)
            if 1 <= h <= HEADS:
                step("normalise", l, h - 1)
            job, at, n = between[h]
            panel(job, l, n, "w_in_2", 0, at + 256 * n, KT, 256, 1)
            if 1 <= h <= HEADS:
                step("turn", l, h - 1)
            if h >= 2:
                step("context", l, h - 2)
            if h == 3:
                step("conv_b", l)
            elif h < 5:
                step("conv_a", l, next(parts))
            if h == 8:
                step("split", ("b", l))
        step("conv_a", l, next(parts))
        step("split", ("c", l))
        half("branch1", l, "w_b_out_2", D)
        for part in parts:
            step("conv_a", l, part)
        for n in range(4):
            panel("merge1", l, n, "w_in_2", 0, CM + D + 256 * n, KT, 256, 1)
            if n == 1:
                step("ln_a_mean", l)
            if n == 3:
                step("ln_a_var", l)
        half("branch2", l, "w_c_out_2", D)
        for n in range(4):
            panel("merge2", l, n, "w_in_2", 0, CM + 2 * D + 256 * n, KT, 256, 1)
            if n == 0:
                step("ln_a_out", l)
            if n == 1:
                step("split", ("a", l))
        half("branch0", l, "w_a_out_2", D)
        wide("merge0", l, "w_in_2", CM, D)
        step("split", ("m", l))
        if l == 0:
            step("modulate_columns", 1)
        for n in range(4):
            panel("w_o", l, n, "w_o_2", 0, 256 * n, KT, 256, 1)
            if n:
                step("ln_mean", l, n - 1)
        if l == 0:
            ada_panel(20)
        step("ln_mean", l, 3)
        if l == 0:
            step("ada_take", 20)
        step("ln_centre", l)
        if l == 0:
            ada_panel(21)
            step("ada_turn", 20)
            step("ada_take", 21)
        step("ln", l)
        if l == 0:
            ada_panel(22)
            step("ada_turn", 21)
            step("ada_take", 22)
            step("ada_turn", 22)
            ada_panel(23)
        if l == 0:
            step("modulate", 1)
            step("split", ("u", 1))
            step("ada_take", 23)
        if l == LAYERS - 1:
            step("ln_affine", l)
    return panels, order


PANELS, ORDER = schedule()
SPLIT = [q for q in PANELS if q["split"]]


def groups_of(job, layer=0):
    return [g for q in PANELS if q["job"] == job and q["layer"] == layer for g in range(q["g"], q["g"] + q["groups"])]


def find(job, layer=0, n=0):
    return next(q for q in PANELS if q["job"] == job and q["layer"] == layer and q["n"] == n)


ROOTS = [("norm", 0), ("norm", 1), ("norm", 2)]
for _l in range(LAYERS):
    ROOTS += [("lat_q", _l), ("lat_kv", _l), ("var_a", _l), ("var", _l)]

BU_ORDER = [a for kind, a, _ in ORDER if kind == "bu"]
LAST_PAIR = {a // 4: a for kind, a, _ in ORDER if kind == "s5_out"}

SUMS = [("norm", 0), ("ada", 0), ("norm", 1), ("norm", 2)]
for _l in range(LAYERS):
    SUMS += [("lat", _l), ("mean_a", _l), ("var_a", _l), ("mean", _l), ("var", _l)]


def build(nc, t, out, marks, dry):
    ctx = ExitStack()
    with ctx:
        sems = {}
        counts = {}

        def sem(name):
            if name not in sems:
                sems[name] = ctx.enter_context(nc.semaphore(name))
                counts[name] = 0
            return sems[name]

        def event(name, *key):
            s = sem(name)
            counts[name] += 1
            marks[(name, *key)] = counts[name]
            return s, 1

        def over(name, *key):
            sem(name)
            return 1 if dry and (name, *key) not in marks else marks[(name, *key)]

        def emptied(groups):
            for b in range(2):
                of_bank = [g for g in groups if g % 2 == b]
                if of_bank:
                    yield sem(f"bank_free{b}"), max(of_bank) // 2 + 1

        def landed(q):
            return sem(f"raw{q['index'] % RAW}"), 16 * (q["index"] // RAW + 1)

        def slot_free(q):
            return sem(f"raw_free{q['index'] % RAW}"), q["index"] // RAW + 1

        class Count:

            def __init__(self, own):
                self.own = own
                self.last = (sem(own), 0)

            def event(self, name, *key):
                s, _ = event(name, *key)
                self.last = (s, counts[name])
                return s, 1

            def step(self):
                return self.event(self.own)

            def bank_free(self, g):
                self.last = (sem(f"bank_free{g % 2}"), g // 2 + 1)
                return self.last[0], 1

        def sb(name, shape, dt=F32):
            return ctx.enter_context(nc.sbuf_tensor(name, shape, dt))

        def bank(name):
            return ctx.enter_context(nc.psum_tensor(name, [P, 512], F32))

        raw = sb("raw", [P, RAW, SLOT])
        w_hi = sb("w_hi", [P, HL, SLOT], F32R)
        w_lo = sb("w_lo", [P, HL, SLOT], F32R)
        u_hi = sb("u_hi", [P, KT, T], F32R)
        u_lo = sb("u_lo", [P, KT, T], F32R)
        v_hi = [sb("va_hi", [P, WT, T], F32R), sb("vb_hi", [P, WT, T], F32R)]
        v_lo = [sb("va_lo", [P, WT, T], F32R), sb("vb_lo", [P, WT, T], F32R)]
        h = sb("h", [P, KT, T])
        par = sb("par", [P, NPAR])
        ident = sb("ident", [P, P])
        ones = sb("ones", [P, P])
        ntri = sb("ntri", [P, P])
        nones = sb("nones", [P, P])
        mask1 = sb("mask1", [P, 384])
        neg1 = sb("neg1", [P, 384])
        mask2 = sb("mask2", [P, 384])
        rot = sb("rot", [P, ROPE])
        pos = sb("pos", [P, T], I32)
        rows5 = sb("rows5", [P, 5 * T])
        nmean, rcos, rsin = (rows5[:, T * i:T * i + T] for i in range(3))
        rstd = rows5[:, 3 * T:5 * T].rearrange("p (a n) -> p a n", a=2)
        root = sb("root", [P, 2, T])
        silu_c = sb("silu_c", [P, KT])
        ada = sb("ada", [P, LAYERS, 24])
        scale1 = sb("scale1", [P, KT])
        shift1 = sb("shift1", [P, KT])
        rest_g = sb("rest_g", [P, KT])
        rest_b = sb("rest_b", [P, KT])
        sums = sb("sums", [P, 2, 2])
        nmax = sb("nmax", [P, 2, 2])
        mx = sb("mx", [P, 2, 2])
        rsum = sb("rsum", [P, 2, 2])
        AREA = 18110
        area = sb("area", [P, AREA])
        spot = [0]

        def cut(*shape):
            n = math.prod(shape)
            a = area[:, spot[0]:spot[0] + n]
            spot[0] += n
            assert spot[0] <= AREA, spot
            if len(shape) == 2:
                return a.rearrange("p (a b) -> p a b", a=shape[0])
            if len(shape) == 3:
                return a.rearrange("p (a b c) -> p a b c", a=shape[0], b=shape[1])
            return a

        def pair(ap):
            return ap.rearrange("p (a n) -> p a n", a=2)

        tmp = cut(KT, T)
        gates = cut(16, T)
        ussm = cut(WT, T)
        q1 = cut(WT, T)
        k1 = cut(WT, T)
        v1 = cut(2, W)
        merged = cut(KT, T)
        ct = cut(2, 4, P)
        bt = cut(2, 4, P)
        bst = merged[:, 0:2, :]
        bd = merged[:, 2:6, :].rearrange("p (a b) n -> p a (b n)", a=2)
        btmp = merged[:, 6:7, :].rearrange("p a n -> p (a n)")
        state6 = cut(2 * T)
        small = state6[:, 0:22 * 16].rearrange("p (a n) -> p a n", a=22)
        power = cut(8, 3, 16)
        xs = cut(4, 2, T)
        states = [xs[:, i] for i in range(4)] + [merged[:, 4:6, :], merged[:, 6:8, :], pair(state6), pair(rows5[:, 0:2 * T])]
        stick_w = cut(2, 384)
        stick_z = tmp[:, 4:7, :].rearrange("p a n -> p (a n)").rearrange("p (a n) -> p a n", a=2)
        stick = [stick_z[:, 0], stick_z[:, 1], stick_w[:, 0], stick_w[:, 1]]
        context1 = merged[:, 0:4, :]
        yv = tmp[:, 0:4, :]
        yt = tmp[:, 4:8, :]
        y1 = tmp[:, 7, :]
        spot[0] = KT * T
        qf = cut(HEADS, T)
        kf = cut(HEADS, T)
        v2 = cut(2, W)
        q_lat = cut(3, T)
        kv_lat = cut(2, T)
        kpe = cut(T)
        kpr = cut(T)
        apad = cut(WT, T + CONV_A - 1)
        acc = cut(WT, T)
        agate = cut(WT, T)
        bpad = cut(WT, T + CONV_B - 1)
        cgate = cut(WT, T)
        lat_sq = cut(5, T)
        soft = cut(2, 384)
        soft_t = cut(2, 384)
        rtmp = tmp[:, 0:2, :]
        gtmp = cut(2, 512)
        xbv = lat_sq[:, 0:4, :]
        bconv = tmp[:, 4:8, :]
        ybr = qf
        mer = kf

        pg = [bank("pg0"), bank("pg1")]
        p_bu, p_y, p_z, p_c, p_o, p_s = (bank(n) for n in ("p_bu", "p_y", "p_z", "p_c", "p_o", "p_s"))

        def col(name, n=0, w=1):
            a = COL[name] + n
            return par[:, a:a + w]

        def spread(ap, *shape):
            return ap.unsqueeze(1).broadcast_to(list(shape))

        def slot(tensor, q):
            n = q["index"] % RAW if tensor is raw else q["s"] % HL
            return tensor[:, n, 0:q["kt"] * q["cols"]].rearrange("p (k n) -> p k n", k=q["kt"])

        def operand(src, hi, lo, pieces, ready, after):
            return dict(src=src, hi=hi, lo=lo, pieces=pieces, ready=ready, after=after)

        def u_operand(src, ready, after):
            return operand(src, u_hi, u_lo, [(2 * j, 2 * j + 2) for j in range(4)], ready, after)

        def v_operand(src, n, tiles, ready, after):
            return operand(src, v_hi[n], v_lo[n], [(0, tiles)], ready, after)

        OPERANDS = {
            "u0": u_operand(tmp, "rows", None),
            "ctx": v_operand(context1, 0, WT, None, None),
            "y": v_operand(yv, 1, WT, "rows", None),
            "yg": v_operand(yv, 0, WT, "rows", groups_of("up_attn")[-1]),
            "u1": u_operand(merged, "rows", groups_of("gate")[-1]),
            "u2": u_operand(tmp, "rows", groups_of("out")[-1]),
        }
        for l in range(LAYERS):
            OPERANDS["u", l] = u_operand(tmp, "rows", groups_of("ff1")[-1] if l == 0 else groups_of("w_o", 0)[-1])
            OPERANDS["ql", l] = v_operand(q_lat, 1, 3, "rows",
                                          groups_of("ff2")[-1] if l == 0 else groups_of("branch0", 0)[-1])
            OPERANDS["kvl", l] = v_operand(kv_lat, 0, 2, "rows",
                                           groups_of("ff2")[-1] if l == 0 else groups_of("branch2", 0)[-1])
            OPERANDS["b", l] = v_operand(bconv, 1, WT, "bg", groups_of("uq", l)[-1])
            OPERANDS["a", l] = v_operand(acc, 1, WT, "rows", groups_of("branch1", l)[-1])
            OPERANDS["c", l] = v_operand(cgate, 0, WT, "rows", groups_of("ukv", l)[-1])
            OPERANDS["m", l] = u_operand(mer, "merge0", groups_of("merge0", l)[-1])

        FUSED = ("u0", "u2", ("u", 0), ("u", 1))

        USES = {"ssm": "u0", "q": "u0", "k": "u0", "v": "u0", "gate": "u0", "up_attn": "ctx", "glu": "y",
                "up_ssm": "yg", "out": "u1", "ff1": "u2"}

        def operand_of(q):
            if q["job"] in USES:
                return USES[q["job"]]
            own = {"uq": "ql", "ukv": "kvl", "branch1": "b", "branch0": "a", "branch2": "c", "w_o": "m"}
            return own.get(q["job"], "u"), q["layer"]

        def sums_before(key):
            key = SUMS[SUMS.index(key) - 1]
            name = "ada" if key[0] == "ada" else "nmean" if key[0] in ("mean_a", "mean") else "root"
            return sem(name), over(name, 0) if key[0] == "ada" else over(name, ("lat_kv", key[1]) if key[0] == "lat" else key)

        def next_splits(at, ahead):
            passed = sum(q["split"] for q in PANELS[:at])
            within = RAW if PANELS[at]["split"] else 2
            while ahead[0] < min(passed + HL, len(SPLIT)) and SPLIT[ahead[0]]["index"] < at + within:
                yield SPLIT[ahead[0]]
                ahead[0] += 1

        def first_splits(n, ahead):
            while ahead[0] < n:
                yield SPLIT[ahead[0]]
                ahead[0] += 1

        block = ctx.enter_context(nc.Block())

        @block.sync
        def _(sp):
            for j in range(4):
                sp.dma_start(h[:, 2 * j:2 * j + 2, :], t["x_t"].rearrange("(k p) n -> p k n", p=P)[:, 2 * j:2 * j + 2, :]
                             ).then_inc(sem(f"x_landed{j}"), 16)
            for q in PANELS:
                n = q["index"] % RAW
                if q["index"] >= RAW:
                    sp.wait_ge(sem(f"raw_free{n}"), q["index"] // RAW)
                w = t[q["name"]][q["layer"], q["row"]:q["row"] + P * q["kt"], q["col"]:q["col"] + q["cols"]]
                sp.dma_start(slot(raw, q), w.rearrange("(k p) n -> p k n", p=P)).then_inc(sem(f"raw{n}"), 16)
            for j in range(4):
                sp.wait_ge(sem("affine"), over("affine", LAYERS - 1, 2 * j + 1))
                sp.dma_start(out.rearrange("(k p) n -> p k n", p=P)[:, 2 * j:2 * j + 2, :],
                             h[:, 2 * j:2 * j + 2, :]).then_inc(sem("stored"), 16)
            sp.wait_ge(sem("stored"), 4 * 16)

        @block.gpsimd
        def _(pool):
            c = Count("const")
            pool.dma_start(par[:, :], t["params"]).then_inc(sem("par_landed"), 16)
            pool.dma_start(bst, t["b_state"]).then_inc(sem("s5_landed"), 16)
            pool.dma_start(ct, t["c_state"]).then_inc(sem("s5_landed"), 16)
            pool.dma_start(pos[NOPE:QK, :], t["positions"].partition_broadcast(ROPE)).then_inc(sem("pos_landed"), 16)
            pool.memset(ones[:, :], 1.0).then_inc(*c.event("const", "ones"))
            pool.memset(nones[:, :], -1.0).then_inc(*c.step())
            pool.memset(ident[:, :], 0.0).then_inc(*c.step())
            pool.memset(mask1[:, :], 1.0).then_inc(*c.step())
            pool.memset(neg1[:, :], 0.0).then_inc(*c.step())
            pool.memset(mask2[:, :], 0.0).then_inc(*c.step())
            pool.memset(ntri[:, :], -1.0).then_inc(*c.step())
            pool.memset(rot[:, :], 0.0).then_inc(*c.step())
            pool.wait_ge(*c.last)
            pool.affine_select(out=ident[:, :], in_=ident[:, :], compare_op=ALU.not_equal, fill=1.0,
                                      base=0, pattern=[[-1, P]], channel_multiplier=1).then_inc(*c.step())
            pool.affine_select(out=ntri[:, :], in_=ntri[:, :], compare_op=ALU.is_ge, fill=0.0,
                                      base=0, pattern=[[-1, P]], channel_multiplier=1).then_inc(*c.step())
            for lo, w in ((0, 256), (256, 128)):
                pool.affine_select(out=mask1[:, lo:lo + w], in_=mask1[:, lo:lo + w], compare_op=ALU.is_gt,
                                          fill=0.0, base=0, pattern=[[1, w]], channel_multiplier=-1).then_inc(*c.step())
                pool.affine_select(out=neg1[:, lo:lo + w], in_=neg1[:, lo:lo + w], compare_op=ALU.is_gt,
                                          fill=-BIG, base=0, pattern=[[1, w]], channel_multiplier=-1).then_inc(*c.step())
            for lo in (0, 256):
                pool.affine_select(out=mask2[:, lo:lo + P], in_=mask2[:, lo:lo + P], compare_op=ALU.is_ge,
                                          fill=-BIG, base=0, pattern=[[-1, P]], channel_multiplier=1).then_inc(*c.step())
            half_rope = ROPE // 2
            for sign, base in ((-1.0, -half_rope), (1.0, half_rope)):
                pool.wait_ge(*c.last)
                pool.affine_select(out=rot[NOPE:QK, :], in_=rot[NOPE:QK, :], compare_op=ALU.not_equal,
                                          fill=sign, base=base, pattern=[[-1, ROPE]], channel_multiplier=1).then_inc(*c.step())
            pool.wait_ge(*c.last)
            pool.memset(sums[:, :, :], 0.0).then_inc(*c.event("const", "all"))
            ahead = [0]

            def low_halves(some):
                for q in some:
                    pool.wait_ge(sem("w_hi"), over("w_hi", q["s"]))
                    if q["s"] >= HL:
                        past = SPLIT[q["s"] - HL]
                        pool.wait_ge(sem("groups"), past["g"] + past["groups"] - 1 + 1)
                    n = q["kt"] * q["cols"]
                    r, s = q["index"] % RAW, q["s"] % HL
                    pool.tensor_tensor(w_lo[:, s, 0:n], raw[:, r, 0:n], w_hi[:, s, 0:n].bitcast(F32),
                                       ALU.subtract).then_inc(sem(f"raw_free{r}"), 1)

            for kind, a, b in ORDER:
                if kind == "panel":
                    low_halves(next_splits(a, ahead))
                elif kind == "split_ahead":
                    low_halves(first_splits(a, ahead))

        @block.scalar
        def _(act):
            c = Count("act")
            ahead = [0]

            def fn(out_, in_, func, **kw):
                act.wait_ge(*c.last)
                return act.activation(out_, in_, func, **kw)

            def split_ahead(n, _):
                high_halves(first_splits(n, ahead))

            def silu(_, __):
                act.wait_ge(sem("par_landed"), 16)
                act.wait_ge(sem("const"), over("const", "all"))
                fn(silu_c[:, :], col("c", 0, KT), ACT.Sigmoid).then_inc(*c.event("c_sig"))

            def high_halves(some):
                for q in some:
                    act.wait_ge(*landed(q))
                    if q["s"] >= HL:
                        past = SPLIT[q["s"] - HL]
                        act.wait_ge(sem("groups"), past["g"] + past["groups"] - 1 + 1)
                        act.wait_ge(*slot_free(past))
                    n = q["kt"] * q["cols"]
                    act.activation(w_hi[:, q["s"] % HL, 0:n], raw[:, q["index"] % RAW, 0:n], ACT.Copy).then_inc(*c.event("w_hi", q["s"]))

            def take(g, dst, src, func=ACT.Copy, **kw):
                act.wait_ge(sem("groups"), g + 1)
                act.wait_ge(*c.last)
                act.activation(dst, src, func, **kw).then_inc(*c.bank_free(g))

            def square_root(key, region, mean_of, eps, which=0):
                act.wait_ge(sem("stats"), over("stats", ("lat", key[1]) if key[0] in ("lat_q", "lat_kv") else key))
                if key[0] != "norm" or key[1]:
                    act.wait_ge(sem("rstd"), over("rstd", ROOTS[ROOTS.index(key) - 1]))
                fn(root[:, which, :], p_s[:, region * T:region * T + T], ACT.Sqrt, bias=eps,
                   scale=1.0 / mean_of).then_inc(*c.event("root", key))

            def split(key, _):
                o = OPERANDS[key]
                if o["after"] is not None:
                    act.wait_ge(sem("groups"), o["after"] + 1)
                if isinstance(key, tuple) and key[0] == "u":
                    l = key[1]
                    act.wait_ge(sem("scale1"), over("scale1", l))
                    for j in range(KT):
                        if l == 0:
                            act.wait_ge(sem("h_rows"), over("h_rows", j))
                        else:
                            act.wait_ge(sem("ln_rows"), over("ln_rows", l - 1, j // 2))
                        fn(u_hi[:, j, :], h[:, j, :], ACT.Identity, bias=shift1[:, j:j + 1],
                           scale=scale1[:, j:j + 1]).then_inc(*(c.event("hi", key, j // 2) if j % 2 else c.step()))
                    return
                for j, (a, b) in enumerate(o["pieces"]):
                    if o["ready"] == "rows":
                        act.wait_ge(sem("rows"), over("rows", key, j))
                    elif o["ready"]:
                        act.wait_ge(sem("gt_used"), over("gt_used", find(o["ready"], key[1], j if len(o["pieces"]) > 1 else 1)["gt"]))
                    fn(o["hi"][:, a:b, :], o["src"][:, a:b, :], ACT.Copy).then_inc(*c.event("hi", key, j))

            def norm_squares(k, j):
                if k == 0:
                    act.wait_ge(sem(f"x_landed{j}"), 16)
                else:
                    for s, v in emptied([groups_of("out" if k == 1 else "ff2")[j - 4]]):
                        act.wait_ge(s, v)
                fn(tmp[:, 2 * j:2 * j + 2, :], h[:, 2 * j:2 * j + 2, :], ACT.Square).then_inc(*c.event("squares", ("norm", k), j))

            def norm(k, _):
                square_root(("norm", k), 0, D, RMS_EPS)

            def ada_take(i, _):
                if i:
                    act.wait_ge(sem("ada_turned"), over("ada_turned", i - 1))
                g = find("ada", i // 12, i % 12)["g"]
                take(g, root[0:1, 1, :], pg[g % 2][0:1, 0:256])

            def panel(p, _):
                q = PANELS[p]
                job, l, n, g = q["job"], q["layer"], q["n"], q["g"]
                high_halves(next_splits(p, ahead))
                both = pair(pg[g % 2][:, :])
                if job == "ssm":
                    take(g, ussm[:, 2 * n:2 * n + 2, :], both)
                elif job == "q":
                    take(g, q1[:, 2 * n:2 * n + 2, :], both, scale=DH ** -0.5)
                elif job == "k":
                    take(g, k1[:, 2 * n:2 * n + 2, :], both)
                elif job == "v":
                    take(g, v1[:, :, 256 * n:256 * n + 256], both)
                elif job == "gate":
                    act.wait_ge(sem("groups"), g + 1)
                    fn(gates[:, 2 * n, :], both[:, 0, :], ACT.Sigmoid, bias=col("b_gate", 2 * n)).then_inc(*c.step())
                    take(g, gates[:, 2 * n + 1, :], both[:, 1, :], ACT.Sigmoid, bias=col("b_gate", 2 * n + 1))
                elif job == "glu":
                    for i in range(2):
                        b = pair(pg[(g + i) % 2][:, :])
                        act.wait_ge(sem("groups"), g + i + 1)
                        act.wait_ge(sem("lo"), over("lo", "y", 0))
                        fn(yt[:, 2 * i, :], b[:, 0, :], ACT.Sigmoid, bias=col("b_glu", 2 * i)).then_inc(*c.step())
                        take(g + i, yt[:, 2 * i + 1, :], b[:, 1, :], ACT.Sigmoid, bias=col("b_glu", 2 * i + 1))
                elif job == "ff1":
                    f, f2 = 4 * (n % 2), 4 * (n % 2) + 2
                    for s, v in emptied([g]):
                        act.wait_ge(s, v)
                    if n >= 2:
                        act.wait_ge(sem("ff_lo"), over("ff_lo", n - 2))
                    fn(tmp[:, f2:f2 + 2, :], tmp[:, f:f + 2, :], ACT.Square).then_inc(*c.step())
                    ch = n // 2
                    past = groups_of("ff2")[4 * (ch - 2) + 3] if ch >= 2 else groups_of("glu" if ch == 0 else "up_ssm")[-1]
                    act.wait_ge(sem("groups"), past + 1)
                    fn(v_hi[(ch + 1) % 2][:, 2 * (n % 2):2 * (n % 2) + 2, :], tmp[:, f2:f2 + 2, :], ACT.Copy).then_inc(*c.event("ff_hi", n))
                elif job == "q_lat":
                    take(g, q_lat[:, 2 * n:2 * n + q["cols"] // P, :], both[:, 0:q["cols"] // P, :])
                elif job == "kv_lat":
                    take(g, kv_lat, both)
                elif job == "k_rope":
                    take(g, kpe[NOPE:QK, :], pg[g % 2][NOPE:QK, 0:T])
                elif job == "a2":
                    take(g, acc[:, 2 * n:2 * n + 2, :], both, ACT.Sigmoid)
                elif job == "uq":
                    for i in range(2):
                        a = 4 * n + 2 * i
                        take(g + i, qf[0:QK, a:a + 2, :], pair(pg[(g + i) % 2][0:QK, :]))
                elif job == "ukv":
                    for i in range(4):
                        take(g + i, kf[0:NOPE, 2 * i:2 * i + 2, :], pair(pg[(g + i) % 2][0:NOPE, :]))
                    for i in range(2):
                        take(g + 4 + i, v2[:, i, :], pg[(g + 4 + i) % 2][:, :])
                elif job == "xb":
                    take(g, xbv[:, 2 * n:2 * n + 2, :], both)
                elif job in ("cg", "ag", "bg"):
                    gt_free(q["gt"])
                    act.wait_ge(sem("groups"), g + 1)
                    fn(gtmp[:, q["gt"] % 2, :], pg[g % 2][:, :], ACT.Sigmoid).then_inc(*c.event("sigmoid", q["gt"]))
                elif job in ("branch0", "branch1", "branch2"):
                    before = {"branch1": None, "branch2": "merge1", "branch0": "merge2"}[job]
                    for i in range(2):
                        a = 4 * n + 2 * i
                        if before:
                            act.wait_ge(sem("gt_used"), over("gt_used", find(before, l, a // 2)["gt"]))
                        take(g + i, ybr[:, a:a + 2, :], pair(pg[(g + i) % 2][:, :]))
                elif job in ("merge0", "merge1", "merge2"):
                    gt_free(q["gt"])
                    take(g, gtmp[:, q["gt"] % 2, :], pg[g % 2][:, :], ACT.Sigmoid)

            def gt_free(k):
                if k >= 2:
                    past = next(q for q in PANELS if q["gt"] == k - 2)
                    if past["job"] in ("cg", "ag"):
                        for s, v in emptied([past["g"]]):
                            act.wait_ge(s, v)
                    else:
                        act.wait_ge(sem("gt_used"), over("gt_used", k - 2))

            def s5_sines(_, __):
                act.wait_ge(sem("angle"), over("angle"))
                fn(small[:, 20:22, :], small[:, 18:20, :], ACT.Sin).then_inc(*c.event("sines"))

            def s5_turn(_, __):
                act.wait_ge(sem("bt_ps"), over("bt_ps"))
                for k, b in enumerate((p_bu, p_z)):
                    fn(bt[:, k, :, :], b[:, :].rearrange("p (a n) -> p a n", a=4), ACT.Copy).then_inc(*c.event("bt", k))

            def bu(r, _):
                act.wait_ge(sem("bu"), over("bu", r))
                if r >= len(states):
                    act.wait_ge(sem("cx"), over("cx", r - len(states)))
                fn(states[r % len(states)], pair(p_bu[:, :]), ACT.Copy).then_inc(*c.event("bu_sb", r))

            def s5_y(f, _):
                act.wait_ge(sem("y_rows"), over("y_rows", f))
                fn(y1, yv[:, f, :], ACT.Square).then_inc(*c.event("y_sq", f))

            def s5_inner(f, _):
                act.wait_ge(sem("y_inner"), over("y_inner", f))
                fn(y1, y1, ACT.Sigmoid, scale=2 * math.sqrt(2 / math.pi)).then_inc(*c.event("y_sig", f))

            def stick_scores(hd, _):
                act.wait_ge(sem("z"), over("z", hd))
                if hd:
                    act.wait_ge(sem("soft"), over("soft", hd - 1))
                fn(stick[0], p_z[:, 0:384], ACT.Abs).then_inc(*c.step())
                fn(stick[0], stick[0], ACT.Exp, scale=-1.0).then_inc(*c.step())
                fn(stick[0], stick[0], ACT.Ln, bias=1.0).then_inc(*c.event("log1p", hd))

            def stick_weights(hd, _):
                act.wait_ge(sem("logw"), over("logw", hd))
                fn(stick[2 + hd % 2], stick[2 + hd % 2], ACT.Exp).then_inc(*c.event("w_stick", hd))

            def stick_out(hd, _):
                if hd % 2:
                    i = hd // 2
                    act.wait_ge(sem("o_stick"), over("o_stick", hd))
                    fn(context1[:, i, :], p_o[:, T * (i % 2):T * (i % 2) + T], ACT.Copy).then_inc(*c.event("ctx", i))

            def rope_tables(_, __):
                act.wait_ge(sem("rope_angle"), over("rope_angle"))
                fn(rsin[NOPE:QK], rsin[NOPE:QK], ACT.Sin).then_inc(*c.step())
                fn(rcos[NOPE:QK], rcos[NOPE:QK], ACT.Sin).then_inc(*c.event("rope_sines"))

            def prescale(l, _):
                act.wait_ge(sem("rows"), over("rows", ("u", l), 3))
                fn(h[:, :, :], h[:, :, :], ACT.Copy, scale=ALPHA).then_inc(*c.event("alpha_h", l))

            def latent_sums(l, _):
                fn(lat_sq[:, 0:3, :], q_lat, ACT.Square).then_inc(*c.step())
                fn(lat_sq[:, 3:5, :], kv_lat, ACT.Square).then_inc(*c.event("squares", ("lat", l)))

            def latent_norm(l, _):
                square_root(("lat_q", l), 0, QL, RMS_EPS, 0)
                square_root(("lat_kv", l), 1, KVL, RMS_EPS, 1)

            def scores(l, hd):
                b = hd % 2
                act.wait_ge(sem("nmax"), over("nmax", l, hd))
                for tt, (lo, hi) in enumerate(((0, P), (P, 3 * P))):
                    fn(soft[:, b, lo:hi], soft[:, b, lo:hi], ACT.Exp,
                       bias=nmax[:, b, tt:tt + 1], scale=SCALE2, accum_out=sums[:, b, tt:tt + 1]).then_inc(*c.event("probs", l, hd, tt))

            def turn(l, hd):
                act.wait_ge(sem("turned"), over("turned", l, hd))
                fn(soft_t[:, hd % 2, :], p_c[:, 0:384], ACT.Copy).then_inc(*c.event("probs_t", l, hd))

            def ln_a_var(l, _):
                act.wait_ge(sem("centred_a"), over("centred_a", l))
                fn(tmp[:, 0:4, :], acc, ACT.Square).then_inc(*c.event("squares", ("var_a", l)))
                square_root(("var_a", l), 1, W, LN_EPS)

            def ln_a_out(l, _):
                for j in range(WT):
                    act.wait_ge(sem("a_affine"), over("a_affine", l, j))
                    fn(tmp[:, j, :], acc[:, j, :], ACT.Sigmoid).then_inc(*c.event("a_sig", l, j))

            def ln_centre(l, _):
                for j in range(4):
                    act.wait_ge(sem("centred"), over("centred", l, j))
                    fn(tmp[:, 2 * j:2 * j + 2, :], h[:, 2 * j:2 * j + 2, :], ACT.Square).then_inc(*c.event("squares", ("var", l), j))

            def ln(l, _):
                square_root(("var", l), 1, D, LN_EPS)

            def ln_affine(l, _):
                for j in range(KT):
                    if l < LAYERS - 1:
                        act.wait_ge(sem("rows"), over("rows", ("u", l + 1), j // 2))
                        fn(h[:, j, :], h[:, j, :], ACT.Identity, bias=rest_b[:, j:j + 1],
                           scale=rest_g[:, j:j + 1]).then_inc(*(c.event("alpha_h", l + 1) if j == KT - 1 else c.step()))
                    else:
                        act.wait_ge(sem("ln_rows"), over("ln_rows", l, j // 2))
                        fn(h[:, j, :], h[:, j, :], ACT.Identity,
                           bias=col(("ln_b", l), j), scale=col(("ln_g", l), j)).then_inc(*c.event("affine", l, j))

            steps = dict(split_ahead=split_ahead, silu=silu, norm_squares=norm_squares, norm=norm, ada_take=ada_take, ln_centre=ln_centre,
                         ln_affine=ln_affine, split=split, panel=panel, s5_sines=s5_sines, s5_turn=s5_turn, bu=bu, s5_y=s5_y, s5_inner=s5_inner,
                         stick_scores=stick_scores, stick_weights=stick_weights, stick_out=stick_out,
                         rope_tables=rope_tables, prescale=prescale, latent_sums=latent_sums,
                         latent_norm=latent_norm, scores=scores, turn=turn, ln_a_var=ln_a_var,
                         ln_a_out=ln_a_out, ln=ln)
            for kind, a, b in ORDER:
                if kind in steps:
                    steps[kind](a, b)

        @block.vector
        def _(dve):
            c = Count("dve")

            def tt(out_, a, b, op):
                dve.wait_ge(*c.last)
                return dve.tensor_tensor(out_, a, b, op)

            def ts(out_, a, s1, s2, op0, op1=ALU.bypass):
                dve.wait_ge(*c.last)
                return dve.tensor_scalar(out_, a, s1, s2, op0, op1)

            def stt(out_, a, s, b, op0, op1):
                dve.wait_ge(*c.last)
                return dve.scalar_tensor_tensor(out=out_, in0=a, scalar=s, in1=b, op0=op0, op1=op1)

            def copy(out_, a):
                dve.wait_ge(*c.last)
                return dve.tensor_copy(out_, a)

            def take(g, out_, a, b, op):
                dve.wait_ge(sem("groups"), g + 1)
                dve.wait_ge(*c.last)
                dve.tensor_tensor(out_, a, b, op).then_inc(*c.bank_free(g))

            def split(key, _):
                if key not in FUSED:
                    for j in range(len(OPERANDS[key]["pieces"])):
                        low(key, j)

            def low(key, j):
                o = OPERANDS[key]
                a, b = o["pieces"][j]
                dve.wait_ge(sem("hi"), over("hi", key, j))
                tt(o["lo"][:, a:b, :], o["src"][:, a:b, :], o["hi"][:, a:b, :].bitcast(F32),
                   ALU.subtract).then_inc(*c.event("lo", key, j))

            def invert(key, which=0):
                dve.wait_ge(sem("root"), over("root", key))
                dve.wait_ge(*c.last)
                dve.reciprocal(rstd[:, which, :], root[:, which, :]).then_inc(*c.event("rstd", key))

            def norm(k, _):
                invert(("norm", k))
                name = ("norm_mix", "norm_mlp", "norm_final")[k]
                if k == 0:
                    dve.wait_ge(sem("par_landed"), 16)
                key = ("u0", "u2", None)[k]
                before = c.last
                for j in range(KT):
                    dve.wait_ge(*before)
                    dst = tmp[:, j, :] if k < 2 else h[:, j, :]
                    ins = dve.scalar_tensor_tensor(out=dst, in0=h[:, j, :], scalar=col(name, j), in1=rstd[:, 0, :],
                                                   op0=ALU.mult, op1=ALU.mult)
                    ins.then_inc(*(c.event("h_rows", j) if k == 2 else c.event("rows", key, j // 2) if j % 2 else c.step()))
                    if k < 2 and j % 2 and j >= 3:
                        low(key, j // 2 - 1)
                if k < 2:
                    low(key, 3)

            S = lambda k: small[:, k, :]

            def s5_angle(_, __):
                dve.wait_ge(sem("par_landed"), 16)

                def exp_parts(x, f, two_n, p, n):
                    ts(f, x, -87.0, 88.0, ALU.max, ALU.min).then_inc(*c.step())
                    ts(n, f, 1.0 / math.log(2.0), ROUND, ALU.mult, ALU.add).then_inc(*c.step())
                    ts(n, n, -ROUND, None, ALU.add).then_inc(*c.step())
                    stt(f, n, -LN2_HI, f, ALU.mult, ALU.add).then_inc(*c.step())
                    stt(f, n, -LN2_LO, f, ALU.mult, ALU.add).then_inc(*c.step())
                    ts(n.bitcast(I32), n, 127.0, None, ALU.add).then_inc(*c.step())
                    ts(two_n.bitcast(I32), n.bitcast(I32), 23, None, ALU.logical_shift_left).then_inc(*c.step())
                    ts(p, f, 1.0 / math.factorial(8), None, ALU.mult).then_inc(*c.step())
                    for k in range(7, 0, -1):
                        stt(p, p, 1.0 / math.factorial(k), f, ALU.add, ALU.mult).then_inc(*c.step())

                f, two_n, p, n = S(0), S(1), S(2), S(3)
                exp_parts(col("log_dt", 0, 16), f, two_n, p, n)
                dt = S(4)
                stt(dt, p, 1.0, two_n, ALU.add, ALU.mult).then_inc(*c.step())
                tt(S(5), col("A_re", 0, 16), dt, ALU.mult).then_inc(*c.step())
                exp_parts(S(5), f, two_n, p, n)
                tt(S(6), p, two_n, ALU.mult).then_inc(*c.step())
                stt(S(6), two_n, -1.0, S(6), ALU.add, ALU.add).then_inc(*c.step())
                tt(S(7), col("A_im", 0, 16), dt, ALU.mult).then_inc(*c.step())
                turns(S(7), S(18), S(8))
                ts(S(19), S(18), 0.5, None, ALU.mult).then_inc(*c.event("angle"))

            def s5_prep(_, __):
                dve.wait_ge(sem("s5_landed"), 32)
                dve.wait_ge(sem("sines"), over("sines"))
                sin, half_sin = S(20), S(21)
                cm1 = S(9)
                stt(cm1, half_sin, -2.0, half_sin, ALU.mult, ALU.mult).then_inc(*c.step())
                nre, nim = S(10), S(11)
                stt(nre, cm1, 1.0, S(6), ALU.add, ALU.mult).then_inc(*c.step())
                tt(nre, nre, cm1, ALU.add).then_inc(*c.step())
                stt(nim, S(6), 1.0, sin, ALU.add, ALU.mult).then_inc(*c.step())
                ts(power[:, 0, 0, :], nre, 1.0, None, ALU.add).then_inc(*c.step())
                copy(power[:, 0, 1, :], nim).then_inc(*c.step())
                ts(power[:, 0, 2, :], nim, -1.0, None, ALU.mult).then_inc(*c.step())
                for k in range(1, 8):
                    re, im, nm = (power[:, k - 1, i, :] for i in range(3))
                    tt(S(12), im, nm, ALU.mult).then_inc(*c.step())
                    tt(S(13), re, re, ALU.mult).then_inc(*c.step())
                    tt(power[:, k, 0, :], S(13), S(12), ALU.add).then_inc(*c.step())
                    stt(power[:, k, 1, :], re, 2.0, im, ALU.mult, ALU.mult).then_inc(*c.step())
                    ts(power[:, k, 2, :], power[:, k, 1, :], -1.0, None, ALU.mult).then_inc(*c.step())
                are, aim = col("A_re", 0, 16), col("A_im", 0, 16)
                tt(S(12), are, are, ALU.mult).then_inc(*c.step())
                tt(S(13), aim, aim, ALU.mult).then_inc(*c.step())
                tt(S(12), S(12), S(13), ALU.add).then_inc(*c.step())
                dve.wait_ge(*c.last)
                dve.reciprocal(S(14), S(12)).then_inc(*c.step())
                tt(S(12), nre, are, ALU.mult).then_inc(*c.step())
                tt(S(13), nim, aim, ALU.mult).then_inc(*c.step())
                tt(S(12), S(12), S(13), ALU.add).then_inc(*c.step())
                tt(S(15), S(12), S(14), ALU.mult).then_inc(*c.step())
                tt(S(12), nim, are, ALU.mult).then_inc(*c.step())
                tt(S(13), nre, aim, ALU.mult).then_inc(*c.step())
                tt(S(12), S(12), S(13), ALU.subtract).then_inc(*c.step())
                tt(S(16), S(12), S(14), ALU.mult).then_inc(*c.step())
                dve.wait_ge(*c.last)
                dve.memset(bd, 0.0).then_inc(*c.step())
                wide = [P, 16, 16]
                fre = S(15).unsqueeze(2).broadcast_to(wide)
                fim = S(16).unsqueeze(2).broadcast_to(wide)
                bre, bim = (bst[:, i, :].rearrange("p (r c) -> p r c", r=16) for i in range(2))
                bt3 = btmp.rearrange("p (r c) -> p r c", r=16)
                bt4 = rows5[:, 4 * T:5 * T].rearrange("p (r c) -> p r c", r=16)
                for comp, (x, y, op) in enumerate(((bre, bim, ALU.subtract), (bim, bre, ALU.add))):
                    tt(bt3, fre, x, ALU.mult).then_inc(*c.step())
                    tt(bt4, fim, y, ALU.mult).then_inc(*c.step())
                    for g2 in range(2):
                        rows = slice(64 * g2, 64 * g2 + 64)
                        dst = bd[rows, comp, :].rearrange("p (r g c) -> p r g c", r=16, g=2)[:, :, g2, :]
                        tt(dst, bt3[rows], bt4[rows], op).then_inc(*c.event("b_diag", comp, g2))
                ts(ct[:, 1, :, :], ct[:, 1, :, :], -1.0, None, ALU.mult).then_inc(*c.event("ct"))
            def turns(angle, dst, k):
                ts(k, angle, 1.0 / (2 * math.pi), ROUND, ALU.mult, ALU.add).then_inc(*c.step())
                ts(k, k, -ROUND, None, ALU.add).then_inc(*c.step())
                stt(dst, k, -TWO_PI[0], angle, ALU.mult, ALU.add).then_inc(*c.step())
                stt(dst, k, -TWO_PI[1], dst, ALU.mult, ALU.add).then_inc(*c.step())
                stt(dst, k, -TWO_PI[2], dst, ALU.mult, ALU.add).then_inc(*c.step())
                ts(dst, dst, -PI_IN, PI_IN, ALU.max, ALU.min).then_inc(*c.step())

            def sweep_step(f, k, here, past, last_):
                for r in range(FOUR * f, FOUR * f + FOUR):
                    x = states[r % len(states)]
                    dve.wait_ge(*pair_done[r])
                    dve.scalar_tensor_tensor(out=x[:, :, here], in0=x[:, :, past], scalar=power[:, k, 0, r:r + 1],
                                             in1=x[:, :, here], op0=ALU.mult, op1=ALU.add).then_inc(*c.step())
                    pair_done[r] = c.last
                for r in range(FOUR * f, FOUR * f + FOUR):
                    x = states[r % len(states)]
                    dve.wait_ge(*pair_done[r])
                    dve.scalar_tensor_tensor(out=x[:, 0, here], in0=x[:, 1, past], scalar=power[:, k, 2, r:r + 1],
                                             in1=x[:, 0, here], op0=ALU.mult, op1=ALU.add).then_inc(*c.step())
                    dve.wait_ge(*pair_done[r])
                    dve.scalar_tensor_tensor(out=x[:, 1, here], in0=x[:, 0, past], scalar=power[:, k, 1, r:r + 1],
                                             in1=x[:, 1, here], op0=ALU.mult, op1=ALU.add).then_inc(*(c.event("scan", r) if last_ else c.step()))
                    pair_done[r] = c.last

            pair_done = {}

            def scan_up(f, _):
                for r in range(FOUR * f, FOUR * f + FOUR):
                    pair_done[r] = (sem("bu_sb"), over("bu_sb", r))
                for k in range(LEVELS):
                    d = 1 << k
                    sweep_step(f, k, slice(2 * d - 1, T, 2 * d), slice(d - 1, T, 2 * d), False)

            def scan_down(f, _):
                for k in range(LEVELS - 2, -1, -1):
                    d = 1 << k
                    sweep_step(f, k, slice(3 * d - 1, T, 2 * d), slice(2 * d - 1, T - d, 2 * d), k == 0)

            def s5_y(f, _):
                dve.wait_ge(sem("cx"), over("cx", LAST_PAIR[f]))
                stt(yv[:, f, :], ussm[:, f, :], col("D_skip", f),
                    p_y[:, T * (f % 2):T * (f % 2) + T], ALU.mult, ALU.add).then_inc(*c.event("y_rows", f))

            def s5_inner(f, _):
                dve.wait_ge(sem("y_sq"), over("y_sq", f))
                ts(y1, y1, 0.044715, 1.0, ALU.mult, ALU.add).then_inc(*c.step())
                tt(y1, y1, yv[:, f, :], ALU.mult).then_inc(*c.event("y_inner", f))

            def s5_gelu(f, _):
                dve.wait_ge(sem("y_sig"), over("y_sig", f))
                tt(yv[:, f, :], yv[:, f, :], y1, ALU.mult).then_inc(*(c.event("rows", "y", 0) if f == WT - 1 else c.step()))

            def stick_soft(hd, _):
                dve.wait_ge(sem("log1p"), over("log1p", hd))
                stt(stick[1], p_z[:, 0:384], 0.0, stick[0], ALU.max, ALU.add).then_inc(*c.step())
                tt(stick[1], stick[1], mask1[:, :], ALU.mult).then_inc(*c.event("soft", hd))

            def stick_weights(hd, _):
                dve.wait_ge(sem("fails"), over("fails", hd))
                if hd >= 2:
                    dve.wait_ge(sem("o_stick"), over("o_stick", hd - 2))
                stt(stick[2 + hd % 2], p_c[:, 0:384], 0.0, neg1[:, :], ALU.min, ALU.add).then_inc(*c.event("logw", hd))

            def ada_end(part, _):
                first, end = ADA_PARTS[part]
                dve.wait_ge(sem("ada_turned"), over("ada_turned", end - 1))
                for l in range(LAYERS):
                    a, b = max(2 * first, 24 * l), min(2 * end, 24 * l + 24)
                    if a < b:
                        ps = p_s if part == 0 else p_c
                        tt(ada[:, l, a - 24 * l:b - 24 * l], ps[:, a:b], col(("b_ada", l), a - 24 * l, b - a),
                           ALU.add).then_inc(*(c.event("ada", part) if b == 2 * end else c.step()))

            def silu(_, __):
                dve.wait_ge(sem("c_sig"), over("c_sig"))
                tt(silu_c[:, :], silu_c[:, :], col("c", 0, KT), ALU.mult).then_inc(*c.event("silu_c"))

            def glu_mul(_, __):
                for s, v in emptied(groups_of("glu")):
                    dve.wait_ge(s, v)
                tt(yv, yv, yt, ALU.mult).then_inc(*c.event("rows", "yg", 0))

            def panel(p, _):
                q = PANELS[p]
                job, l, n, g = q["job"], q["layer"], q["n"], q["g"]
                both = pair(pg[g % 2][:, :])
                gt = pair(gtmp[:, q["gt"] % 2, :]) if q["gt"] is not None else None
                if job in ("up_attn", "up_ssm"):
                    for i in range(2):
                        a = 4 * n + 2 * i
                        b = pair(pg[(g + i) % 2][:, :])
                        if job == "up_attn":
                            take(g + i, merged[:, a:a + 2, :], b, gates[:, KT + a:KT + a + 2, :], ALU.mult)
                        else:
                            take(g + i, tmp[:, 0:2, :], b, gates[:, a:a + 2, :], ALU.mult)
                            tt(merged[:, a:a + 2, :], merged[:, a:a + 2, :], tmp[:, 0:2, :],
                               ALU.add).then_inc(*c.event("rows", "u1", a // 2))
                elif job == "out":
                    take(g, h[:, 2 * n:2 * n + 2, :], both, h[:, 2 * n:2 * n + 2, :], ALU.add)
                elif job == "ff2":
                    for i in range(2):
                        a = 4 * (n % 2) + 2 * i
                        take(g + i, h[:, a:a + 2, :], pair(pg[(g + i) % 2][:, :]), h[:, a:a + 2, :], ALU.add)
                elif job == "ff1":
                    f, ch = 4 * (n % 2), n // 2
                    dve.wait_ge(sem("groups"), g + 1)
                    dve.wait_ge(*c.last)
                    dve.tensor_scalar(tmp[:, f:f + 2, :], both, 0.0, None, ALU.max).then_inc(*c.bank_free(g))
                    dve.wait_ge(sem("ff_hi"), over("ff_hi", n))
                    half = slice(2 * (n % 2), 2 * (n % 2) + 2)
                    tt(v_lo[(ch + 1) % 2][:, half, :], tmp[:, f + 2:f + 4, :],
                       v_hi[(ch + 1) % 2][:, half, :].bitcast(F32), ALU.subtract).then_inc(*c.event("ff_lo", n))
                elif job == "a1":
                    for s, v in emptied(groups_of("a2", l)):
                        dve.wait_ge(s, v)
                    take(g, apad[:, 2 * n:2 * n + 2, CONV_A - 1:], both, acc[:, 2 * n:2 * n + 2, :], ALU.mult)
                elif job == "gc":
                    for s, v in emptied(groups_of("xb", l)):
                        dve.wait_ge(s, v)
                    take(g, bpad[:, 2 * n:2 * n + 2, CONV_B - 1:], both, xbv[:, 2 * n:2 * n + 2, :], ALU.mult)
                elif job == "gb":
                    take(g, bconv[:, 2 * n:2 * n + 2, :], both, bconv[:, 2 * n:2 * n + 2, :], ALU.mult)
                elif job in ("cg", "ag", "bg"):
                    dve.wait_ge(sem("sigmoid"), over("sigmoid", q["gt"]))
                    dst = {"cg": cgate, "ag": agate}[job][:, 2 * n:2 * n + 2, :] if job != "bg" else gt
                    take(g, dst, both, gt, ALU.mult)
                    if job == "bg":
                        tt(bconv[:, 2 * n:2 * n + 2, :], bconv[:, 2 * n:2 * n + 2, :], gt, ALU.mult).then_inc(*c.event("gt_used", q["gt"]))
                elif job in ("merge0", "merge1", "merge2"):
                    for s, v in emptied([g, find("branch%s" % job[-1], l, n // 2)["g"] + n % 2]):
                        dve.wait_ge(s, v)
                    a = slice(2 * n, 2 * n + 2)
                    if job == "merge1":
                        tt(mer[:, a, :], gt, ybr[:, a, :], ALU.mult).then_inc(*c.event("gt_used", q["gt"]))
                    else:
                        tt(gt, gt, ybr[:, a, :], ALU.mult).then_inc(*c.step())
                        tt(mer[:, a, :], mer[:, a, :], gt, ALU.add).then_inc(*c.event("gt_used", q["gt"]))
                elif job == "w_o":
                    dve.wait_ge(sem("groups"), g + 1)
                    dve.wait_ge(sem("alpha_h"), over("alpha_h", l))
                    stt(h[:, 2 * n, :], both[:, 0, :], ada[:, l, 16 + 2 * n:17 + 2 * n], h[:, 2 * n, :],
                        ALU.mult, ALU.add).then_inc(*c.step())
                    dve.wait_ge(*c.last)
                    dve.scalar_tensor_tensor(
                        out=h[:, 2 * n + 1, :], in0=both[:, 1, :], scalar=ada[:, l, 17 + 2 * n:18 + 2 * n],
                        in1=h[:, 2 * n + 1, :], op0=ALU.mult, op1=ALU.add).then_inc(*c.bank_free(g))

            def rope_tables(_, __):
                for pad in (apad[:, :, 0:CONV_A - 1], bpad[:, :, 0:CONV_B - 1]):
                    dve.wait_ge(*c.last)
                    dve.memset(pad, 0.0).then_inc(*c.step())
                rows = slice(NOPE, QK)
                dve.wait_ge(sem("pos_landed"), 16)
                copy(nmean[rows], pos[rows, :]).then_inc(*c.step())
                ts(nmean[rows], nmean[rows], col("inv_freq")[rows], None, ALU.mult).then_inc(*c.step())
                turns(nmean[rows], rsin[rows], rcos[rows])
                ts(rcos[rows], rsin[rows], 0.5, None, ALU.mult).then_inc(*c.event("rope_angle"))
                dve.wait_ge(sem("rope_sines"), over("rope_sines"))
                stt(rcos[rows], rcos[rows], -2.0, rcos[rows], ALU.mult, ALU.mult).then_inc(*c.step())
                ts(rcos[rows], rcos[rows], 1.0, None, ALU.add).then_inc(*c.step())

            def modulate(l, _):
                if l == 0:
                    copy(shift1[:, :], ada[:, 0, 0:8]).then_inc(*c.step())
                    ts(scale1[:, :], ada[:, 0, 8:16], 1.0, None, ALU.add).then_inc(*c.event("scale1", 0))
                before = c.last
                for j in range(KT):
                    dve.wait_ge(*before)
                    dve.tensor_scalar(tmp[:, j, :], h[:, j, :], scale1[:, j:j + 1], shift1[:, j:j + 1], ALU.mult,
                                      ALU.add).then_inc(*(c.event("rows", ("u", l), j // 2) if j % 2 else c.step()))
                    if j % 2 and j >= 3:
                        low(("u", l), j // 2 - 1)
                low(("u", l), 3)

            def modulate_columns(l, _):
                gain, bias = col(("ln_g", l - 1), 0, KT), col(("ln_b", l - 1), 0, KT)
                ts(scale1[:, :], ada[:, l, 8:16], 1.0, None, ALU.add).then_inc(*c.step())
                tt(shift1[:, :], bias, scale1[:, :], ALU.mult).then_inc(*c.step())
                tt(shift1[:, :], shift1[:, :], ada[:, l, 0:8], ALU.add).then_inc(*c.step())
                tt(scale1[:, :], scale1[:, :], gain, ALU.mult).then_inc(*c.step())
                ts(rest_g[:, :], gain, ALPHA, None, ALU.mult).then_inc(*c.step())
                ts(rest_b[:, :], bias, ALPHA, None, ALU.mult).then_inc(*c.event("scale1", l))

            def latent_norm(l, _):
                for key, which, x, n, name in ((("lat_q", l), 0, q_lat, 3, "q_norm_g"),
                                               (("lat_kv", l), 1, kv_lat, 2, "kv_norm_g")):
                    invert(key, which)
                    for j in range(n):
                        stt(x[:, j, :],
                            x[:, j, :], col((name, l), j), rstd[:, which, :], ALU.mult, ALU.mult).then_inc(*(c.event("rows", ("ql" if which == 0 else "kvl", l), 0) if j == n - 1 else c.step()))

            def rope(l, _):
                rows = slice(NOPE, QK)
                wide = [ROPE, 2, T]
                sin2, cos2 = spread(rsin[rows], *wide), spread(rcos[rows], *wide)
                dve.wait_ge(sem("rotated"), over("rotated", l, 0))
                tt(kpr[rows, :], p_y[rows, 0:T], rsin[rows], ALU.mult).then_inc(*c.step())
                tt(kpe[rows, :], kpe[rows, :], rcos[rows], ALU.mult).then_inc(*c.step())
                tt(kpe[rows, :], kpe[rows, :], kpr[rows, :], ALU.add).then_inc(*c.step())
                copy(kf[rows, :, :], spread(kpe[rows, :], ROPE, HEADS, T)).then_inc(*c.step())
                for i in range(4):
                    b = (p_bu, p_z, p_c, p_o)[i]
                    a = slice(2 * i, 2 * i + 2)
                    dve.wait_ge(sem("rotated"), over("rotated", l, 1 + i))
                    tt(rtmp[rows, :, :], pair(b[rows, :]), sin2, ALU.mult).then_inc(*c.step())
                    tt(qf[rows, a, :], qf[rows, a, :], cos2, ALU.mult).then_inc(*c.step())
                    tt(qf[rows, a, :], qf[rows, a, :], rtmp[rows, :, :], ALU.add).then_inc(*(c.event("roped", l) if i == 3 else c.step()))

            def conv_a(l, part):
                tiles = (2 * (part // CONV_PARTS), 2 * (part // CONV_PARTS) + 1)
                first = CONV_STEP * (part % CONV_PARTS)
                done = {j: c.last for j in tiles}
                for k in range(first, min(first + CONV_STEP, CONV_A)):
                    for j in tiles:
                        w = col(("conv_a_w", l), 4 * k + j)
                        dve.wait_ge(*done[j])
                        if k == 0:
                            ins = dve.tensor_scalar(acc[:, j, :], apad[:, j, 0:T], w, col(("conv_a_b", l), j), ALU.mult, ALU.add)
                        else:
                            ins = dve.scalar_tensor_tensor(out=acc[:, j, :], in0=apad[:, j, k:k + T], scalar=w,
                                                           in1=acc[:, j, :], op0=ALU.mult, op1=ALU.add)
                        ins.then_inc(*(c.event("conv_a", l, j) if k == CONV_A - 1 else c.step()))
                        done[j] = c.last

            def conv_b(l, _):
                for j in range(WT):
                    w = lambda k: col(("conv_b_w", l), 4 * k + j)
                    ts(bconv[:, j, :], bpad[:, j, 0:T], w(0), None, ALU.mult).then_inc(*c.step())
                    for k in range(1, CONV_B):
                        stt(bconv[:, j, :], bpad[:, j, k:k + T], w(k), bconv[:, j, :], ALU.mult, ALU.add).then_inc(*c.step())

            def scores(l, hd):
                b = hd % 2
                dve.wait_ge(sem("scores"), over("scores", l, hd))
                if hd >= 2 or l:
                    dve.wait_ge(sem("turned"), over("turned", l if hd >= 2 else l - 1, (hd - 2) % HEADS))
                tt(soft[:, b, :], p_z[:, 0:384], mask2[:, :], ALU.add).then_inc(*c.step())
                for i, (lo, hi) in enumerate(((0, P), (P, 3 * P))):
                    dve.wait_ge(*c.last)
                    dve.tensor_reduce(mx[:, b, i:i + 1], soft[:, b, lo:hi], AX.X, ALU.max).then_inc(*c.step())
                ts(nmax[:, b, :], mx[:, b, :], -SCALE2, None, ALU.mult).then_inc(*c.event("nmax", l, hd))

            def normalise(l, hd):
                b = hd % 2
                dve.wait_ge(sem("probs"), over("probs", l, hd, 1))
                dve.wait_ge(*c.last)
                dve.reciprocal(rsum[:, b, :], sums[:, b, :]).then_inc(*c.step())
                ts(soft[:, b, 0:P], soft[:, b, 0:P], rsum[:, b, 0:1], None, ALU.mult).then_inc(*c.step())
                ts(soft[:, b, P:3 * P], soft[:, b, P:3 * P], rsum[:, b, 1:2], None, ALU.mult).then_inc(*c.event("probs_n", l, hd))

            def context(l, hd):
                if hd % 2:
                    i = hd // 2
                    dve.wait_ge(sem("o2"), over("o2", l, hd))
                    tt(cgate[:, i, :],
                       p_o[:, T * (i % 2):T * (i % 2) + T], cgate[:, i, :], ALU.mult).then_inc(*(c.event("rows", ("c", l), 0) if i == 3 else c.event("ctx_read", l, i)))

            def mean(key, n):
                dve.wait_ge(sem("stats"), over("stats", key))
                ts(nmean, p_s[:, 0:T], -1.0 / n, None, ALU.mult).then_inc(*c.event("nmean", key))

            def ln_a_mean(l, _):
                mean(("mean_a", l), W)
                tt(acc, acc, spread(nmean, P, WT, T), ALU.add).then_inc(*c.event("centred_a", l))

            def ln_a_var(l, _):
                invert(("var_a", l))
                tt(acc, acc, spread(rstd[:, 0, :], P, WT, T), ALU.mult).then_inc(*c.step())
                for j in range(WT):
                    ts(acc[:, j, :], acc[:, j, :], col(("ln_a_g", l), j), col(("ln_a_b", l), j),
                       ALU.mult, ALU.add).then_inc(*c.event("a_affine", l, j))

            def ln_a_out(l, _):
                dve.wait_ge(sem("a_sig"), over("a_sig", l, WT - 1))
                tt(acc, acc, tmp[:, 0:4, :], ALU.mult).then_inc(*c.step())
                tt(acc, acc, agate, ALU.mult).then_inc(*c.event("rows", ("a", l), 0))

            def ln_centre(l, _):
                mean(("mean", l), D)
                before = c.last
                for j in range(4):
                    dve.wait_ge(*before)
                    dve.tensor_tensor(h[:, 2 * j:2 * j + 2, :], h[:, 2 * j:2 * j + 2, :], spread(nmean, P, 2, T),
                                      ALU.add).then_inc(*c.event("centred", l, j))

            def ln(l, _):
                invert(("var", l))
                before = c.last
                for j in range(4):
                    dve.wait_ge(*before)
                    dve.tensor_tensor(h[:, 2 * j:2 * j + 2, :], h[:, 2 * j:2 * j + 2, :], spread(rstd[:, 0, :], P, 2, T),
                                      ALU.mult).then_inc(*c.event("ln_rows", l, j))

            dve.wait_ge(sem("const"), over("const", "all"))
            steps = dict(silu=silu, norm=norm, split=split, panel=panel, s5_angle=s5_angle, s5_prep=s5_prep, scan_up=scan_up, scan_down=scan_down, s5_y=s5_y,
                         s5_inner=s5_inner, s5_gelu=s5_gelu,
                         stick_soft=stick_soft, stick_weights=stick_weights,
                         ada_end=ada_end, glu_mul=glu_mul, rope_tables=rope_tables, modulate=modulate, modulate_columns=modulate_columns,
                         latent_norm=latent_norm, rope=rope, conv_a=conv_a, conv_b=conv_b, scores=scores,
                         normalise=normalise, context=context, ln_a_mean=ln_a_mean, ln_a_var=ln_a_var,
                         ln_a_out=ln_a_out, ln_centre=ln_centre, ln=ln)
            for kind, a, b in ORDER:
                if kind in steps:
                    steps[kind](a, b)

        @block.tensor
        def _(pe):
            def sum_tiles(key, src, tiles, region):
                if SUMS.index(key):
                    pe.wait_ge(*sums_before(key))
                for j in range(tiles):
                    ins = pe.matmul(p_s[:, region * T:region * T + T], ones[:, :], src[:, j, :], start=j == 0,
                                    stop=j == tiles - 1)
                return ins

            def three(dst, w_h, w_l, x_h, x_l, first, last_):
                pe.matmul(dst, w_h, x_h, start=first, stop=False)
                pe.matmul(dst, w_h, x_l, start=False, stop=False)
                return pe.matmul(dst, w_l, x_h, start=False, stop=last_)

            def group_start(g):
                if g >= 2:
                    for s, v in emptied([g - 2]):
                        pe.wait_ge(s, v)

            begun = set()

            def blocks(q, g, widths, x_hi, x_lo, waits):
                wh, wl = slot(w_hi, q), slot(w_lo, q)
                group_start(g)
                for i, (a, m) in enumerate(widths):
                    for k in range(q["kt"]):
                        if i == 0 and k in waits:
                            pe.wait_ge(*waits[k])
                        ins = three(pg[g % 2][0:m, i * T:i * T + T], wh[:, k, a:a + m], wl[:, k, a:a + m],
                                    x_hi[:, k, :], x_lo[:, k, :], k == 0, k == q["kt"] - 1)
                ins.then_inc(sem("groups"), 1)

            def panel(p, _):
                q = PANELS[p]
                job, l, n, g = q["job"], q["layer"], q["n"], q["g"]
                if job == "ada":
                    pe.wait_ge(*landed(q))
                    pe.wait_ge(sem("silu_c"), over("silu_c"))
                    group_start(g)
                    w = slot(raw, q)
                    for k in range(KT):
                        ins = pe.matmul(pg[g % 2][0:1, 0:256], silu_c[:, k:k + 1], w[:, k, :], start=k == 0, stop=k == KT - 1)
                    ins.then_inc(sem("groups"), 1)
                    return
                pe.wait_ge(*slot_free(q))
                waits = {}
                if job == "ff2":
                    ch = n // 2
                    pe.wait_ge(sem("ff_lo"), over("ff_lo", 2 * ch + 1))
                    xh, xl = v_hi[(ch + 1) % 2], v_lo[(ch + 1) % 2]
                else:
                    key = operand_of(q)
                    o = OPERANDS[key]
                    waits = {a: (sem("lo"), over("lo", key, j)) for j, (a, b) in enumerate(o["pieces"])} if key not in begun else {}
                    begun.add(key)
                    xh, xl = o["hi"], o["lo"]
                if job == "v":
                    wh, wl = slot(w_hi, q), slot(w_lo, q)
                    group_start(g)
                    for tt in range(2):
                        for k in range(KT):
                            tok = slice(P * tt, P * tt + P)
                            dst = pg[g % 2][:, T * tt:T * tt + T]
                            pe.matmul(dst, xh[:, k, tok], wh[:, k, :], start=k == 0, stop=False)
                            pe.matmul(dst, xh[:, k, tok], wl[:, k, :], start=False, stop=False)
                            ins = pe.matmul(dst, xl[:, k, tok], wh[:, k, :], start=False, stop=k == KT - 1)
                    ins.then_inc(sem("groups"), 1)
                elif job == "uq":
                    for i in range(2):
                        blocks(q, g + i, [(QK * (2 * i + j), QK) for j in range(2)], xh, xl, waits if i == 0 else {})
                elif job == "ukv":
                    for i in range(4):
                        blocks(q, g + i, [(P * (2 * i + j), P) for j in range(2)], xh, xl, waits if i == 0 else {})
                    wh, wl = (slot(x, q).rearrange("p k (h m) -> p k h m", h=HEADS)[:, :, :, NOPE:P] for x in (w_hi, w_lo))
                    for tt in range(2):
                        group_start(g + 4 + tt)
                        dst = pg[(g + tt) % 2][:, :].rearrange("p (h m) -> p h m", h=HEADS)
                        tok = slice(P * tt, P * tt + P)
                        for k in range(q["kt"]):
                            pe.matmul(dst, xh[:, k, tok], wh[:, k], start=k == 0, stop=False)
                            pe.matmul(dst, xh[:, k, tok], wl[:, k], start=False, stop=False)
                            ins = pe.matmul(dst, xl[:, k, tok], wh[:, k], start=False, stop=k == q["kt"] - 1)
                        ins.then_inc(sem("groups"), 1)
                else:
                    for i in range(q["groups"]):
                        left = min(256, q["cols"] - 256 * i)
                        blocks(q, g + i, [(256 * i + P * j, min(P, left - P * j)) for j in range((left + P - 1) // P)],
                               xh, xl, waits if i == 0 else {})

            def sum_piece(key, src, j, region):
                if j == 0 and SUMS.index(key):
                    pe.wait_ge(*sums_before(key))
                for i in (2 * j, 2 * j + 1):
                    ins = pe.matmul(p_s[:, region * T:region * T + T], ones[:, :], src[:, i, :], start=i == 0, stop=i == KT - 1)
                if j == 3:
                    ins.then_inc(*event("stats", key))

            def norm_sums(k, j):
                pe.wait_ge(sem("squares"), over("squares", ("norm", k), j))
                sum_piece(("norm", k), tmp, j, 0)

            def ada_turn(i, _):
                q = find("ada", i // 12, i % 12)
                part = next(k for k, (a, b) in enumerate(ADA_PARTS) if i < b)
                ps = p_s if part == 0 else p_c
                if i == 0:
                    pe.wait_ge(*sums_before(("ada", 0)))
                elif i == ADA_PARTS[1][0]:
                    pe.wait_ge(sem("logw"), over("logw", HEADS - 1))
                elif part > 1 and i == ADA_PARTS[part][0]:
                    pe.wait_ge(sem("ada"), over("ada", part - 1))
                    if part == 3:
                        pe.wait_ge(sem("probs_t"), over("probs_t", 0, HEADS - 1))
                for s, v in emptied([q["g"]]):
                    pe.wait_ge(s, v)
                for j in range(2):
                    at = 2 * i + j
                    ins = pe.matmul(ps[:, at:at + 1], root[0:1, 1, P * j:P * j + P], ones[0:1, 0:1], start=True, stop=True)
                    ins.then_inc(*((sem(f"raw_free{q['index'] % RAW}"), 1) if j == 0 else event("ada_turned", i)))

            def s5_turn(_, __):
                pe.wait_ge(sem("const"), over("const", "all"))
                pe.wait_ge(sem("b_diag"), over("b_diag", 1, 1))
                for comp, b in enumerate((p_bu, p_z)):
                    for f in range(4):
                        ins = pe.transpose(b[:, P * f:P * f + P], bd[:, comp, P * f:P * f + P], ident[:, :])
                ins.then_inc(*event("bt_ps"))

            def bu(r, _):
                pe.wait_ge(sem("bt"), over("bt", 1))
                for s, v in emptied(groups_of("ssm")):
                    pe.wait_ge(s, v)
                if r != BU_ORDER[0]:
                    pe.wait_ge(sem("bu_sb"), over("bu_sb", BU_ORDER[BU_ORDER.index(r) - 1]))
                f, rows = r // 4, slice(32 * (r % 4), 32 * (r % 4) + 32)
                for comp in range(2):
                    ins = pe.matmul(p_bu[:, T * comp:T * comp + T], bt[rows, comp, f, :], ussm[rows, f, :],
                                    start=True, stop=True)
                ins.then_inc(*event("bu", r))

            def s5_out(r, _):
                pe.wait_ge(sem("scan"), over("scan", r))
                pe.wait_ge(sem("ct"), over("ct"))
                f, rows = r // 4, slice(32 * (r % 4), 32 * (r % 4) + 32)
                if f:
                    pe.wait_ge(sem("y_rows"), over("y_rows", f - 1))
                x = states[r % len(states)]
                for comp in range(2):
                    ins = pe.matmul(p_y[rows, T * (f % 2):T * (f % 2) + T], ct[:, comp, f, rows], x[:, comp, :],
                                    start=comp == 0, stop=comp == 1)
                ins.then_inc(*event("cx", r))

            def qk(dst, hd, stop):
                rows, f = slice(64 * (hd % 2), 64 * (hd % 2) + 64), hd // 2
                pe.matmul(dst[:, 0:T], k1[rows, f, 0:P], q1[rows, f, :], start=True, stop=stop)

            def qk_rest(dst, hd, stop):
                rows, f = slice(64 * (hd % 2), 64 * (hd % 2) + 64), hd // 2
                return pe.matmul(dst[:, T:T + P], k1[rows, f, P:T], q1[rows, f, P:T], start=True, stop=stop)

            def stick_scores(hd, _):
                for s, v in emptied(groups_of("q") + groups_of("k")):
                    pe.wait_ge(s, v)
                pe.wait_ge(sem("bt"), over("bt", 1))
                if hd:
                    pe.wait_ge(sem("soft"), over("soft", hd - 1))
                qk(p_z, hd, True)
                qk_rest(p_z, hd, True).then_inc(*event("z", hd))

            def stick_fails(hd, _):
                pe.wait_ge(sem("soft"), over("soft", hd))
                if hd:
                    pe.wait_ge(sem("logw"), over("logw", hd - 1))
                qk(p_c, hd, False)
                pe.matmul(p_c[:, 0:T], ntri[:, :], stick[1][:, 0:T], start=False, stop=False)
                pe.matmul(p_c[:, P:T], nones[:, :], stick[1][:, T:T + P], start=False, stop=True)
                qk_rest(p_c, hd, False)
                pe.matmul(p_c[:, T:T + P], ntri[:, :], stick[1][:, T:T + P], start=False, stop=True).then_inc(*event("fails", hd))

            def weighted_values(values, weights, hd):
                rows, at = slice(64 * (hd % 2), 64 * (hd % 2) + 64), T * (hd // 2 % 2)
                pe.matmul(p_o[rows, at:at + T], values[:, 0, DH * hd:DH * hd + DH], weights[:, 0:T], start=True, stop=False)
                return pe.matmul(p_o[rows, at + P:at + T], values[:, 1, DH * hd:DH * hd + DH], weights[:, T:T + P],
                                 start=False, stop=True)

            def stick_out(hd, _):
                pe.wait_ge(sem("w_stick"), over("w_stick", hd))
                for s, v in emptied(groups_of("v")):
                    pe.wait_ge(s, v)
                if hd >= 2:
                    pe.wait_ge(sem("ctx"), over("ctx", hd // 2 - 1))
                weighted_values(v1, stick[2 + hd % 2], hd).then_inc(*event("o_stick", hd))

            def latent_sums(l, _):
                pe.wait_ge(sem("squares"), over("squares", ("lat", l)))
                sum_tiles(("lat", l), lat_sq[:, 0:3, :], 3, 0)
                sum_tiles(("lat", l), lat_sq[:, 3:5, :], 2, 1).then_inc(*event("stats", ("lat", l)))

            def rope(l, _):
                rows = slice(NOPE, QK)
                for s, v in emptied(groups_of("k_rope", l)):
                    pe.wait_ge(s, v)
                pe.matmul(p_y[rows, 0:T], rot[rows, :], kpe[rows, :], start=True, stop=True).then_inc(*event("rotated", l, 0))
                for s, v in emptied(groups_of("uq", l)):
                    pe.wait_ge(s, v)
                for i in range(4):
                    b = (p_bu, p_z, p_c, p_o)[i]
                    if i == 2:
                        pe.wait_ge(sem("ada"), over("ada", 2 + l))
                    if i == 3:
                        pe.wait_ge(*((sem("rows"), over("rows", ("c", l - 1), 0)) if l else (sem("ctx"), over("ctx", 3))))
                    pe.matmul(b[rows, :], rot[rows, :], qf[rows, 2 * i:2 * i + 2, :], start=True, stop=True).then_inc(*event("rotated", l, 1 + i))

            def scores(l, hd):
                pe.wait_ge(sem("roped"), over("roped", l))
                for s, v in emptied(groups_of("ukv", l)):
                    pe.wait_ge(s, v)
                if hd:
                    pe.wait_ge(sem("nmax"), over("nmax", l, hd - 1))
                pe.matmul(p_z[:, 0:P], qf[0:QK, hd, 0:P], kf[0:QK, hd, 0:P], start=True, stop=True)
                pe.matmul(p_z[:, P:3 * P], qf[0:QK, hd, P:T], kf[0:QK, hd, :], start=True, stop=True).then_inc(*event("scores", l, hd))

            def turn(l, hd):
                pe.wait_ge(sem("probs_n"), over("probs_n", l, hd))
                if hd:
                    pe.wait_ge(sem("probs_t"), over("probs_t", l, hd - 1))
                for i in range(3):
                    ins = pe.transpose(p_c[:, P * i:P * i + P], soft[:, hd % 2, P * i:P * i + P], ident[:, :])
                ins.then_inc(*event("turned", l, hd))

            def context(l, hd):
                pe.wait_ge(sem("probs_t"), over("probs_t", l, hd))
                i = hd // 2
                if i:
                    pe.wait_ge(sem("ctx_read"), over("ctx_read", l, i - 1))
                weighted_values(v2, soft_t[:, hd % 2, :], hd).then_inc(*event("o2", l, hd))

            def ln_a_mean(l, _):
                pe.wait_ge(sem("conv_a"), over("conv_a", l, WT - 1))
                sum_tiles(("mean_a", l), acc, WT, 0).then_inc(*event("stats", ("mean_a", l)))

            def ln_a_var(l, _):
                pe.wait_ge(sem("squares"), over("squares", ("var_a", l)))
                sum_tiles(("var_a", l), tmp[:, 0:4, :], WT, 1).then_inc(*event("stats", ("var_a", l)))

            def ln_mean(l, j):
                for s, v in emptied([groups_of("w_o", l)[j]]):
                    pe.wait_ge(s, v)
                sum_piece(("mean", l), h, j, 0)

            def ln(l, _):
                for j in range(4):
                    pe.wait_ge(sem("squares"), over("squares", ("var", l), j))
                    sum_piece(("var", l), tmp, j, 1)

            pe.wait_ge(sem("const"), over("const", "ones"))
            steps = dict(norm_sums=norm_sums, panel=panel, ada_turn=ada_turn, s5_turn=s5_turn, bu=bu, s5_out=s5_out,
                         stick_scores=stick_scores, stick_fails=stick_fails, stick_out=stick_out,
                         latent_sums=latent_sums, rope=rope, scores=scores, turn=turn, context=context,
                         ln_a_mean=ln_a_mean, ln_a_var=ln_a_var, ln_mean=ln_mean, ln=ln)
            for kind, a, b in ORDER:
                if kind in steps:
                    steps[kind](a, b)


WEIGHTS = ["w_in", "w_glu", "w_up_ssm", "w_up_attn", "w_gate", "w_out", "w_ff1", "w_ff2", "w_ada_2", "w_in_2",
           "w_a_out_2", "w_b_out_2", "w_uq_2", "w_ukv_2", "w_c_out_2", "w_o_2"]


def columns(v):
    return np.asarray(v).reshape(-1, P).T


def lay_out(x):
    a = {n: np.ascontiguousarray(x[n]) for n in WEIGHTS}
    a["x_t"] = np.ascontiguousarray(np.asarray(x["x"])[0].T)
    a["positions"] = np.ascontiguousarray(x["positions_2"])
    par = np.zeros((P, NPAR), np.float32)

    def put(key, block):
        par[:, COL[key]:COL[key] + block.shape[1]] = block

    for n in ("norm_mix", "b_gate", "norm_mlp", "norm_final", "D_skip", "b_glu"):
        put(n, columns(x[n]))
    put("c", columns(x["c_2"]))
    for n in ("A_re", "A_im"):
        put(n, np.asarray(x[n])[0].reshape(PAIRS, 2 * STATE).T)
    put("log_dt", np.repeat(np.asarray(x["log_dt"])[0].reshape(PAIRS, 2), STATE, axis=1).T)
    freq = np.float32(10000.0) ** (-np.arange(0, ROPE, 2, dtype=np.float32) / np.float32(ROPE))
    rows = np.zeros((P, 1), np.float32)
    rows[NOPE:QK, 0] = np.tile(freq, 2)
    put("inv_freq", rows)
    for l in range(LAYERS):
        for n in ("b_ada", "conv_a_b", "ln_a_g", "ln_a_b", "q_norm_g", "kv_norm_g", "ln_g", "ln_b"):
            put((n, l), columns(x[n + "_2"][l]))
        for n in ("conv_a_w", "conv_b_w"):
            put((n, l), columns(x[n + "_2"][l]))
    a["params"] = par
    b = [np.asarray(x[n])[0].reshape(PAIRS, 2 * STATE, CIN).transpose(1, 0, 2).reshape(P, PAIRS * CIN)
         for n in ("B_re", "B_im")]
    a["b_state"] = np.ascontiguousarray(np.stack(b, 1))
    c = np.zeros((2, STATE, 2, PAIRS, 2, CIN), np.float32)
    for i, n in enumerate(("C_re", "C_im")):
        v = np.asarray(x[n])[0].reshape(PAIRS, 2, CIN, STATE)
        for g in range(2):
            c[g, :, i, :, g, :] = v[:, g].transpose(2, 0, 1)
    a["c_state"] = np.ascontiguousarray(c.reshape(P, 2, 4, P))
    return a


def program(nc, arrays):
    t = {n: nc.dram_tensor(f"in_{n}", a.shape, mybir.dt.from_np(a.dtype), kind="ExternalInput").ap()
         for n, a in arrays.items()}
    out = nc.dram_tensor("out_t", (D, T), F32, kind="ExternalOutput").ap()
    return t, out


def kernel(**inputs):
    import concourse.bacc as bacc
    from concourse.bass_utils import run_bass_kernel_spmd as run

    arrays = lay_out(inputs)
    marks = {}
    for dry in (True, False):
        nc = bacc.Bacc("TRN2", target_bir_lowering=False, num_devices=1)
        t, out = program(nc, arrays)
        build(nc, t, out, marks, dry)
    r = run(nc, [{f"in_{n}": a for n, a in arrays.items()}], core_ids=[0])
    return np.ascontiguousarray(r.results[0]["out_t"].T)[None]
```
